# Optimizing a Trainium2 kernel written in Bass

```python
import math
import jax
import jax.numpy as jnp
from jax import lax
import numpy as np
import jax, jax.numpy as jnp

D_MODEL = 1024
BATCH = 1
SEQ = 1024
DEPTH = 1

MIX_WIDTH = D_MODEL
HEAD_DIM = 64
ATT_WIDTH = MIX_WIDTH // 2
ATT_HEADS = ATT_WIDTH // HEAD_DIM
IDX_HEADS = 4
IDX_DIM = HEAD_DIM
TOPK_MAX = 256
Q_BLOCK = 128
ROPE_THETA = 10000.0
INDEXER_SCALE = (IDX_HEADS ** -0.5) * (IDX_DIM ** -0.5)
SSD_WIDTH = MIX_WIDTH - ATT_WIDTH
SSD_HEAD_DIM = 64
SSD_HEADS = SSD_WIDTH // SSD_HEAD_DIM
SSD_GROUPS = 2
D_STATE = 64
CONV_WIDTH = 4
CONV_CH = SSD_WIDTH + 2 * SSD_GROUPS * D_STATE
CHUNK = 128
N_GROUPS_MOE = 4
EXPERTS_PER_GROUP = 4
N_EXPERTS = N_GROUPS_MOE * EXPERTS_PER_GROUP
TOP_K_IN_GROUP = 2
EXPERT_FF = 256
ALPHA = (2 * DEPTH) ** 0.25
BETA = (8 * DEPTH) ** -0.25
LN_EPS = 1e-5
IN_SPLIT_SIZES = (ATT_WIDTH, HEAD_DIM, HEAD_DIM, IDX_HEADS * IDX_DIM, IDX_DIM, IDX_HEADS, SSD_WIDTH, CONV_CH, SSD_HEADS)
IN_WIDTH = sum(IN_SPLIT_SIZES)
IN_SPLIT_POINTS = tuple(int(v) for v in np.cumsum(IN_SPLIT_SIZES)[:-1])


def layer_norm(x, g, b):
    xf = x.astype(jnp.float32)
    mu = jnp.mean(xf, -1, keepdims=True)
    var = jnp.mean(jnp.square(xf - mu), -1, keepdims=True)
    return ((xf - mu) * lax.rsqrt(var + LN_EPS)).astype(x.dtype) * g + b

def rope_tables(seq_len):
    inv = ROPE_THETA ** (-jnp.arange(0, HEAD_DIM, 2, dtype=jnp.float32) / HEAD_DIM)
    ang = jnp.arange(seq_len, dtype=jnp.float32)[:, None] * inv[None, :]
    return jnp.cos(ang), jnp.sin(ang)

def apply_rope(x, cos, sin):
    half = x.shape[-1] // 2
    x1, x2 = x[..., :half], x[..., half:]
    cos = cos.astype(x.dtype)
    sin = sin.astype(x.dtype)
    return jnp.concatenate([x1 * cos - x2 * sin, x1 * sin + x2 * cos], -1)

def dsa_attention(q, k, v, iq, ik, iw, topk):
    bsz, s, h, dh = q.shape
    n_blocks = s // Q_BLOCK
    key_pos = jnp.arange(s)

    def block(i):
        t0 = i * Q_BLOCK
        qb = lax.dynamic_slice_in_dim(q, t0, Q_BLOCK, 1)
        iqb = lax.dynamic_slice_in_dim(iq, t0, Q_BLOCK, 1)
        iwb = lax.dynamic_slice_in_dim(iw, t0, Q_BLOCK, 1)
        qpos = t0 + jnp.arange(Q_BLOCK)
        causal = key_pos[None, :] <= qpos[:, None]
        sc = jax.nn.relu(jnp.einsum('bthd,bsd->bths', iqb, ik))
        sc = jnp.einsum('bths,bth->bts', sc, iwb).astype(jnp.float32)
        sc = jnp.where(causal[None], sc, -jnp.inf)
        _, sel = lax.top_k(sc, topk)
        valid = sel <= qpos[None, :, None]
        k_sel = jax.vmap(lambda a, idx: a[idx])(k, sel)
        v_sel = jax.vmap(lambda a, idx: a[idx])(v, sel)
        logits = jnp.einsum('bthd,btkd->bthk', qb, k_sel).astype(jnp.float32) * (dh ** -0.5)
        logits = jnp.where(valid[:, :, None, :], logits, -jnp.inf)
        p = jax.nn.softmax(logits, -1).astype(v.dtype)
        return jnp.einsum('bthk,btkd->bthd', p, v_sel)

    out = lax.map(block, jnp.arange(n_blocks))
    return jnp.moveaxis(out, 0, 1).reshape(bsz, s, h * dh)

def causal_depthwise_conv(u, w, b):
    out = lax.conv_general_dilated(
        u, w[:, None, :].astype(u.dtype), window_strides=(1,),
        padding=[(CONV_WIDTH - 1, 0)], dimension_numbers=('NWC', 'WIO', 'NWC'),
        feature_group_count=u.shape[-1])
    return out + b

def segsum(a):
    t = a.shape[-1]
    ar = jnp.broadcast_to(a[..., :, None], a.shape + (t,))
    strict = jnp.tril(jnp.ones((t, t), dtype=bool), -1)
    cs = jnp.cumsum(jnp.where(strict, ar, 0.0), axis=-2)
    return jnp.where(jnp.tril(jnp.ones((t, t), dtype=bool)), cs, -jnp.inf)

def ssd_chunked(xdt, adt, bm, cm):
    b, s, h, p = xdt.shape
    n = bm.shape[-1]
    c = s // CHUNK
    X = xdt.reshape(b, c, CHUNK, h, p)
    Bc = bm.reshape(b, c, CHUNK, h, n)
    Cc = cm.reshape(b, c, CHUNK, h, n)
    A = adt.reshape(b, c, CHUNK, h).transpose(0, 3, 1, 2)
    a_cum = jnp.cumsum(A, -1)
    Lmat = jnp.exp(segsum(A))
    y_diag = jnp.einsum('bclhn,bcshn,bhcls,bcshp->bclhp', Cc, Bc, Lmat, X)
    decay_states = jnp.exp(a_cum[..., -1:] - a_cum)
    chunk_states = jnp.einsum('bclhn,bhcl,bclhp->bchpn', Bc, decay_states, X)
    chunk_decay = jnp.exp(a_cum[..., -1])

    def step(carry, inp):
        st, dec = inp
        return carry * dec[..., None, None] + st, carry

    init = jnp.zeros((b, h, p, n), X.dtype)
    _, prev = lax.scan(step, init, (jnp.moveaxis(chunk_states, 1, 0), jnp.moveaxis(chunk_decay, 2, 0)))
    prev = jnp.moveaxis(prev, 0, 1)
    y_off = jnp.einsum('bclhn,bchpn,bhcl->bclhp', Cc, prev, jnp.exp(a_cum))
    return (y_diag + y_off).reshape(b, s, h, p)

def ssd_mixer(z, xbc, dt_raw, conv_w, conv_b, dt_bias, a_log, d_skip, norm_w):
    bsz, s, _ = xbc.shape
    f32 = jnp.float32
    xbc = jax.nn.silu(causal_depthwise_conv(xbc, conv_w, conv_b))
    gn = SSD_GROUPS * D_STATE
    xs = xbc[..., :SSD_WIDTH].reshape(bsz, s, SSD_HEADS, SSD_HEAD_DIM).astype(f32)
    bm = xbc[..., SSD_WIDTH:SSD_WIDTH + gn].reshape(bsz, s, SSD_GROUPS, D_STATE)
    cm = xbc[..., SSD_WIDTH + gn:].reshape(bsz, s, SSD_GROUPS, D_STATE)
    rep = SSD_HEADS // SSD_GROUPS
    bm = jnp.repeat(bm, rep, axis=2).astype(f32)
    cm = jnp.repeat(cm, rep, axis=2).astype(f32)
    dt = jax.nn.softplus(dt_raw.astype(f32) + dt_bias.astype(f32))
    a = -jnp.exp(a_log.astype(f32))
    y = ssd_chunked(xs * dt[..., None], dt * a, bm, cm)
    y = y + d_skip.astype(f32)[:, None] * xs
    y = y.reshape(bsz, s, SSD_WIDTH) * jax.nn.silu(z.astype(f32))
    y = y * lax.rsqrt(jnp.mean(jnp.square(y), -1, keepdims=True) + LN_EPS)
    return y.astype(z.dtype) * norm_w

def hier_moe(h, w_rg, b_rg, w_re, b_re, w_gate, w_up, w_down):
    bsz, s, _ = h.shape
    f32 = jnp.float32
    p_group = jax.nn.softmax((h @ w_rg + b_rg).astype(f32), -1)
    g_idx = jnp.argmax(p_group, -1)
    g_prob = jnp.max(p_group, -1)
    e_logits = (h @ w_re + b_re).astype(f32).reshape(bsz, s, N_GROUPS_MOE, EXPERTS_PER_GROUP)
    e_in_group = jnp.take_along_axis(e_logits, g_idx[..., None, None], axis=2)[..., 0, :]
    top_logits, top_idx = lax.top_k(e_in_group, TOP_K_IN_GROUP)
    top_w = jax.nn.softmax(top_logits, -1) * g_prob[..., None]
    expert_id = g_idx[..., None] * EXPERTS_PER_GROUP + top_idx
    gates = jnp.sum(jax.nn.one_hot(expert_id, N_EXPERTS, dtype=f32) * top_w[..., None], axis=-2).astype(h.dtype)
    y = jnp.zeros_like(h)
    for e in range(N_EXPERTS):
        hid = jax.nn.silu(h @ w_gate[e]) * (h @ w_up[e])
        y = y + gates[..., e:e + 1] * (hid @ w_down[e])
    return y

def first_inputs(seed: int = 0) -> dict:
    key = jax.random.key(seed)
    ks = jax.random.split(key, 21)
    f32 = jnp.float32

    def nrm(k, shape, scale):
        return jax.random.normal(k, shape, f32) * scale

    x = nrm(ks[0], (BATCH, SEQ, D_MODEL), 1.0)
    w_in = nrm(ks[1], (DEPTH, D_MODEL, IN_WIDTH), D_MODEL ** -0.5)
    conv_w = nrm(ks[2], (DEPTH, CONV_WIDTH, CONV_CH), CONV_WIDTH ** -0.5)
    conv_b = nrm(ks[3], (DEPTH, CONV_CH), 0.02)
    dt0 = jnp.exp(jax.random.uniform(ks[4], (DEPTH, SSD_HEADS), f32, math.log(1e-3), math.log(1e-1)))
    dt_bias = dt0 + jnp.log(-jnp.expm1(-dt0))
    a_log = jnp.log(jax.random.uniform(ks[5], (DEPTH, SSD_HEADS), f32, 1.0, 16.0))
    d_skip = 1.0 + nrm(ks[6], (DEPTH, SSD_HEADS), 0.1)
    ssd_norm_w = 1.0 + nrm(ks[7], (DEPTH, SSD_WIDTH), 0.05)
    w_out = nrm(ks[8], (DEPTH, MIX_WIDTH, D_MODEL), (MIX_WIDTH ** -0.5) * BETA)
    ln1_g = 1.0 + nrm(ks[9], (DEPTH, D_MODEL), 0.05)
    ln1_b = nrm(ks[10], (DEPTH, D_MODEL), 0.02)
    w_route_group = nrm(ks[11], (DEPTH, D_MODEL, N_GROUPS_MOE), D_MODEL ** -0.5)
    b_route_group = nrm(ks[12], (DEPTH, N_GROUPS_MOE), 0.01)
    w_route_expert = nrm(ks[13], (DEPTH, D_MODEL, N_EXPERTS), D_MODEL ** -0.5)
    b_route_expert = nrm(ks[14], (DEPTH, N_EXPERTS), 0.01)
    w_gate = nrm(ks[15], (DEPTH, N_EXPERTS, D_MODEL, EXPERT_FF), D_MODEL ** -0.5)
    w_up = nrm(ks[16], (DEPTH, N_EXPERTS, D_MODEL, EXPERT_FF), D_MODEL ** -0.5)
    w_down = nrm(ks[17], (DEPTH, N_EXPERTS, EXPERT_FF, D_MODEL), (EXPERT_FF ** -0.5) * BETA)
    ln2_g = 1.0 + nrm(ks[18], (DEPTH, D_MODEL), 0.05)
    ln2_b = nrm(ks[19], (DEPTH, D_MODEL), 0.02)
    return {'x': x, 'w_in': w_in, 'conv_w': conv_w, 'conv_b': conv_b, 'dt_bias': dt_bias,
            'a_log': a_log, 'd_skip': d_skip, 'ssd_norm_w': ssd_norm_w, 'w_out': w_out,
            'ln1_g': ln1_g, 'ln1_b': ln1_b, 'w_route_group': w_route_group,
            'b_route_group': b_route_group, 'w_route_expert': w_route_expert,
            'b_route_expert': b_route_expert, 'w_gate': w_gate, 'w_up': w_up,
            'w_down': w_down, 'ln2_g': ln2_g, 'ln2_b': ln2_b}

def first_block(x, w_in, conv_w, conv_b, dt_bias, a_log, d_skip, ssd_norm_w, w_out, ln1_g, ln1_b,
              w_route_group, b_route_group, w_route_expert, b_route_expert, w_gate, w_up,
              w_down, ln2_g, ln2_b):
    bsz, s, _ = x.shape
    topk = min(TOPK_MAX, s // 4)
    cos, sin = rope_tables(s)
    cos_h, sin_h = cos[:, None, :], sin[:, None, :]
    for l in range(DEPTH):
        proj = jnp.einsum('bsd,de->bse', x, w_in[l])
        q, k, v, iq, ik, iw, z, xbc, dt_raw = jnp.split(proj, IN_SPLIT_POINTS, axis=-1)
        q = apply_rope(q.reshape(bsz, s, ATT_HEADS, HEAD_DIM), cos_h, sin_h)
        k = apply_rope(k, cos, sin)
        iq = apply_rope(iq.reshape(bsz, s, IDX_HEADS, IDX_DIM), cos_h, sin_h)
        ik = apply_rope(ik, cos, sin)
        att = dsa_attention(q, k, v, iq, ik, iw * INDEXER_SCALE, topk)
        ssd = ssd_mixer(z, xbc, dt_raw, conv_w[l], conv_b[l], dt_bias[l], a_log[l],
                        d_skip[l], ssd_norm_w[l])
        mixed = jnp.einsum('bse,ed->bsd', jnp.concatenate([att, ssd], -1), w_out[l])
        x = layer_norm(ALPHA * x + mixed, ln1_g[l], ln1_b[l])
        ffn = hier_moe(x, w_route_group[l], b_route_group[l], w_route_expert[l],
                       b_route_expert[l], w_gate[l], w_up[l], w_down[l])
        x = layer_norm(ALPHA * x + ffn, ln2_g[l], ln2_b[l])
    return x


DEPTH_2 = 2

GRID_W = 64
NA_HEADS = D_MODEL // (4 * HEAD_DIM)
NA_WIN_H = 8
NA_WIN_W = 16
MLA_HEADS = 3 * D_MODEL // (8 * HEAD_DIM)
MLA_Q_LORA = D_MODEL // 4
MLA_KV_LORA = D_MODEL // 8
MLA_NOPE = 64
MLA_ROPE = 32
MLA_V = 64
MLA_BLOCK = 128
SWA_HEADS = 3 * D_MODEL // (8 * HEAD_DIM)
SWA_KV_HEADS = 2
SWA_WINDOW = 128
SWA_BLOCK = 128
N_EXPERTS_2 = 16
EC_CAPACITY = 2
D_EXPERT = D_MODEL
RMS_EPS = 1e-6
NEG_INF = -1e30

A_W = NA_HEADS * HEAD_DIM
B_W = MLA_HEADS * MLA_V
C_W = SWA_HEADS * HEAD_DIM
D_MIX = A_W + B_W + C_W
IN_WIDTHS = (A_W, A_W, A_W,
             MLA_Q_LORA, MLA_KV_LORA, MLA_ROPE,
             SWA_HEADS * HEAD_DIM, SWA_KV_HEADS * HEAD_DIM, SWA_KV_HEADS * HEAD_DIM)
IN_COLS = sum(IN_WIDTHS)
IN_OFFSETS = tuple(int(v) for v in np.cumsum(IN_WIDTHS)[:-1])


def rms_norm(x, g):
    x32 = x.astype(jnp.float32)
    y = x32 * lax.rsqrt(jnp.mean(x32 * x32, axis=-1, keepdims=True) + RMS_EPS)
    return (y * g.astype(jnp.float32)).astype(x.dtype)

def rope_tables_2(seq, dim, dtype):
    inv = 1.0 / (ROPE_THETA ** (jnp.arange(0, dim, 2, dtype=jnp.float32) / dim))
    ang = jnp.arange(seq, dtype=jnp.float32)[:, None] * inv[None, :]
    return jnp.cos(ang).astype(dtype), jnp.sin(ang).astype(dtype)

def apply_rope_2(x, cos, sin):
    x1, x2 = jnp.split(x, 2, axis=-1)
    c = cos[None, :, None, :]
    s = sin[None, :, None, :]
    return jnp.concatenate([x1 * c - x2 * s, x2 * c + x1 * s], axis=-1)

def neighbourhood_attention(q, k, v, rpb):
    B, S, _ = q.shape
    rows = S // GRID_W
    wh = min(NA_WIN_H, rows)
    ww = NA_WIN_W
    shp = (B, rows, GRID_W, NA_HEADS, HEAD_DIM)
    qg, kg, vg = q.reshape(shp), k.reshape(shp), v.reshape(shp)
    cols = jnp.arange(GRID_W)
    col_start = jnp.clip(cols - ww // 2, 0, GRID_W - ww)
    col_idx = col_start[:, None] + jnp.arange(ww)[None, :]
    dc = col_idx - cols[:, None] + (NA_WIN_W - 1)
    scale = HEAD_DIM ** -0.5

    def one_row(args):
        r, q_row = args
        rs = jnp.clip(r - wh // 2, 0, rows - wh)
        k_rows = lax.dynamic_slice_in_dim(kg, rs, wh, axis=1)
        v_rows = lax.dynamic_slice_in_dim(vg, rs, wh, axis=1)
        k_win = k_rows[:, :, col_idx]
        v_win = v_rows[:, :, col_idx]
        dr = rs + jnp.arange(wh) - r + (NA_WIN_H - 1)
        bias = rpb[:, dr][:, :, dc].transpose(0, 2, 1, 3)
        s = jnp.einsum('bchd,brcjhd->bhcrj', q_row, k_win).astype(jnp.float32) * scale
        s = s + bias[None].astype(jnp.float32)
        p = jax.nn.softmax(s.reshape(B, NA_HEADS, GRID_W, wh * ww), axis=-1)
        p = p.reshape(s.shape).astype(v.dtype)
        return jnp.einsum('bhcrj,brcjhd->bchd', p, v_win)

    out = lax.map(one_row, (jnp.arange(rows), qg.swapaxes(0, 1)))
    return out.swapaxes(0, 1).reshape(B, S, NA_HEADS * HEAD_DIM)

def latent_attention(c_q, c_kv, k_rope, q_norm, w_uq, kv_norm, w_ukv, cos_r, sin_r):
    B, S, _ = c_q.shape
    q = (rms_norm(c_q, q_norm) @ w_uq).reshape(B, S, MLA_HEADS, MLA_NOPE + MLA_ROPE)
    q_nope = q[..., :MLA_NOPE]
    q_pe = apply_rope_2(q[..., MLA_NOPE:], cos_r, sin_r)
    kv = (rms_norm(c_kv, kv_norm) @ w_ukv).reshape(B, S, MLA_HEADS, MLA_NOPE + MLA_V)
    k_nope = kv[..., :MLA_NOPE]
    v = kv[..., MLA_NOPE:]
    k_pe = apply_rope_2(k_rope[:, :, None, :], cos_r, sin_r)[:, :, 0]
    nb = S // MLA_BLOCK
    scale = (MLA_NOPE + MLA_ROPE) ** -0.5

    def to_blocks(t):
        return t.reshape(B, nb, MLA_BLOCK, *t.shape[2:]).swapaxes(0, 1)

    def one_block(args):
        qn, qp = args
        s = (jnp.einsum('bqhd,bkhd->bhqk', qn, k_nope)
             + jnp.einsum('bqhd,bkd->bhqk', qp, k_pe)).astype(jnp.float32) * scale
        p = jax.nn.softmax(s, axis=-1).astype(v.dtype)
        return jnp.einsum('bhqk,bkhd->bqhd', p, v)

    o = lax.map(one_block, (to_blocks(q_nope), to_blocks(q_pe)))
    return o.swapaxes(0, 1).reshape(B, S, MLA_HEADS * MLA_V)

def window_gqa(q, k, v, sink, cos, sin):
    B, S, _ = q.shape
    G = SWA_HEADS // SWA_KV_HEADS
    q = apply_rope_2(q.reshape(B, S, SWA_HEADS, HEAD_DIM), cos, sin)
    k = apply_rope_2(k.reshape(B, S, SWA_KV_HEADS, HEAD_DIM), cos, sin)
    v = v.reshape(B, S, SWA_KV_HEADS, HEAD_DIM)
    nb = S // SWA_BLOCK
    n_side = -(-SWA_WINDOW // SWA_BLOCK)
    pad = n_side * SWA_BLOCK
    n_keys = (2 * n_side + 1) * SWA_BLOCK

    def band(t):
        tp = jnp.pad(t, ((0, 0), (pad, pad), (0, 0), (0, 0)))
        tp = tp.reshape(B, nb + 2 * n_side, SWA_BLOCK, SWA_KV_HEADS, HEAD_DIM)
        return jnp.concatenate([tp[:, i:i + nb] for i in range(2 * n_side + 1)], axis=2)

    kb, vb = band(k), band(v)
    qb = q.reshape(B, nb, SWA_BLOCK, SWA_KV_HEADS, G, HEAD_DIM)
    s = jnp.einsum('bnqkgd,bnjkd->bnkgqj', qb, kb).astype(jnp.float32) * (HEAD_DIM ** -0.5)
    blk = jnp.arange(nb)[:, None, None] * SWA_BLOCK
    qpos = blk + jnp.arange(SWA_BLOCK)[None, :, None]
    kpos = blk - pad + jnp.arange(n_keys)[None, None, :]
    valid = (jnp.abs(qpos - kpos) <= SWA_WINDOW) & (kpos >= 0) & (kpos < S)
    s = jnp.where(valid[None, :, None, None], s, NEG_INF)
    sink_logit = jnp.broadcast_to(sink.astype(jnp.float32).reshape(1, 1, SWA_KV_HEADS, G, 1, 1),
                                  s.shape[:-1] + (1,))
    p = jax.nn.softmax(jnp.concatenate([s, sink_logit], axis=-1), axis=-1)[..., :-1].astype(v.dtype)
    o = jnp.einsum('bnkgqj,bnjkd->bnqkgd', p, vb)
    return o.reshape(B, S, SWA_HEADS * HEAD_DIM)

def expert_choice_ffn(xn, w_router, w_gate, w_up, w_down):
    B, S, D = xn.shape
    cap = EC_CAPACITY * S // N_EXPERTS_2
    aff = jax.nn.softmax((xn @ w_router).astype(jnp.float32), axis=-1)
    g, idx = lax.top_k(aff.swapaxes(1, 2), cap)
    bidx = jnp.arange(B)[:, None, None]
    xs = xn[bidx, idx]
    hid = jax.nn.silu(jnp.einsum('becd,edf->becf', xs, w_gate)) * jnp.einsum('becd,edf->becf', xs, w_up)
    y = jnp.einsum('becf,efd->becd', hid, w_down) * g[..., None].astype(xn.dtype)
    return jnp.zeros_like(xn).at[bidx, idx].add(y)

def second_inputs(seed: int = 0) -> dict:
    key = jax.random.key(seed)
    ks = jax.random.split(key, 17)
    f32 = jnp.float32

    def nrm(k, shape, scale):
        return jax.random.normal(k, shape, f32) * scale

    def gain(k, shape):
        return 1.0 + 0.05 * jax.random.normal(k, shape, f32)

    return {
        'x': nrm(ks[0], (BATCH, SEQ, D_MODEL), 1.0),
        'attn_norm': gain(ks[1], (DEPTH_2, D_MODEL)),
        'w_in': nrm(ks[2], (DEPTH_2, D_MODEL, IN_COLS), D_MODEL ** -0.5),
        'na_rpb': nrm(ks[3], (DEPTH_2, NA_HEADS, 2 * NA_WIN_H - 1, 2 * NA_WIN_W - 1), 0.1),
        'mla_q_norm': gain(ks[4], (DEPTH_2, MLA_Q_LORA)),
        'mla_w_uq': nrm(ks[5], (DEPTH_2, MLA_Q_LORA, MLA_HEADS * (MLA_NOPE + MLA_ROPE)), MLA_Q_LORA ** -0.5),
        'mla_kv_norm': gain(ks[6], (DEPTH_2, MLA_KV_LORA)),
        'mla_w_ukv': nrm(ks[7], (DEPTH_2, MLA_KV_LORA, MLA_HEADS * (MLA_NOPE + MLA_V)), MLA_KV_LORA ** -0.5),
        'swa_sink': nrm(ks[8], (DEPTH_2, SWA_HEADS), 1.0),
        'group_norm': gain(ks[9], (DEPTH_2, D_MIX)),
        'w_out': nrm(ks[10], (DEPTH_2, D_MIX, D_MODEL), D_MIX ** -0.5),
        'ffn_norm': gain(ks[11], (DEPTH_2, D_MODEL)),
        'w_router': nrm(ks[12], (DEPTH_2, D_MODEL, N_EXPERTS_2), D_MODEL ** -0.5),
        'w_gate': nrm(ks[13], (DEPTH_2, N_EXPERTS_2, D_MODEL, D_EXPERT), D_MODEL ** -0.5),
        'w_up': nrm(ks[14], (DEPTH_2, N_EXPERTS_2, D_MODEL, D_EXPERT), D_MODEL ** -0.5),
        'w_down': nrm(ks[15], (DEPTH_2, N_EXPERTS_2, D_EXPERT, D_MODEL), D_EXPERT ** -0.5),
        'final_norm': gain(ks[16], (D_MODEL,)),
    }

def second_block(x, attn_norm, w_in, na_rpb, mla_q_norm, mla_w_uq, mla_kv_norm, mla_w_ukv, swa_sink,
              group_norm, w_out, ffn_norm, w_router, w_gate, w_up, w_down, final_norm):
    B, S, _ = x.shape
    cos, sin = rope_tables_2(S, HEAD_DIM, x.dtype)
    cos_r, sin_r = rope_tables_2(S, MLA_ROPE, x.dtype)
    h = x
    for l in range(DEPTH_2):
        xn = rms_norm(h, attn_norm[l])
        proj = xn @ w_in[l]
        a_q, a_k, a_v, b_cq, b_ckv, b_kr, c_q, c_k, c_v = jnp.split(proj, IN_OFFSETS, axis=-1)
        o_a = neighbourhood_attention(a_q, a_k, a_v, na_rpb[l])
        o_b = latent_attention(b_cq, b_ckv, b_kr, mla_q_norm[l], mla_w_uq[l],
                               mla_kv_norm[l], mla_w_ukv[l], cos_r, sin_r)
        o_c = window_gqa(c_q, c_k, c_v, swa_sink[l], cos, sin)
        gn = group_norm[l]
        o = jnp.concatenate([rms_norm(o_a, gn[:A_W]),
                             rms_norm(o_b, gn[A_W:A_W + B_W]),
                             rms_norm(o_c, gn[A_W + B_W:])], axis=-1)
        h = h + o @ w_out[l]
        h = h + expert_choice_ffn(rms_norm(h, ffn_norm[l]), w_router[l], w_gate[l], w_up[l], w_down[l])
    return rms_norm(h, final_norm)


def setup_inputs(seed=0):
    out = dict(first_inputs(seed))
    for name, value in second_inputs(seed + 1).items():
        if name != "x":
            out[name + "_2"] = value
    return out


def reference(
    x, w_in, conv_w, conv_b, dt_bias, a_log, d_skip, ssd_norm_w, w_out, ln1_g, ln1_b,
    w_route_group, b_route_group, w_route_expert, b_route_expert, w_gate, w_up, w_down, ln2_g,
    ln2_b, attn_norm_2, w_in_2, na_rpb_2, mla_q_norm_2, mla_w_uq_2, mla_kv_norm_2, mla_w_ukv_2,
    swa_sink_2, group_norm_2, w_out_2, ffn_norm_2, w_router_2, w_gate_2, w_up_2, w_down_2,
    final_norm_2,
):
    x = first_block(
        x, w_in, conv_w, conv_b, dt_bias, a_log, d_skip, ssd_norm_w, w_out, ln1_g, ln1_b,
        w_route_group, b_route_group, w_route_expert, b_route_expert, w_gate, w_up, w_down,
        ln2_g, ln2_b,
    )
    return second_block(
        x, attn_norm_2, w_in_2, na_rpb_2, mla_q_norm_2, mla_w_uq_2, mla_kv_norm_2, mla_w_ukv_2,
        swa_sink_2, group_norm_2, w_out_2, ffn_norm_2, w_router_2, w_gate_2, w_up_2, w_down_2,
        final_norm_2,
    )


_drawn_inputs = setup_inputs


def setup_inputs(seed=0):
    import zlib

    import numpy as np

    out = dict(_drawn_inputs(seed))
    spreads = {}
    factors = {'b_route_group': 5.802, 'b_route_expert': 5.144, 'swa_sink_2': 8.0, 'mla_q_norm_2': 2.681}
    for name, (base, spread) in spreads.items():
        noise = np.random.default_rng([zlib.crc32(name.encode()), seed]).standard_normal(out[name].shape)
        drawn = base * np.exp(spread * noise) if base else spread * noise
        out[name] = jnp.asarray(drawn.astype(out[name].dtype))
    for name, factor in factors.items():
        out[name] = (out[name] * factor).astype(out[name].dtype)
    return out
```

```python
from contextlib import ExitStack

import numpy as np

import concourse.bass as bass
from concourse import mybir

F32 = mybir.dt.float32
U32 = mybir.dt.uint32
ALU = mybir.AluOpType
ACT = mybir.ActivationFunctionType
AX = mybir.AxisListType

P = 128
S = 1024
D = 1024
T = S // P
KD = D // P
HALF = 512
BANK = 512

HEADS = 8
HD = 64
IDX_HEADS = 4
INDEXER_SCALE = (IDX_HEADS ** -0.5) * (HD ** -0.5)
TOPK = 256
SSD_HEADS = 8
STATE = 64
CONV = 4
EXPERTS = 16
FF = 256
ALPHA = 2.0 ** 0.25
LN_EPS = 1e-5
ROWS_Z = 512
V0, IW0, DT0 = 0, 64, 68
SMALL = 76
ROPE_CHUNKS = 8
XBC_CHUNKS = 6

LAYERS = 2
RMS_EPS = 1e-6
GRID_W = 64
GRID_H = S // GRID_W
NA_HEADS = 4
NA_H = 8
NA_W = 16
MLA_HEADS = 6
MLA_D = 96
SWA_HEADS = 6
CAP = 128
HIDE = -1e30
TAKEN = -3e38


class Book:

    def __init__(self, nc):
        self.nc = nc
        self.before = None
        self.count = 0


class Stage:

    def __init__(self, book, *names):
        self.book = book
        self.names = names

    def __enter__(self):
        book = self.book
        nc = book.nc
        book.count += 1
        self.own = ExitStack()
        self.sems = [self.own.enter_context(nc.semaphore(f"{n}_{book.count}")) for n in self.names]
        self.opened = ExitStack()
        block = self.opened.enter_context(nc.Block(no_gpsimd_drain=False))
        old = book.before.sems if book.before else []

        @block.sync
        def _(sp):
            for s in old:
                sp.sem_clear(s)

        return (block, *self.sems)

    def __exit__(self, kind, value, trace):
        if kind is not None:
            return False
        self.opened.close()
        if self.book.before:
            self.book.before.own.close()
        self.book.before = self
        return False


class Chain:

    def __init__(self, eng, sem):
        self.eng, self.sem, self.n = eng, sem, 0

    def step(self, ins):
        ins.then_inc(self.sem, 1)
        self.n += 1
        self.eng.wait_ge(self.sem, self.n)


def tile(t, size=P):
    return slice(t * size, (t + 1) * size)


def spread(ap, shape):
    return ap.unsqueeze(len(shape) - 1).broadcast_to(shape)




def turn(book, ps, ident, rows, turned, width, gain=None):
    nc = book.nc
    chunks = width // P
    groups = [(c, h) for c in range(chunks) for h in range(2)]
    with Stage(book, "turned_full", "read_by_act", "read_by_dve") as (block, full, by_act, by_dve):

        @block.tensor
        def _(pe):
            for g, (c, h) in enumerate(groups):
                if g >= 8:
                    if g % 2:
                        pe.wait_ge(by_dve, g // 2 - 3)
                    else:
                        pe.wait_ge(by_act, g // 2 - 3)
                for j in range(4):
                    t = 4 * h + j
                    last = nc.tensor.transpose(ps[:, g % 8, tile(j)], rows[:, t, tile(c)], ident[:, :])
                last.then_inc(full, 1)

        @block.scalar
        def _(act):
            for g, (c, h) in enumerate(groups):
                if g % 2 == 0:
                    act.wait_ge(full, g + 1)
                    out = turned[:, c, tile(h, HALF)]
                    if gain is None:
                        nc.scalar.activation(out, ps[:, g % 8, :], ACT.Copy).then_inc(by_act, 1)
                    else:
                        nc.scalar.activation(out, ps[:, g % 8, :], ACT.Copy, scale=gain[:, c:c + 1]).then_inc(by_act, 1)

        @block.vector
        def _(dve):
            for g, (c, h) in enumerate(groups):
                if g % 2 == 1:
                    dve.wait_ge(full, g + 1)
                    out = turned[:, c, tile(h, HALF)]
                    if gain is None:
                        nc.vector.tensor_copy(out, ps[:, g % 8, :]).then_inc(by_dve, 1)
                    else:
                        nc.vector.tensor_scalar(out, ps[:, g % 8, :], gain[:, c:c + 1], None, ALU.mult).then_inc(by_dve, 1)


def root_mean_squares(book, rows, segments, eps, stats, junk, out=None):
    nc = book.nc
    n = len(segments)
    if out is None:
        out = rows
    ss = stats[:, 0, 0:T * n].rearrange("p (t n) -> p t n", n=n)
    root = stats[:, 1, 0:T * n].rearrange("p (t n) -> p t n", n=n)
    with Stage(book, "squares", "means", "roots", "dve_steps") as (block, squares, means, roots, steps):

        @block.scalar
        def _(act):
            for t in range(T):
                for j, (a, b) in enumerate(segments):
                    if t * n + j >= 2:
                        act.wait_ge(squares, t * n + j - 1)
                    nc.scalar.activation(junk[:, (t * n + j) % 2, 0:b - a], rows[:, t, a:b], ACT.Square,
                                         accum_out=ss[:, t, j:j + 1]).then_inc(squares, 1)
            act.wait_ge(means, 1)
            act.wait_ge(squares, T * n)
            nc.scalar.activation(root, ss, ACT.Sqrt).then_inc(roots, 1)

        @block.vector
        def _(dve):
            chain = Chain(dve, steps)
            dve.wait_ge(squares, T * n)
            for j, (a, b) in enumerate(segments):
                ins = nc.vector.tensor_scalar(ss[:, :, j], ss[:, :, j], 1.0 / (b - a), eps, ALU.mult, ALU.add)
                if j == n - 1:
                    ins.then_inc(means, 1)
                else:
                    chain.step(ins)
            dve.wait_ge(roots, 1)
            chain.step(nc.vector.reciprocal(root, root))
            for t in range(T):
                for j, (a, b) in enumerate(segments):
                    nc.vector.tensor_scalar(out[:, t, a:b], rows[:, t, a:b], root[:, t, j:j + 1], None, ALU.mult)


def layer_norm(book, rows, gain, shift, stats, after=None):
    nc = book.nc
    with ExitStack() as ctx, Stage(book, "moments", "roots", "dve_steps", "scaled", "stored") as (
            block, moments, roots, steps, scaled, stored):
        bn = ctx.enter_context(nc.sbuf_tensor(f"bn{book.count}", [P, T, 2, 6], F32))
        mv = ctx.enter_context(nc.sbuf_tensor(f"mv{book.count}", [P, T, 2], F32))
        var, root = stats[:, 0, 0:T], stats[:, 1, 0:T]

        @block.vector
        def _(dve):
            chain = Chain(dve, steps)
            for t in range(T):
                for h in range(2):
                    ins = nc.vector.bn_stats(bn[:, t, h, :], rows[:, t, tile(h, HALF)])
            chain.step(ins)
            for t in range(T):
                ins = nc.vector.bn_aggr(mv[:, t, :], bn[:, t, :, :])
            chain.step(ins)
            nc.vector.tensor_scalar(var, mv[:, :, 1], LN_EPS, None, ALU.add).then_inc(moments, 1)
            dve.wait_ge(roots, 1)
            chain.step(nc.vector.reciprocal(root, root))
            for t in range(T):
                chain.step(nc.vector.tensor_scalar(rows[:, t, :], rows[:, t, :], mv[:, t, 0:1], root[:, t:t + 1],
                                                   ALU.subtract, ALU.mult))
                chain.step(nc.vector.tensor_tensor(rows[:, t, :], rows[:, t, :], gain[:, :], ALU.mult))
                nc.vector.tensor_tensor(rows[:, t, :], rows[:, t, :], shift[:, :], ALU.add).then_inc(scaled, 1)

        @block.scalar
        def _(act):
            act.wait_ge(moments, 1)
            nc.scalar.activation(root, var, ACT.Sqrt).then_inc(roots, 1)

        if after is not None:
            @block.sync
            def _(sp):
                sp.wait_ge(scaled, T)
                sp.dma_start(after, rows[:, :, :]).then_inc(stored, 16)
                sp.wait_ge(stored, 16)


def rotate(book, ps, turner, cos, sin, raw, chunks, parts=P):
    nc = book.nc
    with ExitStack() as ctx, Stage(book, "turned_full", "cos_done", "sin_done", "rotated") as (
            block, full, cos_done, sin_done, rotated):
        by_cos = ctx.enter_context(nc.sbuf_tensor(f"by_cos{book.count}", [P, 2, S], F32))
        by_sin = ctx.enter_context(nc.sbuf_tensor(f"by_sin{book.count}", [P, 2, S], F32))

        @block.tensor
        def _(pe):
            for n in range(chunks):
                if n >= 4:
                    pe.wait_ge(sin_done, n - 3)
                for h in range(2):
                    last = nc.tensor.matmul(ps[0:parts, 2 * (n % 4) + h, :], turner[0:parts, 0:parts],
                                            raw[0:parts, n, tile(h, HALF)], start=True, stop=True)
                last.then_inc(full, 1)

        @block.gpsimd
        def _(pool):
            for n in range(chunks):
                if n >= 2:
                    pool.wait_ge(rotated, n - 1)
                nc.gpsimd.tensor_tensor(by_cos[0:parts, n % 2, :], raw[0:parts, n, :], cos[0:parts, :],
                                        ALU.mult).then_inc(cos_done, 1)

        @block.vector
        def _(dve):
            for n in range(chunks):
                dve.wait_ge(full, n + 1)
                if n >= 2:
                    dve.wait_ge(rotated, n - 1)
                nc.vector.tensor_tensor(by_sin[0:parts, n % 2, :],
                                        ps[0:parts, 2 * (n % 4):2 * (n % 4) + 2, :].rearrange("p a b -> p (a b)"),
                                        sin[0:parts, :], ALU.mult).then_inc(sin_done, 1)
                dve.wait_ge(cos_done, n + 1)
                dve.wait_ge(sin_done, n + 1)
                nc.vector.tensor_tensor(raw[0:parts, n, :], by_cos[0:parts, n % 2, :], by_sin[0:parts, n % 2, :],
                                        ALU.add).then_inc(rotated, 1)


def attend(book, ps, ident, items, scale, widest):
    nc = book.nc
    groups = [(n, j) for n, item in enumerate(items) for j in range((item["keys"] // P + 3) // 4)]
    first = {}
    for g, (n, j) in enumerate(groups):
        if j == 0:
            first[n] = g
    count = [len([1 for m, _ in groups if m == n]) for n in range(len(items))]
    with ExitStack() as ctx, Stage(
            book, "scores_full", "logits_ready", "probs_ready", "turned_full", "act_copied", "dve_copied",
            "values_used", "dve_steps", "sink_done", "written") as (
            block, scores_full, logits_ready, probs_ready, turned_full, act_copied, dve_copied,
            values_used, steps, sink_done, written):
        sb = lambda name, shape: ctx.enter_context(nc.sbuf_tensor(f"{name}{book.count}", shape, F32))
        logits = sb("logits", [P, 2, widest])
        probs = sb("probs", [P, 2, widest])
        turned = sb("turned", [P, 4, BANK])
        top = sb("top", [P, 2])
        less = sb("less", [P, 2])
        total = sb("total", [P, 2])
        sunk = sb("sunk", [P, 2])
        over = sb("over", [P, 2])

        def raw(n, a=0, b=P):
            flat = ps[:, 2 * (n % 2):2 * (n % 2) + 2, :].rearrange("p a b -> p (a b)")
            return flat[a:b, 0:items[n]["keys"]]

        @block.tensor
        def _(pe):
            def score(n):
                item = items[n]
                if n >= 2:
                    pe.wait_ge(probs_ready, n - 1)
                for a, b, q, k in item["scores"]:
                    for h in range((item["keys"] + BANK - 1) // BANK):
                        lo, hi = h * BANK, min((h + 1) * BANK, item["keys"])
                        last = nc.tensor.matmul(ps[a:b, 2 * (n % 2) + h, 0:hi - lo], q, k[:, lo:hi],
                                                start=True, stop=True)
                last.then_inc(scores_full, 1)

            score(0)
            for n, item in enumerate(items):
                pe.wait_ge(probs_ready, n + 1)
                chunks = item["keys"] // P
                for j in range(count[n]):
                    g = first[n] + j
                    if g >= 2:
                        if g % 2:
                            pe.wait_ge(dve_copied, g // 2)
                        else:
                            pe.wait_ge(act_copied, g // 2)
                    for i in range(min(4, chunks - 4 * j)):
                        last = nc.tensor.transpose(ps[:, 4 + g % 2, tile(i)], probs[:, n % 2, tile(4 * j + i)],
                                                   ident[:, :])
                    last.then_inc(turned_full, 1)
                if n + 1 < len(items):
                    score(n + 1)
                if n >= 2:
                    pe.wait_ge(written, n - 1)
                for j in range(count[n]):
                    g = first[n] + j
                    if g % 2:
                        pe.wait_ge(dve_copied, g // 2 + 1)
                    else:
                        pe.wait_ge(act_copied, g // 2 + 1)
                    for i in range(min(4, chunks - 4 * j)):
                        c = 4 * j + i
                        for a, b, values in item["values"]:
                            last = nc.tensor.matmul(ps[a:b, 6 + n % 2, 0:HD], turned[:, g % 4, i * P + a:i * P + b],
                                                    values[c], start=(c == 0), stop=(c == chunks - 1))
                    last.then_inc(values_used, 1)

        @block.scalar
        def _(act):
            def exponentials(n):
                item = items[n]
                act.wait_ge(logits_ready, n + 1)
                if n >= 2:
                    act.wait_ge(turned_full, first[n - 1])
                source = logits[:, n % 2, 0:item["keys"]] if item["add"] else raw(n)
                nc.scalar.activation(probs[:, n % 2, 0:item["keys"]], source, ACT.Exp, scale=scale,
                                     bias=less[:, n % 2:n % 2 + 1],
                                     accum_out=total[:, n % 2:n % 2 + 1]).then_inc(probs_ready, 1)
                if item["sink"] is not None:
                    nc.scalar.activation(sunk[:, n % 2:n % 2 + 1], item["sink"], ACT.Exp,
                                         bias=less[:, n % 2:n % 2 + 1]).then_inc(sink_done, 1)

            exponentials(0)
            for n, item in enumerate(items):
                if n + 1 < len(items):
                    if n >= 1:
                        act.wait_ge(written, n)
                    exponentials(n + 1)
                for j in range(count[n]):
                    g = first[n] + j
                    if g % 2 == 0:
                        act.wait_ge(turned_full, g + 1)
                        if g >= 4:
                            act.wait_ge(values_used, g - 3)
                        w = min(4, item["keys"] // P - 4 * j) * P
                        nc.scalar.activation(turned[:, g % 4, 0:w], ps[:, 4 + g % 2, 0:w],
                                             ACT.Copy).then_inc(act_copied, 1)

        @block.vector
        def _(dve):
            chain = Chain(dve, steps)

            def maxima(n):
                item = items[n]
                dve.wait_ge(scores_full, n + 1)
                if n >= 2:
                    dve.wait_ge(probs_ready, n - 1)
                if item["sink"] is not None and n >= 2:
                    dve.wait_ge(sink_done, n - 1)
                m = top[:, n % 2:n % 2 + 1]
                if item["add"]:
                    for a, b, add in item["add"]:
                        ins = nc.vector.tensor_tensor_reduce(
                            logits[a:b, n % 2, 0:item["keys"]], raw(n, a, b), add, 1.0, -3e38, ALU.add, ALU.max,
                            m[a:b, :])
                        chain.step(ins)
                else:
                    chain.step(nc.vector.tensor_reduce(m, raw(n), AX.X, ALU.max))
                if item["sink"] is not None:
                    chain.step(nc.vector.tensor_scalar(m, m, scale, item["sink"], ALU.mult, ALU.max))
                nc.vector.tensor_scalar(less[:, n % 2:n % 2 + 1], m, -1.0 if item["sink"] is not None else -scale,
                                        None, ALU.mult).then_inc(logits_ready, 1)

            maxima(0)
            for n, item in enumerate(items):
                if n + 1 < len(items):
                    maxima(n + 1)
                for j in range(count[n]):
                    g = first[n] + j
                    if g % 2 == 1:
                        dve.wait_ge(turned_full, g + 1)
                        if g >= 4:
                            dve.wait_ge(values_used, g - 3)
                        w = min(4, item["keys"] // P - 4 * j) * P
                        nc.vector.tensor_copy(turned[:, g % 4, 0:w], ps[:, 4 + g % 2, 0:w]).then_inc(dve_copied, 1)
                dve.wait_ge(probs_ready, n + 1)
                part = slice(n % 2, n % 2 + 1)
                if item["sink"] is not None:
                    dve.wait_ge(sink_done, n + 1)
                    chain.step(nc.vector.tensor_tensor(total[:, part], total[:, part], sunk[:, part], ALU.add))
                chain.step(nc.vector.reciprocal(over[:, part], total[:, part]))
                dve.wait_ge(values_used, first[n] + count[n])
                nc.vector.tensor_scalar(item["out"], ps[:, 6 + n % 2, 0:HD], over[:, part], None,
                                        ALU.mult).then_inc(written, 1)




def project_one(book, ps, A, raw, xbc, z, small):
    nc = book.nc
    chunks = ROPE_CHUNKS + XBC_CHUNKS
    pieces = [(0, 2), (2, 8), (8, 14)]
    piece_of = [n for n, (a, b) in enumerate(pieces) for _ in range(a, b)]
    with ExitStack() as ctx, Stage(book, "x_in", "w_in0", "w_in1", "w_in2", "w_rows_in", "full", "read",
                                   "edge_zero") as (
            block, x_in, w_in0, w_in1, w_in2, w_rows_in, full, read, edge_zero):
        w_in = [w_in0, w_in1, w_in2]
        sb = lambda name, shape: ctx.enter_context(nc.sbuf_tensor(name, shape, F32))
        xt = sb("xt", [P, KD, S])
        wt = sb("wt", [P, chunks, KD, P])
        wr = sb("wr", [P, KD, ROWS_Z + SMALL])

        @block.sync
        def _(sp):
            a, b = pieces[0]
            sp.dma_start(wt[:, a:b], A["w_turned"][:, a:b]).then_inc(w_in[0], 16)
            sp.dma_start(xt[:, :, :], A["xt"].rearrange("(k p) s -> p k s", p=P)).then_inc(x_in, 16)
            for n, (a, b) in enumerate(pieces[1:]):
                sp.dma_start(wt[:, a:b], A["w_turned"][:, a:b]).then_inc(w_in[n + 1], 16)
            sp.dma_start(wr[:, :, :], A["w_rows"]).then_inc(w_rows_in, 16)

        @block.gpsimd
        def _(pool):
            nc.gpsimd.memset(xbc[:, :, 0:CONV - 1], 0.0).then_inc(edge_zero, 1)

        @block.tensor
        def _(pe):
            g = 0
            pe.wait_ge(x_in, 16)
            for m in range(chunks):
                pe.wait_ge(w_in[piece_of[m]], 16)
                for h in range(2):
                    if g >= 8:
                        pe.wait_ge(read, g - 7)
                    for k in range(KD):
                        last = nc.tensor.matmul(ps[:, g % 8, :], wt[:, m, k, :], xt[:, k, tile(h, HALF)],
                                                start=(k == 0), stop=(k == KD - 1))
                    last.then_inc(full, 1)
                    g += 1
            pe.wait_ge(w_rows_in, 16)
            for t in range(T):
                for a, b in ((0, ROWS_Z), (ROWS_Z, ROWS_Z + SMALL)):
                    pe.wait_ge(read, g - 7)
                    for k in range(KD):
                        last = nc.tensor.matmul(ps[:, g % 8, 0:b - a], xt[:, k, tile(t)], wr[:, k, a:b],
                                                start=(k == 0), stop=(k == KD - 1))
                    last.then_inc(full, 1)
                    g += 1

        @block.scalar
        def _(act):
            g = 0
            for m in range(chunks):
                for h in range(2):
                    act.wait_ge(full, g + 1)
                    if m < ROPE_CHUNKS:
                        out = raw[:, m, tile(h, HALF)]
                    else:
                        out = xbc[:, m - ROPE_CHUNKS, CONV - 1 + h * HALF:CONV - 1 + (h + 1) * HALF]
                    nc.scalar.activation(out, ps[:, g % 8, :], ACT.Copy).then_inc(read, 1)
                    g += 1
            for t in range(T):
                for out, w in ((z[:, t, :], ROWS_Z), (small[:, t, :], SMALL)):
                    act.wait_ge(full, g + 1)
                    nc.scalar.activation(out, ps[:, g % 8, 0:w], ACT.Copy).then_inc(read, 1)
                    g += 1


def convolve(book, A, xbc, mixed):
    nc = book.nc
    with ExitStack() as ctx, Stage(book, "taps_in", "dve_steps", "summed", "done") as (
            block, taps_in, steps, summed, done):
        taps = ctx.enter_context(nc.sbuf_tensor("taps", [P, XBC_CHUNKS, CONV], F32))
        bias = ctx.enter_context(nc.sbuf_tensor("conv_bias", [P, XBC_CHUNKS], F32))
        acc = ctx.enter_context(nc.sbuf_tensor("conv_acc", [P, 2, S], F32))

        @block.sync
        def _(sp):
            sp.dma_start(taps[:, :, :], A["conv_w"]).then_inc(taps_in, 16)
            sp.dma_start(bias[:, :], A["conv_b"]).then_inc(taps_in, 16)

        @block.vector
        def _(dve):
            chain = Chain(dve, steps)
            dve.wait_ge(taps_in, 32)
            for m in range(XBC_CHUNKS):
                if m >= 2:
                    dve.wait_ge(done, m - 1)
                a = acc[:, m % 2, :]
                chain.step(nc.vector.tensor_scalar(a, xbc[:, m, 0:S], taps[:, m, 0:1], None, ALU.mult))
                for j in range(1, CONV):
                    ins = nc.vector.scalar_tensor_tensor(out=a, in0=xbc[:, m, j:j + S], scalar=taps[:, m, j:j + 1],
                                                         in1=a, op0=ALU.mult, op1=ALU.add)
                    if j < CONV - 1:
                        chain.step(ins)
                ins.then_inc(summed, 1)

        @block.scalar
        def _(act):
            act.wait_ge(taps_in, 32)
            for m in range(XBC_CHUNKS):
                act.wait_ge(summed, m + 1)
                nc.scalar.activation(mixed[:, m, :], acc[:, m % 2, :], ACT.Silu,
                                     bias=bias[:, m:m + 1]).then_inc(done, 1)


def state_space(book, ps, A, ident, ones, mixed, small, z, ssd):
    nc = book.nc
    H = SSD_HEADS
    G = H // 2
    with ExitStack() as ctx:
        sb = lambda name, shape: ctx.enter_context(nc.sbuf_tensor(name, shape, F32))
        xs = sb("xs", [P, T, 5 * P])
        upto = sb("upto", [P, P])
        hidden = sb("hidden", [P, 4, P])
        bias = sb("dt_bias", [P, H])
        a_log = sb("a_log", [P, H])
        skip = sb("skip", [P, H])
        norm_w = sb("norm_w", [P, BANK])
        dt = sb("dt", [P, T, H])
        u1 = sb("u1", [P, T, H])
        u2 = sb("u2", [P, T, H])
        u3 = sb("u3", [P, T, H])
        adt = sb("adt", [P, T, H])
        cum = sb("cum", [P, T, H])
        less_cum = sb("less_cum", [P, T, H])
        grown = sb("grown", [P, T, H])
        fade = sb("fade", [P, T, H])
        last_fade = sb("last_fade", [P, T, H])
        ss = sb("ss_ssd", [P, T])
        root = sb("root_ssd", [P, T])

        with Stage(book, "consts_in", "full", "read", "exp_a", "exp_x", "one_more", "logged", "dt_ready",
                   "adt_ready", "cum_full", "cum_read", "fades", "dve_steps") as (
                block, consts_in, full, read, exp_a, exp_x, one_more, logged, dt_ready, adt_ready, cum_full,
                cum_read, fades, steps):
            raw_dt = small[:, :, DT0:DT0 + H]

            @block.sync
            def _(sp):
                for to, what in ((upto, A["upto"]), (bias, A["dt_bias"].broadcast_to([P, H])),
                                 (a_log, A["a_log"].broadcast_to([P, H])), (skip, A["d_skip"].broadcast_to([P, H])),
                                 (norm_w, A["ssd_norm_w"].broadcast_to([P, BANK]))):
                    sp.dma_start(to[:, :], what).then_inc(consts_in, 16)
                sp.dma_start(hidden[:, :, :], A["hidden"]).then_inc(consts_in, 16)

            @block.tensor
            def _(pe):
                for g in range(T * 2):
                    t, part = divmod(g, 2)
                    if g >= 8:
                        pe.wait_ge(read, g - 7)
                    for j in range(4 if part == 0 else 1):
                        c = 4 * part + j
                        last = nc.tensor.transpose(ps[:, g % 8, tile(j)], mixed[:, c, tile(t)], ident[:, :])
                    last.then_inc(full, 1)
                pe.wait_ge(read, T * 2)
                pe.wait_ge(adt_ready, 1)
                nc.tensor.matmul(ps[:, 0, 0:T * H], upto[:, :], adt[:, :, :].rearrange("p t h -> p (t h)"),
                                 start=True, stop=True).then_inc(cum_full, 1)
                nc.tensor.matmul(ps[:, 1, 0:T * H], ones[:, :], adt[:, :, :].rearrange("p t h -> p (t h)"),
                                 start=True, stop=True).then_inc(cum_full, 1)

            @block.scalar
            def _(act):
                act.wait_ge(consts_in, 96)
                nc.scalar.activation(a_log[:, :], a_log[:, :], ACT.Exp).then_inc(exp_a, 1)
                act.wait_ge(exp_x, 1)
                nc.scalar.activation(u1[:, :, :], u1[:, :, :], ACT.Exp, scale=-1.0).then_inc(exp_a, 1)
                act.wait_ge(one_more, 1)
                nc.scalar.activation(u3[:, :, :], u2[:, :, :], ACT.Ln).then_inc(logged, 1)
                for g in range(T * 2):
                    t, part = divmod(g, 2)
                    act.wait_ge(full, g + 1)
                    w = HALF if part == 0 else P
                    nc.scalar.activation(xs[:, t, part * HALF:part * HALF + w], ps[:, g % 8, 0:w],
                                         ACT.Copy).then_inc(read, 1)
                act.wait_ge(cum_read, 1)
                nc.scalar.activation(grown[:, :, :], cum[:, :, :], ACT.Exp).then_inc(fades, 1)
                nc.scalar.activation(fade[:, :, :], u1[:, :, :], ACT.Exp).then_inc(fades, 1)
                nc.scalar.activation(last_fade[:, :, :], u2[:, :, :], ACT.Exp).then_inc(fades, 1)

            @block.vector
            def _(dve):
                chain = Chain(dve, steps)
                dve.wait_ge(consts_in, 96)
                over = bias[:, :].unsqueeze(1).broadcast_to([P, T, H])
                chain.step(nc.vector.tensor_tensor(dt[:, :, :], raw_dt, over, ALU.add))
                chain.step(nc.vector.tensor_scalar(u1[:, :, :], dt[:, :, :], -1.0, None, ALU.mult))
                nc.vector.tensor_tensor(u1[:, :, :], u1[:, :, :], dt[:, :, :], ALU.max).then_inc(exp_x, 1)
                dve.wait_ge(exp_a, 2)
                nc.vector.tensor_scalar(u2[:, :, :], u1[:, :, :], 1.0, None, ALU.add).then_inc(one_more, 1)
                dve.wait_ge(one_more, 1)
                dve.wait_ge(logged, 1)
                chain.step(nc.vector.tensor_scalar(u2[:, :, :], u2[:, :, :], -1.0, None, ALU.add))
                chain.step(nc.vector.tensor_scalar(cum[:, :, :], u2[:, :, :], 0.0, None, ALU.is_equal))
                chain.step(nc.vector.tensor_tensor(u2[:, :, :], u2[:, :, :], cum[:, :, :], ALU.add))
                chain.step(nc.vector.tensor_tensor(u3[:, :, :], u3[:, :, :], cum[:, :, :], ALU.add))
                chain.step(nc.vector.reciprocal(u2[:, :, :], u2[:, :, :]))
                chain.step(nc.vector.tensor_tensor(u3[:, :, :], u3[:, :, :], u2[:, :, :], ALU.mult))
                chain.step(nc.vector.tensor_tensor(u3[:, :, :], u3[:, :, :], u1[:, :, :], ALU.mult))
                chain.step(nc.vector.tensor_scalar(dt[:, :, :], dt[:, :, :], 0.0, None, ALU.max))
                chain.step(nc.vector.tensor_tensor(dt[:, :, :], dt[:, :, :], u3[:, :, :], ALU.add))
                rate = a_log[:, :].unsqueeze(1).broadcast_to([P, T, H])
                chain.step(nc.vector.tensor_tensor(adt[:, :, :], dt[:, :, :], rate, ALU.mult))
                nc.vector.tensor_scalar(adt[:, :, :], adt[:, :, :], -1.0, None, ALU.mult).then_inc(adt_ready, 1)
                dve.wait_ge(cum_full, 2)
                cums = ps[:, 0, 0:T * H].rearrange("p (t h) -> p t h", t=T)
                lasts = ps[:, 1, 0:T * H].rearrange("p (t h) -> p t h", t=T)
                chain.step(nc.vector.tensor_copy(cum[:, :, :], cums))
                chain.step(nc.vector.tensor_scalar(less_cum[:, :, :], cum[:, :, :], -1.0, None, ALU.mult))
                chain.step(nc.vector.tensor_copy(u2[:, :, :], lasts))
                nc.vector.tensor_tensor(u1[:, :, :], u2[:, :, :], cum[:, :, :], ALU.subtract).then_inc(cum_read, 1)

        with Stage(book, "a_upto_ready", "spans_full", "spans_ready", "pairs_full", "pairs_ready", "x_ready",
                   "inner_full", "outer_full", "state_full", "state_ready", "decayed", "skip_ready", "y_ready",
                   "pool_steps", "dve_steps") as (
                block, a_upto_ready, spans_full, spans_ready, pairs_full, pairs_ready, x_ready, inner_full,
                outer_full, state_full, state_ready, decayed, skip_ready, y_ready, pool_steps, steps), \
                ExitStack() as inner:
            sb = lambda name, shape: inner.enter_context(nc.sbuf_tensor(name, shape, F32))
            a_upto = sb("a_upto", [P, H, P])
            spans = sb("spans", [P, H, P])
            pairs = sb("pairs", [P, H, P])
            xdt = sb("xdt", [P, 2, H * HD])
            xdec = sb("xdec", [P, 2, H * HD])
            state = sb("state", [P, G * HD])
            state_new = sb("state_new", [P, G * HD])
            fade_pair = sb("fade_pair", [P, T, G])
            skipped = sb("skipped", [P, 2, H * HD])
            yo = sb("yo", [P, H * HD])

            @block.tensor
            def _(pe):
                for c in range(T):
                    pe.wait_ge(a_upto_ready, c + 1)
                    for h in range(2):
                        if c >= 1 and h == 0:
                            pe.wait_ge(spans_ready, c)
                        nc.tensor.matmul(ps[:, h, :], ident[:, :], hidden[:, :, :].rearrange("p a b -> p (a b)"),
                                         start=True, stop=False)
                        last = nc.tensor.matmul(ps[:, h, :], ones[:, :],
                                                a_upto[:, 4 * h:4 * h + 4, :].rearrange("p a b -> p (a b)"),
                                                start=False, stop=True)
                    last.then_inc(spans_full, 1)
                    if c >= 1:
                        pe.wait_ge(pairs_ready, 2 * c)
                    for g in range(2):
                        half = slice(g * STATE, (g + 1) * STATE)
                        last = nc.tensor.matmul(ps[:, 2 + g, 0:P], mixed[half, 4, tile(c)], mixed[half, 5, tile(c)],
                                                start=True, stop=True)
                    last.then_inc(pairs_full, 1)
                    if c >= 1:
                        pe.wait_ge(state_ready, c)
                        pe.wait_ge(y_ready, c)
                        for g in range(2):
                            half = slice(g * STATE, (g + 1) * STATE)
                            last = nc.tensor.matmul(ps[:, 5 + 2 * g, 0:256], mixed[half, 5, tile(c)],
                                                    state[half, :], start=True, stop=True)
                        last.then_inc(outer_full, 1)
                    pe.wait_ge(x_ready, c + 1)
                    if c >= 1:
                        pe.wait_ge(state_ready, c)
                    for g in range(2):
                        last = nc.tensor.matmul(ps[g * STATE:(g + 1) * STATE, 6, 0:256],
                                                xs[:, c, HALF + g * STATE:HALF + (g + 1) * STATE],
                                                xdec[:, c % 2, g * 256:(g + 1) * 256], start=True, stop=True)
                    last.then_inc(state_full, 1)
                    pe.wait_ge(pairs_ready, 2 * c + 2)
                    if c >= 1:
                        pe.wait_ge(y_ready, c)
                    for h in range(H):
                        last = nc.tensor.matmul(ps[:, 4, h * HD:(h + 1) * HD], pairs[:, h, :],
                                                xdt[:, c % 2, h * HD:(h + 1) * HD], start=True, stop=True,
                                                skip_group_check=True)
                    last.then_inc(inner_full, 1)

            @block.scalar
            def _(act):
                for c in range(T):
                    act.wait_ge(spans_full, c + 1)
                    if c >= 1:
                        act.wait_ge(pairs_ready, 2 * c)
                    for h in range(H):
                        ins = nc.scalar.activation(spans[:, h, :], ps[:, h // 4, tile(h % 4)], ACT.Exp,
                                                   bias=less_cum[:, c, h:h + 1])
                    ins.then_inc(spans_ready, 1)

            @block.gpsimd
            def _(pool):
                def heads(ap):
                    return ap.rearrange("p (h d) -> p h d", d=HD)

                for g in range(2):
                    half = slice(g * STATE, (g + 1) * STATE)
                    nc.gpsimd.tensor_copy(fade_pair[half, :, :], last_fade[half, :, g * G:(g + 1) * G])\
                        .then_inc(decayed, 1)
                pool.wait_ge(decayed, 2)
                for c in range(T):
                    if c >= 2:
                        pool.wait_ge(inner_full, c - 1)
                        pool.wait_ge(y_ready, c - 1)
                    nc.gpsimd.tensor_tensor(heads(xdt[:, c % 2, :]), heads(xs[:, c, 0:HALF]),
                                            spread(dt[:, c, :], [P, H, HD]), ALU.mult).then_inc(pool_steps, 1)
                    pool.wait_ge(pool_steps, c + 1)
                    nc.gpsimd.tensor_tensor(heads(xdec[:, c % 2, :]), heads(xdt[:, c % 2, :]),
                                            spread(fade[:, c, :], [P, H, HD]), ALU.mult).then_inc(x_ready, 1)
                    nc.gpsimd.tensor_tensor(heads(skipped[:, c % 2, :]), heads(xs[:, c, 0:HALF]),
                                            spread(skip[:, :], [P, H, HD]), ALU.mult).then_inc(skip_ready, 1)

            @block.vector
            def _(dve):
                def heads(ap):
                    return ap.rearrange("p (h d) -> p h d", d=HD)

                chain = Chain(dve, steps)
                for c in range(T):
                    if c >= 1:
                        dve.wait_ge(spans_full, c)
                    nc.vector.tensor_tensor(a_upto[:, :, :], upto[:, :].unsqueeze(1).broadcast_to([P, H, P]),
                                            spread(adt[:, c, :], [P, H, P]), ALU.mult).then_inc(a_upto_ready, 1)
                    dve.wait_ge(spans_ready, c + 1)
                    dve.wait_ge(pairs_full, c + 1)
                    if c >= 1:
                        dve.wait_ge(inner_full, c)
                    for g in range(2):
                        nc.vector.tensor_tensor(pairs[:, 4 * g:4 * g + 4, :], spans[:, 4 * g:4 * g + 4, :],
                                                ps[:, 2 + g, 0:P].unsqueeze(1).broadcast_to([P, 4, P]),
                                                ALU.mult).then_inc(pairs_ready, 1)
                    dve.wait_ge(state_full, c + 1)
                    if c == 0:
                        dve.wait_ge(decayed, 2)
                        nc.vector.tensor_copy(state[:, :], ps[:, 6, 0:256]).then_inc(state_ready, 1)
                    else:
                        dve.wait_ge(outer_full, c)
                        chain.step(nc.vector.tensor_tensor(heads(state_new[:, :]), heads(state[:, :]),
                                                           spread(fade_pair[:, c, :], [P, G, HD]), ALU.mult))
                        nc.vector.tensor_tensor(state[:, :], state_new[:, :], ps[:, 6, 0:256],
                                                ALU.add).then_inc(state_ready, 1)
                    dve.wait_ge(skip_ready, c + 1)
                    dve.wait_ge(inner_full, c + 1)
                    y = ssd[:, c, :]
                    if c >= 1:
                        for g in range(2):
                            part = slice(g * 256, (g + 1) * 256)
                            ins = nc.vector.tensor_tensor(heads(yo[:, part]), heads(ps[:, 5 + 2 * g, 0:256]),
                                                          spread(grown[:, c, g * G:(g + 1) * G], [P, G, HD]),
                                                          ALU.mult)
                        chain.step(ins)
                        chain.step(nc.vector.tensor_tensor(yo[:, :], yo[:, :], ps[:, 4, :], ALU.add))
                        nc.vector.tensor_tensor(y, yo[:, :], skipped[:, c % 2, :], ALU.add).then_inc(y_ready, 1)
                    else:
                        nc.vector.tensor_tensor(y, ps[:, 4, :], skipped[:, c % 2, :], ALU.add).then_inc(y_ready, 1)
        with Stage(book, "gates", "gated", "squares", "means", "roots", "dve_steps") as (
                block, gates, gated, squares, means, roots, steps), ExitStack() as inner:
            junk = inner.enter_context(nc.sbuf_tensor("junk2_ssd", [P, HALF], F32))

            @block.scalar
            def _(act):
                for c in range(T):
                    nc.scalar.activation(z[:, c, :], z[:, c, :], ACT.Silu).then_inc(gates, 1)
                for c in range(T):
                    act.wait_ge(gated, c + 1)
                    nc.scalar.activation(junk[:, :], ssd[:, c, :], ACT.Square,
                                         accum_out=ss[:, c:c + 1]).then_inc(squares, 1)
                    act.wait_ge(squares, c + 1)
                act.wait_ge(means, 1)
                nc.scalar.activation(root[:, :], ss[:, :], ACT.Sqrt).then_inc(roots, 1)

            @block.vector
            def _(dve):
                chain = Chain(dve, steps)
                for c in range(T):
                    dve.wait_ge(gates, c + 1)
                    nc.vector.tensor_tensor(ssd[:, c, :], ssd[:, c, :], z[:, c, :], ALU.mult).then_inc(gated, 1)
                dve.wait_ge(gated, T)
                dve.wait_ge(squares, T)
                nc.vector.tensor_scalar(ss[:, :], ss[:, :], 1.0 / HALF, LN_EPS, ALU.mult, ALU.add).then_inc(means, 1)
                dve.wait_ge(roots, 1)
                chain.step(nc.vector.reciprocal(root[:, :], root[:, :]))
                for c in range(T):
                    nc.vector.scalar_tensor_tensor(out=ssd[:, c, :], in0=ssd[:, c, :], scalar=root[:, c:c + 1],
                                                   in1=norm_w[:, :], op0=ALU.mult, op1=ALU.mult)


def index_keys(book, ps, A, raw, small, masks, moff):
    nc = book.nc
    rounds = TOPK // 8
    with ExitStack() as ctx, Stage(book, "causal_in", "full", "positive", "scored", "dve_steps", "weights") as (
            block, causal_in, full, positive, scored, steps, weights):
        sb = lambda name, shape: ctx.enter_context(nc.sbuf_tensor(name, shape, F32))
        causal = sb("causal", [P, P])
        iw = sb("iw", [P, T, IDX_HEADS])
        relu = sb("relu", [P, 4, S])
        score = sb("score", [P, S])
        best = sb("best", [P, 8])

        @block.sync
        def _(sp):
            sp.dma_start(causal[:, :], A["causal"]).then_inc(causal_in, 16)

        @block.tensor
        def _(pe):
            n = 0
            for t in range(2, T):
                keys = (t + 1) * P
                for h in range(IDX_HEADS):
                    half = slice((h % 2) * HD, (h % 2 + 1) * HD)
                    if n >= 4:
                        pe.wait_ge(positive, n - 3)
                    for b in range((keys + BANK - 1) // BANK):
                        lo, hi = b * BANK, min((b + 1) * BANK, keys)
                        last = nc.tensor.matmul(ps[:, 2 * (n % 4) + b, 0:hi - lo], raw[half, 4 + h // 2, tile(t)],
                                                raw[half, 7, lo:hi], start=True, stop=True)
                    last.then_inc(full, 1)
                    n += 1

        @block.scalar
        def _(act):
            n = 0
            for t in range(2, T):
                keys = (t + 1) * P
                for h in range(IDX_HEADS):
                    act.wait_ge(full, n + 1)
                    if n >= 4:
                        act.wait_ge(scored, n - 3)
                    flat = ps[:, 2 * (n % 4):2 * (n % 4) + 2, :].rearrange("p a b -> p (a b)")
                    nc.scalar.activation(relu[:, n % 4, 0:keys], flat[:, 0:keys], ACT.Relu).then_inc(positive, 1)
                    n += 1

        @block.vector
        def _(dve):
            chain = Chain(dve, steps)
            chain.step(nc.vector.tensor_scalar(iw[:, :, :], small[:, :, IW0:IW0 + IDX_HEADS], INDEXER_SCALE, None,
                                               ALU.mult))
            dve.wait_ge(causal_in, 16)
            n = 0
            for t in range(T):
                keys = (t + 1) * P
                mask = masks[:, moff[t]:moff[t] + keys]
                if t < 2:
                    if t:
                        nc.vector.memset(mask[:, 0:t * P], 0.0)
                    nc.vector.tensor_copy(mask[:, t * P:keys], causal[:, :])
                    continue
                sc = score[:, 0:keys]
                for h in range(IDX_HEADS):
                    dve.wait_ge(positive, n + 1)
                    if h == 0:
                        ins = nc.vector.tensor_scalar(sc, relu[:, n % 4, 0:keys], iw[:, t, h:h + 1], None, ALU.mult)
                    else:
                        ins = nc.vector.scalar_tensor_tensor(out=sc, in0=relu[:, n % 4, 0:keys],
                                                             scalar=iw[:, t, h:h + 1], in1=sc, op0=ALU.mult,
                                                             op1=ALU.add)
                    ins.then_inc(scored, 1)
                    n += 1
                    dve.wait_ge(scored, n)
                chain.step(nc.vector.tensor_tensor(sc[:, t * P:keys], sc[:, t * P:keys], causal[:, :], ALU.add))
                for _ in range(rounds):
                    chain.step(nc.vector.max(best[:, :], sc))
                    chain.step(nc.vector.match_replace(sc, best[:, :], sc, TAKEN))
                chain.step(nc.vector.tensor_scalar(mask, sc, TAKEN / 2, HIDE, ALU.is_ge, ALU.mult))


def mix_out(book, ps, A, weights, turned, residual_scale, rows, source, chunks=KD):
    nc = book.nc
    with ExitStack() as ctx, Stage(book, "w_in", "rows_in", "full", "read") as (block, w_in, rows_in, full, read):
        w = ctx.enter_context(nc.sbuf_tensor(f"w_mix{book.count}", [P, chunks, D], F32))

        @block.sync
        def _(sp):
            sp.dma_start(w[:, :, :], weights).then_inc(w_in, 16)
            if source is not None:
                sp.dma_start(rows[:, :, :], source).then_inc(rows_in, 16)

        @block.tensor
        def _(pe):
            pe.wait_ge(w_in, 16)
            for g in range(2 * T):
                t, h = divmod(g, 2)
                if g >= 8:
                    pe.wait_ge(read, g - 7)
                for k in range(chunks):
                    last = nc.tensor.matmul(ps[:, g % 8, :], turned[:, k, tile(t)], w[:, k, tile(h, HALF)],
                                            start=(k == 0), stop=(k == chunks - 1))
                last.then_inc(full, 1)

        @block.vector
        def _(dve):
            if source is not None:
                dve.wait_ge(rows_in, 16)
            for g in range(2 * T):
                t, h = divmod(g, 2)
                dve.wait_ge(full, g + 1)
                out = rows[:, t, tile(h, HALF)]
                if residual_scale == 1.0:
                    nc.vector.tensor_tensor(out, out, ps[:, g % 8, :], ALU.add).then_inc(read, 1)
                else:
                    nc.vector.scalar_tensor_tensor(out=out, in0=out, scalar=residual_scale, in1=ps[:, g % 8, :],
                                                   op0=ALU.mult, op1=ALU.add).then_inc(read, 1)


def route_one(book, ps, A, turned, gates):
    nc = book.nc
    GR, PER = 4, 4
    W = GR + EXPERTS
    with ExitStack() as ctx, Stage(book, "w_in", "bias_in", "full", "shifted", "exps", "dve_steps") as (
            block, w_in, bias_in, full, shifted, exps, steps):
        sb = lambda name, shape: ctx.enter_context(nc.sbuf_tensor(name, shape, F32))
        w = sb("w_route", [P, KD, W])
        bias = sb("b_route", [P, W])
        logit = sb("logit", [P, T, W])
        a = sb("route_a", [P, T, GR])
        b = sb("route_b", [P, T, GR])
        onehot = sb("onehot", [P, T, GR])
        free = sb("free", [P, T])
        m = sb("route_m", [P, T])
        m2 = sb("route_m2", [P, T])
        prob = sb("route_prob", [P, T])
        pick = sb("pick", [P, T, PER])
        both = sb("both", [P, T, PER])
        inner = sb("inner", [P, T, PER])
        tmp = sb("route_tmp", [P, T, PER])
        first_w = sb("first_w", [P, T])
        second_w = sb("second_w", [P, T])

        @block.sync
        def _(sp):
            sp.dma_start(w[:, :, :], A["w_route"]).then_inc(w_in, 16)
            sp.dma_start(bias[:, :], A["b_route"].broadcast_to([P, W])).then_inc(bias_in, 16)

        @block.tensor
        def _(pe):
            pe.wait_ge(w_in, 16)
            for t in range(T):
                for k in range(KD):
                    last = nc.tensor.matmul(ps[:, t, 0:W], turned[:, k, tile(t)], w[:, k, :], start=(k == 0),
                                            stop=(k == KD - 1))
                last.then_inc(full, 1)

        @block.scalar
        def _(act):
            act.wait_ge(shifted, 1)
            nc.scalar.activation(b[:, :, :], b[:, :, :], ACT.Exp).then_inc(exps, 1)
            act.wait_ge(shifted, 2)
            nc.scalar.activation(second_w[:, :], second_w[:, :], ACT.Exp).then_inc(exps, 1)

        @block.vector
        def _(dve):
            chain = Chain(dve, steps)

            def first_of(out, values, top):
                chain.step(nc.vector.tensor_tensor(out[:, :, :], values, spread(top, [P, T, 4]), ALU.is_equal))
                chain.step(nc.vector.tensor_scalar(free[:, :], out[:, :, 0], -1.0, 1.0, ALU.mult, ALU.add))
                for j in range(1, 4):
                    chain.step(nc.vector.tensor_tensor(out[:, :, j], out[:, :, j], free[:, :], ALU.mult))
                    if j < 3:
                        chain.step(nc.vector.tensor_tensor(free[:, :], free[:, :], out[:, :, j], ALU.subtract))

            dve.wait_ge(bias_in, 16)
            for t in range(T):
                dve.wait_ge(full, t + 1)
                ins = nc.vector.tensor_tensor(logit[:, t, :], ps[:, t, 0:W], bias[:, :], ALU.add)
            chain.step(ins)
            groups = logit[:, :, 0:GR]
            chain.step(nc.vector.tensor_reduce(m[:, :], groups, AX.X, ALU.max))
            nc.vector.tensor_tensor(b[:, :, :], groups, spread(m[:, :], [P, T, GR]), ALU.subtract).then_inc(shifted, 1)
            first_of(onehot, groups, m[:, :])
            dve.wait_ge(exps, 1)
            chain.step(nc.vector.tensor_reduce(prob[:, :], b[:, :, :], AX.X, ALU.add))
            chain.step(nc.vector.reciprocal(prob[:, :], prob[:, :]))
            for g in range(GR):
                of_group = logit[:, :, GR + g * PER:GR + (g + 1) * PER]
                to = inner if g == 0 else tmp
                chain.step(nc.vector.tensor_tensor(to[:, :, :], of_group, spread(onehot[:, :, g], [P, T, PER]),
                                                   ALU.mult))
                if g:
                    chain.step(nc.vector.tensor_tensor(inner[:, :, :], inner[:, :, :], tmp[:, :, :], ALU.add))
            chain.step(nc.vector.tensor_reduce(m[:, :], inner[:, :, :], AX.X, ALU.max))
            first_of(pick, inner[:, :, :], m[:, :])
            chain.step(nc.vector.scalar_tensor_tensor(out=tmp[:, :, :], in0=pick[:, :, :], scalar=HIDE,
                                                      in1=inner[:, :, :], op0=ALU.mult, op1=ALU.add))
            chain.step(nc.vector.tensor_reduce(m2[:, :], tmp[:, :, :], AX.X, ALU.max))
            nc.vector.tensor_tensor(second_w[:, :], m2[:, :], m[:, :], ALU.subtract).then_inc(shifted, 1)
            first_of(both, tmp[:, :, :], m2[:, :])
            dve.wait_ge(exps, 2)
            chain.step(nc.vector.tensor_scalar(first_w[:, :], second_w[:, :], 1.0, None, ALU.add))
            chain.step(nc.vector.reciprocal(first_w[:, :], first_w[:, :]))
            chain.step(nc.vector.tensor_tensor(first_w[:, :], first_w[:, :], prob[:, :], ALU.mult))
            chain.step(nc.vector.tensor_tensor(second_w[:, :], second_w[:, :], first_w[:, :], ALU.mult))
            chain.step(nc.vector.tensor_tensor(pick[:, :, :], pick[:, :, :], spread(first_w[:, :], [P, T, PER]),
                                               ALU.mult))
            chain.step(nc.vector.tensor_tensor(both[:, :, :], both[:, :, :], spread(second_w[:, :], [P, T, PER]),
                                               ALU.mult))
            chain.step(nc.vector.tensor_tensor(pick[:, :, :], pick[:, :, :], both[:, :, :], ALU.add))
            for g in range(GR):
                nc.vector.tensor_tensor(gates[:, :, g * PER:(g + 1) * PER], pick[:, :, :],
                                        spread(onehot[:, :, g], [P, T, PER]), ALU.mult)


def experts_one(book, ps, A, turned, gates, rows):
    nc = book.nc
    FC = FF // P
    with ExitStack() as ctx:
        sb = lambda name, shape: ctx.enter_context(nc.sbuf_tensor(name, shape, F32))
        wg = sb("wg", [P, KD, FF])
        wu = sb("wu", [P, KD, FF])
        wd = sb("wd", [P, FC, D])
        act_out = sb("act_out", [P, 2, HALF])
        hid = sb("hid", [P, FC, S])
        gate = sb("gate_e", [P, T])
        with Stage(book, "scaled") as (block, scaled):
            @block.vector
            def _(dve):
                for t in range(T):
                    nc.vector.tensor_scalar(rows[:, t, :], rows[:, t, :], ALPHA, None, ALU.mult)
        with nc.Fori(0, EXPERTS) as e:
            with Stage(book, "up_in", "down_in", "gate_full", "up_full", "silu_done", "hid_ready", "down_full",
                       "added", "gate_copied") as (
                    block, up_in, down_in, gate_full, up_full, silu_done, hid_ready, down_full, added, gate_copied):

                @block.sync
                def _(sp):
                    one = bass.ds(e, 1)
                    sp.dma_start(wg[:, :, :], A["w_gate"][one].rearrange("a (k p) f -> p (a k) f", p=P)).then_inc(up_in, 16)
                    sp.dma_start(wu[:, :, :], A["w_up"][one].rearrange("a (k p) f -> p (a k) f", p=P)).then_inc(up_in, 16)
                    sp.dma_start(wd[:, :, :], A["w_down"][one].rearrange("a (k p) f -> p (a k) f", p=P)).then_inc(down_in, 16)

                @block.tensor
                def _(pe):
                    pe.wait_ge(up_in, 32)
                    g = 0
                    for h in range(2):
                        for f in range(FC):
                            if g >= 2:
                                pe.wait_ge(hid_ready, g - 1)
                            for k in range(KD):
                                last = nc.tensor.matmul(ps[:, g % 2, :], wg[:, k, tile(f)], turned[:, k, tile(h, HALF)],
                                                        start=(k == 0), stop=(k == KD - 1))
                            last.then_inc(gate_full, 1)
                            for k in range(KD):
                                last = nc.tensor.matmul(ps[:, 2 + g % 2, :], wu[:, k, tile(f)],
                                                        turned[:, k, tile(h, HALF)], start=(k == 0), stop=(k == KD - 1))
                            last.then_inc(up_full, 1)
                            g += 1
                    pe.wait_ge(down_in, 16)
                    for g in range(2 * T):
                        t, h = divmod(g, 2)
                        if g == 0:
                            pe.wait_ge(hid_ready, 2)
                        if t == 4:
                            pe.wait_ge(hid_ready, 4)
                        if g >= 4:
                            pe.wait_ge(added, g - 3)
                        for f in range(FC):
                            last = nc.tensor.matmul(ps[:, 4 + g % 4, :], hid[:, f, tile(t)], wd[:, f, tile(h, HALF)],
                                                    start=(f == 0), stop=(f == FC - 1))
                        last.then_inc(down_full, 1)

                @block.scalar
                def _(act):
                    for g in range(4):
                        act.wait_ge(gate_full, g + 1)
                        if g >= 2:
                            act.wait_ge(hid_ready, g - 1)
                        nc.scalar.activation(act_out[:, g % 2, :], ps[:, g % 2, :], ACT.Silu).then_inc(silu_done, 1)

                @block.vector
                def _(dve):
                    nc.vector.tensor_copy(gate[:, :], gates[:, :, bass.ds(e, 1)].rearrange("p t a -> p (t a)"))\
                        .then_inc(gate_copied, 1)
                    for g in range(4):
                        h, f = divmod(g, 2)
                        dve.wait_ge(silu_done, g + 1)
                        dve.wait_ge(up_full, g + 1)
                        nc.vector.tensor_tensor(hid[:, f, tile(h, HALF)], act_out[:, g % 2, :], ps[:, 2 + g % 2, :],
                                                ALU.mult).then_inc(hid_ready, 1)
                    dve.wait_ge(gate_copied, 1)
                    for g in range(2 * T):
                        t, h = divmod(g, 2)
                        dve.wait_ge(down_full, g + 1)
                        out = rows[:, t, tile(h, HALF)]
                        nc.vector.scalar_tensor_tensor(out=out, in0=ps[:, 4 + g % 4, :], scalar=gate[:, t:t + 1],
                                                       in1=out, op0=ALU.mult, op1=ALU.add).then_inc(added, 1)
            with Stage(book) as (block,):
                pass


def project_two(book, ps, A, layer, turned, qk, rows_out):
    nc = book.nc
    M, W = 10, 768
    with ExitStack() as ctx, Stage(book, "w_in0", "w_in1", "w_in2", "w_rows_in", "full", "read") as (
            block, w_in0, w_in1, w_in2, w_rows_in, full, read):
        w_in = [w_in0, w_in1, w_in2]
        pieces = [(0, 2), (2, 6), (6, 10)]
        piece_of = [n for n, (a, b) in enumerate(pieces) for _ in range(a, b)]
        wt = ctx.enter_context(nc.sbuf_tensor("wt2", [P, M, KD, P], F32))
        wr = ctx.enter_context(nc.sbuf_tensor("wr2", [P, KD, W], F32))
        mine = bass.ds(layer * P, P)

        @block.sync
        def _(sp):
            for n, (a, b) in enumerate(pieces):
                sp.dma_start(wt[:, a:b], A["w_turned_2"][mine, a:b]).then_inc(w_in[n], 16)
            sp.dma_start(wr[:, :, :], A["w_rows_2"][mine]).then_inc(w_rows_in, 16)

        @block.tensor
        def _(pe):
            g = 0
            for m in range(M):
                pe.wait_ge(w_in[piece_of[m]], 16)
                for h in range(2):
                    if g >= 8:
                        pe.wait_ge(read, g - 7)
                    for k in range(KD):
                        last = nc.tensor.matmul(ps[:, g % 8, :], wt[:, m, k, :], turned[:, k, tile(h, HALF)],
                                                start=(k == 0), stop=(k == KD - 1))
                    last.then_inc(full, 1)
                    g += 1
            pe.wait_ge(w_rows_in, 16)
            for t in range(T):
                for a, b in ((0, BANK), (BANK, W)):
                    pe.wait_ge(read, g - 7)
                    for k in range(KD):
                        last = nc.tensor.matmul(ps[:, g % 8, 0:b - a], turned[:, k, tile(t)], wr[:, k, a:b],
                                                start=(k == 0), stop=(k == KD - 1))
                    last.then_inc(full, 1)
                    g += 1

        @block.scalar
        def _(act):
            g = 0
            for m in range(M):
                for h in range(2):
                    act.wait_ge(full, g + 1)
                    nc.scalar.activation(qk[:, m, tile(h, HALF)], ps[:, g % 8, :], ACT.Copy).then_inc(read, 1)
                    g += 1
            for t in range(T):
                for a, b in ((0, BANK), (BANK, W)):
                    act.wait_ge(full, g + 1)
                    nc.scalar.activation(rows_out[:, t, a:b], ps[:, g % 8, 0:b - a], ACT.Copy).then_inc(read, 1)
                    g += 1


def expand_latents(book, ps, A, layer, latents, k_rope, q, k, v):
    nc = book.nc
    H = MLA_HEADS
    with ExitStack() as ctx, Stage(book, "w_in", "full", "read", "shared") as (block, w_in, full, read, shared):
        wq = ctx.enter_context(nc.sbuf_tensor("w_uq", [P, 2, H * MLA_D], F32))
        wkv = ctx.enter_context(nc.sbuf_tensor("w_ukv", [P, 2 * H * HD], F32))
        mine = bass.ds(layer * P, P)

        @block.sync
        def _(sp):
            sp.dma_start(wq[:, :, :], A["mla_w_uq"][mine]).then_inc(w_in, 16)
            sp.dma_start(wkv[:, :], A["mla_w_ukv"][mine]).then_inc(w_in, 16)

        @block.tensor
        def _(pe):
            pe.wait_ge(w_in, 32)
            g = 0
            for h in range(H):
                for s in range(2):
                    if g >= 8:
                        pe.wait_ge(read, g - 7)
                    for c in range(2):
                        last = nc.tensor.matmul(ps[0:MLA_D, g % 8, :], wq[:, c, h * MLA_D:(h + 1) * MLA_D],
                                                latents[:, c, tile(s, HALF)], start=(c == 0), stop=(c == 1))
                    last.then_inc(full, 1)
                    g += 1
            for h in range(H):
                for s in range(2):
                    pe.wait_ge(read, g - 7)
                    nc.tensor.matmul(ps[0:HD, g % 8, :], wkv[:, h * HD:(h + 1) * HD], latents[:, 2, tile(s, HALF)],
                                     start=True, stop=True).then_inc(full, 1)
                    g += 1
            for t in range(T):
                pe.wait_ge(read, g - 7)
                nc.tensor.matmul(ps[:, g % 8, 0:H * HD], latents[:, 2, tile(t)], wkv[:, H * HD:2 * H * HD],
                                 start=True, stop=True).then_inc(full, 1)
                g += 1

        @block.scalar
        def _(act):
            g = 0
            for h in range(H):
                for s in range(2):
                    act.wait_ge(full, g + 1)
                    nc.scalar.activation(q[0:MLA_D, h, tile(s, HALF)], ps[0:MLA_D, g % 8, :], ACT.Copy)\
                        .then_inc(read, 1)
                    g += 1
            for h in range(H):
                for s in range(2):
                    act.wait_ge(full, g + 1)
                    nc.scalar.activation(k[0:HD, h, tile(s, HALF)], ps[0:HD, g % 8, :], ACT.Copy).then_inc(read, 1)
                    g += 1
            for t in range(T):
                act.wait_ge(full, g + 1)
                nc.scalar.activation(v[:, t, :], ps[:, g % 8, 0:H * HD], ACT.Copy).then_inc(read, 1)
                g += 1

        @block.vector
        def _(dve):
            for h in range(H):
                nc.vector.tensor_copy(k[HD:MLA_D, h, :], k_rope[HD:MLA_D, :])


def choose_tokens(book, ps, A, layer, ident, turned, gates, index):
    nc = book.nc
    rounds = CAP // 8
    with ExitStack() as ctx, Stage(book, "w_in", "full", "shifted", "exps", "aff_ready", "aff_turned", "dve_steps",
                                   "chosen", "slots_full") as (
            block, w_in, full, shifted, exps, aff_ready, aff_turned, steps, chosen, slots_full):
        sb = lambda name, shape, dt=F32: ctx.enter_context(nc.sbuf_tensor(name, shape, dt))
        w = sb("w_router", [P, KD, EXPERTS])
        aff = sb("aff", [P, T, EXPERTS])
        m = sb("aff_m", [P, T])
        total = sb("aff_total", [P, T])
        byexp = sb("byexp", [EXPERTS, S])
        best = sb("best_aff", [EXPERTS, CAP])
        where = sb("where", [EXPERTS, CAP], U32)
        wheref = sb("wheref", [EXPERTS, CAP])

        @block.sync
        def _(sp):
            sp.dma_start(w[:, :, :], A["w_router"][bass.ds(layer * P, P)]).then_inc(w_in, 16)

        @block.tensor
        def _(pe):
            pe.wait_ge(w_in, 16)
            for t in range(T):
                for k in range(KD):
                    last = nc.tensor.matmul(ps[:, t, 0:EXPERTS], turned[:, k, tile(t)], w[:, k, :], start=(k == 0),
                                            stop=(k == KD - 1))
                last.then_inc(full, 1)
            pe.wait_ge(aff_ready, 1)
            for t in range(T):
                last = nc.tensor.transpose(ps[0:EXPERTS, t // 4, tile(t % 4)], aff[:, t, :], ident[:, :])
            last.then_inc(aff_turned, 1)
            pe.wait_ge(chosen, 1)
            nc.tensor.transpose(ps[:, 2, 0:EXPERTS], best[:, :], ident[0:EXPERTS, 0:EXPERTS])
            nc.tensor.transpose(ps[:, 3, 0:EXPERTS], wheref[:, :], ident[0:EXPERTS, 0:EXPERTS]).then_inc(slots_full, 1)

        @block.scalar
        def _(act):
            act.wait_ge(shifted, 1)
            nc.scalar.activation(aff[:, :, :], aff[:, :, :], ACT.Exp).then_inc(exps, 1)

        @block.vector
        def _(dve):
            chain = Chain(dve, steps)
            dve.wait_ge(full, T)
            logit = ps[:, 0:T, 0:EXPERTS]
            chain.step(nc.vector.tensor_reduce(m[:, :], logit, AX.X, ALU.max))
            nc.vector.tensor_tensor(aff[:, :, :], logit, spread(m[:, :], [P, T, EXPERTS]), ALU.subtract)\
                .then_inc(shifted, 1)
            dve.wait_ge(exps, 1)
            chain.step(nc.vector.tensor_reduce(total[:, :], aff[:, :, :], AX.X, ALU.add))
            chain.step(nc.vector.reciprocal(total[:, :], total[:, :]))
            nc.vector.tensor_tensor(aff[:, :, :], aff[:, :, :], spread(total[:, :], [P, T, EXPERTS]), ALU.mult)\
                .then_inc(aff_ready, 1)
            dve.wait_ge(aff_turned, 1)
            chain.step(nc.vector.tensor_copy(byexp[:, :].rearrange("p (a b) -> p a b", a=2), ps[0:EXPERTS, 0:2, :]))
            for r in range(rounds):
                top = best[:, 8 * r:8 * r + 8]
                chain.step(nc.vector.max(top, byexp[:, :]))
                nc.vector.max_index(where[:, 8 * r:8 * r + 8], top, byexp[:, :])
                chain.step(nc.vector.match_replace(byexp[:, :], top, byexp[:, :], -1.0))
            nc.vector.tensor_copy(wheref[:, :], where[:, :]).then_inc(chosen, 1)
            dve.wait_ge(slots_full, 1)
            nc.vector.tensor_copy(gates[:, :], ps[:, 2, 0:EXPERTS])
            nc.vector.tensor_copy(index[:, :], ps[:, 3, 0:EXPERTS])


def experts_two(book, ps, A, layer, taken_in, summed, ident, gain, gates, index, rows_dram, sum_dram):
    nc = book.nc
    UNITS = 12
    with ExitStack() as ctx:
        sb = lambda name, shape, dt=F32: ctx.enter_context(nc.sbuf_tensor(name, shape, dt))
        ring = [sb(f"ring{n}", [P, 2048]) for n in range(UNITS)]
        taken = sb("taken", [P, D])
        xs = sb("xs_e", [P, KD, P])
        silu = sb("silu_e", [P, D])
        hid = sb("hid_e", [P, D])
        hidt = sb("hidt_e", [P, KD, P])
        out = sb("out_e", [P, D])
        take_from = sb("take_from", [P, 1], U32)
        add_to = sb("add_to", [P, 1], U32)
        gcol = sb("gcol", [P, 1])
        base = 16 * EXPERTS * layer
        unit_sems = [f"unit{n}_in" for n in range(UNITS)]
        wg, wu, wd = A["w_gate_2"], A["w_up_2"], A["w_down_2"]

        def unit_source(e, n):
            row = layer * EXPERTS + e
            if n < 8:
                h, kind, q = n // 4, (n // 2) % 2, n % 2
                w = (wg, wu)[kind]
                return w[bass.ds(row, 1)].rearrange("a (k p) f -> p (a k) f", p=P)[:, 4 * q:4 * q + 4, tile(h, HALF)]
            q = n - 8
            return wd[bass.ds(row, 1)].rearrange("a (k p) f -> p (a k) f", p=P)[:, 2 * q:2 * q + 2, :]

        def unit_view(n):
            return ring[n][:, :].rearrange("p (k f) -> p k f", k=4 if n < 8 else 2)

        with Stage(book, *unit_sems, "x_turned", "x_read", "silu_done", "hid_ready", "hid_turned",
                   "hid_read", "out_ready", "unit_used", "first_ready", "from_ready", "to_ready", "gate_ready") as (
                block, *sems):
            unit_in = sems[:UNITS]
            (x_turned, x_read, silu_done, hid_ready, hid_turned, hid_read, out_ready, unit_used,
             first_ready, from_ready, to_ready, gate_ready) = sems[UNITS:]

            @block.sync
            def _(sp):
                for n in range(UNITS):
                    sp.dma_start(unit_view(n), unit_source(0, n)).then_inc(unit_in[n], 16)
                with sp.Fori(1, EXPERTS) as e:
                    for n in range(UNITS):
                        sp.wait_ge(unit_used, (e - 1) * UNITS + n + 1)
                        sp.dma_start(unit_view(n), unit_source(e, n)).then_inc(unit_in[n], 16)

            @block.gpsimd
            def _(pool):
                def gather(e, ready):
                    nc.gpsimd.tensor_copy(take_from[:, :], index[:, bass.ds(e, 1)]).then_inc(ready, 1)
                    pool.wait_ge(ready, 1)
                    pool.wait_ge(ready, 1 if isinstance(e, int) else e)
                    pool.indirect_dma_start(taken[:, :], None, rows_dram,
                                            bass.IndirectOffsetOnAxis(ap=take_from[:, 0:1], axis=0))\
                        .then_inc(taken_in, 16)

                def scatter(e):
                    nc.gpsimd.tensor_copy(add_to[:, :], index[:, bass.ds(e, 1)]).then_inc(to_ready, 1)
                    pool.wait_ge(to_ready, 1)
                    pool.wait_ge(to_ready, e + 1)
                    pool.wait_ge(out_ready, 2 * e + 2)
                    pool.indirect_dma_start(sum_dram, bass.IndirectOffsetOnAxis(ap=add_to[:, 0:1], axis=0),
                                            out[:, :], None, compute_op=ALU.add).then_inc(summed, 16)
                    pool.wait_ge(summed, base + 16 * e + 16)

                gather(0, first_ready)
                with pool.Fori(0, EXPERTS - 1) as e:
                    pool.wait_ge(x_turned, 2 * e + 2)
                    gather(e + 1, from_ready)
                    scatter(e)
                scatter(EXPERTS - 1)

            @block.tensor
            def _(pe):
                def expert(e, later):
                    pe.wait_ge(taken_in, base + 16 * e + 16)
                    for h in range(2):
                        for j in range(4):
                            last = nc.tensor.transpose(ps[:, 4 + h, tile(j)], taken[:, tile(4 * h + j)], ident[:, :])
                        last.then_inc(x_turned, 1)
                    pe.wait_ge(x_read, 2 * e + 2)
                    for h in range(2):
                        for kind in range(2):
                            for q in range(2):
                                n = 4 * h + 2 * kind + q
                                pe.wait_ge(unit_in[n], 16 * e + 16)
                                for k in range(4):
                                    last = nc.tensor.matmul(ps[:, 2 * h + kind, :], xs[:, 4 * q + k, :],
                                                            unit_view(n)[:, k, :], start=(q == 0 and k == 0),
                                                            stop=(q == 1 and k == 3))
                                last.then_inc(unit_used, 1)
                    for h in range(2):
                        pe.wait_ge(hid_ready, 2 * e + h + 1)
                        for j in range(4):
                            last = nc.tensor.transpose(ps[:, 4 + h, tile(j)], hid[:, tile(4 * h + j)], ident[:, :])
                        last.then_inc(hid_turned, 1)
                    if later:
                        pe.wait_ge(out_ready, 2 * e)
                    for n in range(8, UNITS):
                        q = n - 8
                        pe.wait_ge(unit_in[n], 16 * e + 16)
                        if q % 2 == 0:
                            pe.wait_ge(hid_read, 2 * e + q // 2 + 1)
                        for k in range(2):
                            for h in range(2):
                                last = nc.tensor.matmul(ps[:, 6 + h, :], hidt[:, 2 * q + k, :],
                                                        unit_view(n)[:, k, tile(h, HALF)], start=(q == 0 and k == 0),
                                                        stop=(q == 3 and k == 1))
                        last.then_inc(unit_used, 1)

                expert(0, False)
                with pe.Fori(1, EXPERTS) as e:
                    expert(e, True)

            @block.scalar
            def _(act):
                with act.Fori(0, EXPERTS) as e:
                    for h in range(2):
                        act.wait_ge(x_turned, 2 * e + h + 1)
                        for j in range(4):
                            c = 4 * h + j
                            ins = nc.scalar.activation(xs[:, c, :], ps[:, 4 + h, tile(j)], ACT.Copy,
                                                       scale=gain[:, c:c + 1])
                        ins.then_inc(x_read, 1)
                    for h in range(2):
                        act.wait_ge(unit_used, e * UNITS + 4 * h + 2)
                        nc.scalar.activation(silu[:, tile(h, HALF)], ps[:, 2 * h, :], ACT.Silu).then_inc(silu_done, 1)
                    for h in range(2):
                        act.wait_ge(hid_turned, 2 * e + h + 1)
                        nc.scalar.activation(hidt[:, 4 * h:4 * h + 4, :].rearrange("p a b -> p (a b)"),
                                             ps[:, 4 + h, :], ACT.Copy).then_inc(hid_read, 1)

            @block.vector
            def _(dve):
                def expert(e, later):
                    if later:
                        dve.wait_ge(out_ready, 2 * e)
                    nc.vector.tensor_copy(gcol[:, :], gates[:, bass.ds(e, 1)]).then_inc(gate_ready, 1)
                    for h in range(2):
                        dve.wait_ge(silu_done, 2 * e + h + 1)
                        dve.wait_ge(unit_used, e * UNITS + 4 * h + 4)
                        nc.vector.tensor_tensor(hid[:, tile(h, HALF)], silu[:, tile(h, HALF)], ps[:, 2 * h + 1, :],
                                                ALU.mult).then_inc(hid_ready, 1)
                    dve.wait_ge(gate_ready, e + 1)
                    dve.wait_ge(unit_used, e * UNITS + UNITS)
                    if later:
                        dve.wait_ge(summed, base + 16 * e)
                    for h in range(2):
                        nc.vector.tensor_scalar(out[:, tile(h, HALF)], ps[:, 6 + h, :], gcol[:, :], None,
                                                ALU.mult).then_inc(out_ready, 1)

                expert(0, False)
                with dve.Fori(1, EXPERTS) as e:
                    expert(e, True)


def neighbourhood_items(qk, v, v_shifted, bias, out):
    items = []
    for t in range(T):
        for h in range(NA_HEADS):
            half = slice((h % 2) * HD, (h % 2 + 1) * HD)
            scores, add, values = [], [], []
            for j in range(2):
                r = 2 * t + j
                start = min(max(r - NA_H // 2, 0), GRID_H - NA_H)
                a, b = j * GRID_W, (j + 1) * GRID_W
                q = qk[half, h // 2, r * GRID_W:(r + 1) * GRID_W]
                k = qk[half, 2 + h // 2, start * GRID_W:(start + NA_H) * GRID_W]
                scores.append((a, b, q, k))
                dr = start - r + NA_H - 1
                add.append((a, b, bias[a:b, h, dr * GRID_W:(dr + NA_H) * GRID_W]))
                rows, first = (v, start // 2) if start % 2 == 0 else (v_shifted, (start - 1) // 2)
                values.append((a, b, [rows[:, first + c, h * HD:(h + 1) * HD] for c in range(4)]))
            items.append(dict(scores=scores, keys=NA_H * GRID_W, add=add, values=values,
                              out=out[:, t, h * HD:(h + 1) * HD], sink=None))
    return items


def sparse_items(raw, small, masks, moff, out):
    items = []
    for t in range(T):
        keys = (t + 1) * P
        for h in range(HEADS):
            half = slice((h % 2) * HD, (h % 2 + 1) * HD)
            items.append(dict(
                scores=[(0, P, raw[half, h // 2, tile(t)], raw[half, 6, 0:keys])], keys=keys,
                add=[(0, P, masks[:, moff[t]:moff[t] + keys])],
                values=[(0, P, [small[:, c, V0:V0 + HD] for c in range(t + 1)])],
                out=out[:, t, h * HD:(h + 1) * HD], sink=None))
    return items


def latent_items(q, k, v, out):
    return [dict(scores=[(0, P, q[0:MLA_D, h, tile(t)], k[0:MLA_D, h, :])], keys=S, add=None,
                 values=[(0, P, [v[:, c, h * HD:(h + 1) * HD] for c in range(T)])],
                 out=out[:, t, 256 + h * HD:256 + (h + 1) * HD], sink=None)
            for t in range(T) for h in range(MLA_HEADS)]


def window_items(qk, v, band, sink, out):
    items = []
    for t in range(T):
        lo, hi = max(t - 1, 0), min(t + 1, T - 1)
        keys = (hi - lo + 1) * P
        at = (lo - t + 1) * P
        for h in range(SWA_HEADS):
            half = slice((h % 2) * HD, (h % 2 + 1) * HD)
            kv = h // (SWA_HEADS // 2)
            items.append(dict(
                scores=[(0, P, qk[half, 4 + h // 2, tile(t)], qk[half, 7 + kv, lo * P:(hi + 1) * P])], keys=keys,
                add=[(0, P, band[:, at:at + keys])],
                values=[(0, P, [v[:, c, kv * HD:(kv + 1) * HD] for c in range(lo, hi + 1)])],
                out=out[:, t, 640 + h * HD:640 + (h + 1) * HD], sink=sink[:, h:h + 1]))
    return items


def block_one(book, ps, A, ident, ones, stats, stop=None):
    nc = book.nc
    moff = [P * t * (t + 1) // 2 for t in range(T)]
    with ExitStack() as outer:
        sb = lambda ctx, name, shape: ctx.enter_context(nc.sbuf_tensor(name, shape, F32))
        rows = None
        with ExitStack() as mid:
            raw = sb(mid, "raw", [P, ROPE_CHUNKS, S])
            small = sb(mid, "small", [P, T, SMALL])
            heads_out = sb(mid, "heads_out", [P, T, D])
            ssd = heads_out[:, :, HALF:D]
            with ExitStack() as early:
                xbc = sb(early, "xbc", [P, XBC_CHUNKS, S + CONV - 1])
                z = heads_out[:, :, 0:HALF]
                project_one(book, ps, A, raw, xbc, z, small)
                if stop == "proj": return
                with ExitStack() as part:
                    turner = sb(part, "turner", [P, P])
                    cos = sb(part, "cos", [P, S])
                    sin = sb(part, "sin", [P, S])
                    load(book, [(turner[:, :], A["turner64"]), (cos[:, :], A["cos64"]), (sin[:, :], A["sin64"])])
                    rotate(book, ps, turner, cos, sin, raw, ROPE_CHUNKS)
                mixed = sb(early, "mixed", [P, XBC_CHUNKS, S])
                convolve(book, A, xbc, mixed)
                if stop == "conv": return
                state_space(book, ps, A, ident, ones, mixed, small, z, ssd)
                if stop == "ssd": return
            masks = sb(mid, "masks", [P, moff[T - 1] + S])
            index_keys(book, ps, A, raw, small, masks, moff)
            if stop == "index": return
            attend(book, ps, ident, sparse_items(raw, small, masks, moff, heads_out), HD ** -0.5, S)
            if stop == "dsa": return
            turned = sb(mid, "turned_mix", [P, KD, S])
            turn(book, ps, ident, heads_out, turned, D)
            rows = heads_out
            mix_out(book, ps, A, A["w_out"], turned, ALPHA, rows, A["x"])
            gain = sb(mid, "ln_gain", [P, D])
            shift = sb(mid, "ln_shift", [P, D])
            load(book, [(gain[:, :], A["ln1_g"].broadcast_to([P, D])), (shift[:, :], A["ln1_b"].broadcast_to([P, D]))])
            layer_norm(book, rows, gain, shift, stats)
            turn(book, ps, ident, rows, turned, D)
            if stop == "ln1": return
            gates = sb(mid, "gates", [P, T, EXPERTS])
            route_one(book, ps, A, turned, gates)
            if stop == "route": return
            load(book, [(gain[:, :], A["ln2_g"].broadcast_to([P, D])), (shift[:, :], A["ln2_b"].broadcast_to([P, D]))])
            experts_one(book, ps, A, turned, gates, rows)
            if stop == "moe": return
            layer_norm(book, rows, gain, shift, stats, after=A["residual_rows"])
            if stop == "ln2": return


def load(book, pairs):
    nc = book.nc
    with Stage(book, "loaded") as (block, loaded):
        @block.sync
        def _(sp):
            for to, what in pairs:
                sp.dma_start(to, what).then_inc(loaded, 16)
            sp.wait_ge(loaded, 16 * len(pairs))


def block_two(book, ps, A, ident, stats, stop=None):
    nc = book.nc
    sb = lambda ctx, name, shape, dt=F32: ctx.enter_context(nc.sbuf_tensor(name, shape, dt))
    with ExitStack() as ctx:
        taken_in = ctx.enter_context(nc.semaphore("taken_in"))
        summed = ctx.enter_context(nc.semaphore("summed"))
        with nc.Fori(0, LAYERS) as layer:
            layer_two(book, ps, A, layer, taken_in, summed, ident, stats, sb, stop)
            with Stage(book) as (block,):
                pass
    if stop: return
    finish_two(book, A, stats, sb)


def layer_two(book, ps, A, layer, taken_in, summed, ident, stats, sb, stop):
    nc = book.nc
    with ExitStack() as whole:
        mine = bass.ds(layer * P, P)
        mix = sb(whole, "mix", [P, T, D])
        with ExitStack() as attention:
            qk = sb(attention, "qk", [P, 10, S])
            feats = sb(attention, "feats", [P, T, 768])
            with ExitStack() as part:
                xnt = sb(part, "xnt", [P, KD, S])
                gain = sb(part, "gain_a", [P, KD])
                junk = sb(part, "junk_a", [P, 2, D])
                load(book, [(mix[:, :, :], A["residual_rows"]), (gain[:, :], A["attn_norm"][mine])])
                root_mean_squares(book, mix, [(0, D)], RMS_EPS, stats, junk)
                turn(book, ps, ident, mix, xnt, D, gain)
                project_two(book, ps, A, layer, xnt, qk, feats)
            if stop == "proj2": return
            with ExitStack() as part:
                turner = sb(part, "turner2", [P, P])
                cos = sb(part, "cos2", [P, S])
                sin = sb(part, "sin2", [P, S])
                turner96 = sb(part, "turner96", [P, P])
                cos96 = sb(part, "cos96", [P, S])
                sin96 = sb(part, "sin96", [P, S])
                load(book, [(turner[:, :], A["turner64"]), (cos[:, :], A["cos64"]), (sin[:, :], A["sin64"]),
                            (turner96[:, :], A["turner96"]), (cos96[:, :], A["cos96"]), (sin96[:, :], A["sin96"])])
                rotate(book, ps, turner, cos, sin, qk[:, 4:9, :], 5)
                rotate(book, ps, turner96, cos96, sin96, qk[:, 9:10, :], 1, MLA_D)
            if stop == "rope2": return
            with ExitStack() as part:
                shifted = sb(part, "v_shifted", [P, T - 1, 256])
                bias = sb(part, "na_bias", [P, NA_HEADS, (2 * NA_H - 1) * GRID_W])
                outside = sb(part, "outside", [P, (2 * NA_H - 1) * GRID_W])
                band = sb(part, "band", [P, 3 * P])
                sink = sb(part, "sink", [P, SWA_HEADS])
                v = feats[:, :, 0:256]
                with Stage(book, "loaded", "masked", "scaled") as (block, loaded, masked, scaled):
                    @block.sync
                    def _(sp):
                        sp.dma_start(bias[0:GRID_W, :, :], A["na_rpb"][bass.ds(layer * GRID_W, GRID_W)]).then_inc(loaded, 16)
                        sp.dma_start(bias[GRID_W:P, :, :], A["na_rpb"][bass.ds(layer * GRID_W, GRID_W)]).then_inc(loaded, 16)
                        sp.dma_start(outside[:, :], A["na_outside"]).then_inc(loaded, 16)
                        sp.dma_start(band[:, :], A["swa_band"]).then_inc(loaded, 16)
                        sp.dma_start(sink[:, :], A["swa_sink"][bass.ds(layer, 1)].broadcast_to([P, SWA_HEADS])).then_inc(loaded, 16)
                        sp.dma_start(shifted[0:GRID_W, :, :], v[GRID_W:P, 0:T - 1, :]).then_inc(loaded, 16)
                        sp.dma_start(shifted[GRID_W:P, :, :], v[0:GRID_W, 1:T, :]).then_inc(loaded, 16)
                        sp.wait_ge(loaded, 16 * 7)

                    @block.vector
                    def _(dve):
                        dve.wait_ge(loaded, 16 * 7)
                        for h in range(NA_HEADS):
                            nc.vector.scalar_tensor_tensor(out=bias[:, h, :], in0=bias[:, h, :], scalar=HD ** 0.5,
                                                           in1=outside[:, :], op0=ALU.mult, op1=ALU.add)
                attend(book, ps, ident, neighbourhood_items(qk, v, shifted, bias, mix), HD ** -0.5, 512)
                if stop == "na": return
                attend(book, ps, ident, window_items(qk, feats[:, :, 640:768], band, sink, mix), HD ** -0.5, 3 * P)
            if stop == "swa": return
            with ExitStack() as part:
                q = sb(part, "q_mla", [P, MLA_HEADS, S])
                k = qk[:, 0:MLA_HEADS, :]
                v_mla = sb(part, "v_mla", [P, T, MLA_HEADS * HD])
                with ExitStack() as inner:
                    latents = sb(inner, "latents", [P, 3, S])
                    gain = sb(inner, "gain_l", [P, 3])
                    junk = sb(inner, "junk_l", [P, 2, 256])
                    load(book, [(gain[:, :], A["latent_gain"][mine])])
                    lat = feats[:, :, 256:640]
                    root_mean_squares(book, lat, [(0, 256), (256, 384)], RMS_EPS, stats, junk)
                    turn(book, ps, ident, lat, latents, 384, gain)
                    expand_latents(book, ps, A, layer, latents, qk[:, 9, :], q, k, v_mla)
                    turner96 = sb(inner, "turner96b", [P, P])
                    cos96 = sb(inner, "cos96b", [P, S])
                    sin96 = sb(inner, "sin96b", [P, S])
                    load(book, [(turner96[:, :], A["turner96"]), (cos96[:, :], A["cos96"]), (sin96[:, :], A["sin96"])])
                    rotate(book, ps, turner96, cos96, sin96, q, MLA_HEADS, MLA_D)
                attend(book, ps, ident, latent_items(q, k, v_mla, mix), MLA_D ** -0.5, S)
            if stop == "mla": return
        with ExitStack() as part:
            turned = sb(part, "mix_turned", [P, KD, S])
            gain = sb(part, "gain_g", [P, KD])
            gain_f = sb(part, "gain_f", [P, KD])
            junk = sb(part, "junk_g", [P, 2, D])
            load(book, [(gain[:, :], A["group_norm"][mine]), (gain_f[:, :], A["ffn_norm"][mine])])
            root_mean_squares(book, mix, [(0, 256), (256, 640), (640, 1024)], RMS_EPS, stats, junk)
            turn(book, ps, ident, mix, turned, D, gain)
            mix_out(book, ps, A, A["w_out_2"][mine], turned, 1.0, mix, A["residual_rows"])
            if stop == "mix2": return
            with Stage(book, "stored") as (block, stored):
                @block.sync
                def _(sp):
                    sp.dma_start(A["residual_rows"], mix[:, :, :]).then_inc(stored, 16)
                    sp.wait_ge(stored, 16)
            root_mean_squares(book, mix, [(0, D)], RMS_EPS, stats, junk)
            with Stage(book, "stored") as (block, stored):
                @block.sync
                def _(sp):
                    sp.dma_start(A["normed_rows"], mix[:, :, :]).then_inc(stored, 16)
                    sp.wait_ge(stored, 16)
            turn(book, ps, ident, mix, turned, D, gain_f)
            gates = sb(part, "slot_gates", [P, EXPERTS])
            index = sb(part, "slot_index", [P, EXPERTS], U32)
            choose_tokens(book, ps, A, layer, ident, turned, gates, index)
            if stop == "choose": return
            experts_two(book, ps, A, layer, taken_in, summed, ident, gain_f, gates, index, A["normed"], A["residual"])


def finish_two(book, A, stats, sb):
    nc = book.nc
    with ExitStack() as ctx:
        rows = sb(ctx, "final_rows", [P, T, D])
        gain = sb(ctx, "final_gain", [P, D])
        junk = sb(ctx, "junk_f", [P, 2, D])
        load(book, [(rows[:, :, :], A["residual_rows"]), (gain[:, :], A["final_norm"].broadcast_to([P, D]))])
        root_mean_squares(book, rows, [(0, D)], RMS_EPS, stats, junk)
        with Stage(book, "scaled", "stored") as (block, scaled, stored):
            @block.vector
            def _(dve):
                for t in range(T):
                    nc.vector.tensor_tensor(rows[:, t, :], rows[:, t, :], gain[:, :], ALU.mult).then_inc(scaled, 1)

            @block.sync
            def _(sp):
                for t in range(T):
                    sp.wait_ge(scaled, t + 1)
                    sp.dma_start(A["out"][tile(t), :], rows[:, t, :]).then_inc(stored, 16)
                sp.wait_ge(stored, 16 * T)


def program(nc, A, stop=None, only_two=False):
    with ExitStack() as ctx:
        ps = ctx.enter_context(nc.psum_tensor("ps", [P, 8, BANK], F32))
        ident = ctx.enter_context(nc.sbuf_tensor("ident", [P, P], F32))
        ones = ctx.enter_context(nc.sbuf_tensor("ones", [P, P], F32))
        stats = ctx.enter_context(nc.sbuf_tensor("stats", [P, 2, 3 * T], F32))
        book = Book(nc)
        A["residual"] = nc.dram_tensor("residual", (S, D), F32).ap()
        A["normed"] = nc.dram_tensor("normed", (S, D), F32).ap()
        A["residual_rows"] = A["residual"].rearrange("(t p) d -> p t d", p=P)
        A["normed_rows"] = A["normed"].rearrange("(t p) d -> p t d", p=P)
        A["x"] = A["x"].rearrange("(t p) d -> p t d", p=P)
        load(book, [(ident[:, :], A["ident"]), (ones[:, :], A["ones"])])
        if only_two:
            with ExitStack() as c2:
                r = c2.enter_context(nc.sbuf_tensor("rr", [P, T, D], F32))
                load(book, [(r[:, :, :], A["x"])])
                load(book, [(A["residual_rows"], r[:, :, :])])
        else:
            block_one(book, ps, A, ident, ones, stats, stop)
        if stop is None or stop.endswith("2") and stop != "ln2" or stop in ("na", "swa", "mla", "choose", "layer"):
            block_two(book, ps, A, ident, stats, stop)




def constants():
    f = np.float32
    out = {"ident": np.eye(P, dtype=f), "ones": np.ones((P, P), f)}
    out["upto"] = np.triu(np.ones((P, P), f))
    hidden = np.where(np.arange(P)[:, None] <= np.arange(P)[None, :], f(0), f(HIDE)).astype(f)
    out["hidden"] = np.ascontiguousarray(np.broadcast_to(hidden[:, None, :], (P, 4, P)))
    out["causal"] = np.ascontiguousarray(hidden.T)

    def rope(dim, before, after):
        inv = (f(10000.0) ** (-np.arange(0, dim, 2, dtype=f) / f(dim))).astype(f)
        ang = np.arange(S, dtype=f)[:, None] * inv[None, :]
        c, s = np.cos(ang).astype(f).T, np.sin(ang).astype(f).T
        cos = np.concatenate([np.ones((before, S), f), c, c, np.ones((after, S), f)])
        sin = np.concatenate([np.zeros((before, S), f), s, s, np.zeros((after, S), f)])
        turner = np.zeros((before + dim + after,) * 2, f)
        for i in range(dim // 2):
            turner[before + dim // 2 + i, before + i] = -1
            turner[before + i, before + dim // 2 + i] = 1
        return cos, sin, turner

    cos, sin, turner = rope(HD, 0, 0)
    out["cos64"], out["sin64"] = np.concatenate([cos, cos]), np.concatenate([sin, sin])
    out["turner64"] = np.kron(np.eye(2, dtype=f), turner)
    out["cos96"], out["sin96"], out["turner96"] = rope(32, HD, 32)
    c = np.arange(GRID_W)
    first = np.clip(c - NA_W // 2, 0, GRID_W - NA_W)
    inside = (c[None, :] >= first[:, None]) & (c[None, :] < first[:, None] + NA_W)
    outside = np.where(inside, f(0), f(HIDE)).astype(f)
    out["na_outside"] = np.tile(outside, (2, 2 * NA_H - 1))
    q, k = np.arange(P)[:, None], np.arange(3 * P)[None, :] - P
    out["swa_band"] = np.where(np.abs(q - k) <= 128, f(0), f(HIDE)).astype(f)
    return {n: np.ascontiguousarray(a) for n, a in out.items()}


def turned_weights(w, columns):
    k = w.shape[0] // P
    out = np.zeros((P, len(columns), k, P), w.dtype)
    for m, cols in enumerate(columns):
        cols = np.asarray(cols)
        there = cols >= 0
        out[:, m][:, :, there] = w[:, cols[there]].reshape(k, P, -1).transpose(1, 0, 2)
    return out


def row_weights(w):
    return np.ascontiguousarray(w.reshape(w.shape[0] // P, P, -1).transpose(1, 0, 2))


def columns_of(a):
    return np.ascontiguousarray(a.reshape(-1, P).T)


def arrays_of(i):
    r = np.arange
    A = constants()
    x = i["x"][0]
    A["x"], A["xt"] = x, np.ascontiguousarray(x.T)
    w = i["w_in"][0]
    k, ik = r(512, 576), r(896, 960)
    cols = [r(128 * m, 128 * m + 128) for m in range(4)] + [r(640, 768), r(768, 896)]
    cols += [np.concatenate([k, k]), np.concatenate([ik, ik])]
    cols += [r(1476 + 128 * m, 1476 + 128 * m + 128) for m in range(6)]
    A["w_turned"] = turned_weights(w, cols)
    A["w_rows"] = row_weights(w[:, np.concatenate([r(964, 1476), r(576, 640), r(960, 964), r(2244, 2252)])])
    A["conv_w"] = np.ascontiguousarray(i["conv_w"][0].T.reshape(6, P, CONV).transpose(1, 0, 2))
    A["conv_b"] = columns_of(i["conv_b"][0])
    for n in ("dt_bias", "a_log", "d_skip", "ssd_norm_w", "ln1_g", "ln1_b", "ln2_g", "ln2_b"):
        A[n] = i[n]
    A["w_out"] = row_weights(i["w_out"][0])
    A["w_route"] = row_weights(np.concatenate([i["w_route_group"][0], i["w_route_expert"][0]], 1))
    A["b_route"] = np.concatenate([i["b_route_group"], i["b_route_expert"]], 1)
    for n in ("w_gate", "w_up", "w_down"):
        A[n] = i[n][0]
        A[n + "_2"] = i[n + "_2"].reshape(LAYERS * EXPERTS, D, D)
    cols = [r(128 * m, 128 * m + 128) for m in range(4)] + [r(1184 + 128 * m, 1312 + 128 * m) for m in range(3)]
    cols += [np.concatenate([r(1568 + 64 * g, 1632 + 64 * g)] * 2) for g in range(2)]
    cols += [np.concatenate([np.full(64, -1), r(1152, 1184), np.full(32, -1)])]
    rows = np.concatenate([r(512, 768), r(768, 1024), r(1024, 1152), r(1696, 1824)])
    w = i["w_in_2"]
    cat = lambda f: np.concatenate([f(l) for l in range(LAYERS)])
    A["w_turned_2"] = cat(lambda l: turned_weights(w[l], cols))
    A["w_rows_2"] = cat(lambda l: row_weights(w[l][:, rows]))
    A["attn_norm"] = cat(lambda l: columns_of(i["attn_norm_2"][l]))
    A["group_norm"] = cat(lambda l: columns_of(i["group_norm_2"][l]))
    A["ffn_norm"] = cat(lambda l: columns_of(i["ffn_norm_2"][l]))
    A["latent_gain"] = cat(lambda l: columns_of(np.concatenate([i["mla_q_norm_2"][l], i["mla_kv_norm_2"][l]])))
    A["mla_w_uq"] = cat(lambda l: row_weights(i["mla_w_uq_2"][l]))
    kv = np.concatenate([np.concatenate([r(128 * h + s, 128 * h + s + 64) for h in range(MLA_HEADS)]) for s in (0, 64)])
    A["mla_w_ukv"] = cat(lambda l: np.ascontiguousarray(i["mla_w_ukv_2"][l][:, kv]))
    A["swa_sink"] = i["swa_sink_2"]
    A["w_out_2"] = cat(lambda l: row_weights(i["w_out_2"][l]))
    A["w_router"] = cat(lambda l: row_weights(i["w_router_2"][l]))
    A["final_norm"] = i["final_norm_2"].reshape(1, D)
    dc = np.clip(r(GRID_W)[None, :] - r(GRID_W)[:, None] + NA_W - 1, 0, 2 * NA_W - 2)
    A["na_rpb"] = cat(lambda l: i["na_rpb_2"][l][:, :, dc].transpose(2, 0, 1, 3).reshape(GRID_W, NA_HEADS, -1))
    return {n: np.ascontiguousarray(a) for n, a in A.items()}


def kernel(**inputs):
    import concourse.bacc as bacc
    from concourse.bass_utils import run_bass_kernel_spmd as run

    nc = bacc.Bacc("TRN2", target_bir_lowering=False, num_devices=1)
    arrays = arrays_of({n: np.asarray(a) for n, a in inputs.items()})
    A = {n: nc.dram_tensor("in_" + n, a.shape, mybir.dt.from_np(a.dtype), kind="ExternalInput").ap()
         for n, a in arrays.items()}
    A["out"] = nc.dram_tensor("out_0", (S, D), F32, kind="ExternalOutput").ap()
    program(nc, A)
    r = run(nc, [{"in_" + n: a for n, a in arrays.items()}], core_ids=[0])
    return r.results[0]["out_0"].reshape(1, S, D)
```

```python
from contextlib import ExitStack

import numpy as np

import concourse.bass as bass
from concourse import mybir

F32 = mybir.dt.float32
U32 = mybir.dt.uint32
ALU = mybir.AluOpType
ACT = mybir.ActivationFunctionType
AX = mybir.AxisListType

P = 128
S = 1024
D = 1024
T = S // P
KD = D // P
HALF = 512
BANK = 512

HEADS = 8
HD = 64
IDX_HEADS = 4
INDEXER_SCALE = (IDX_HEADS ** -0.5) * (HD ** -0.5)
TOPK = 256
SSD_HEADS = 8
STATE = 64
CONV = 4
EXPERTS = 16
FF = 256
ALPHA = 2.0 ** 0.25
LN_EPS = 1e-5
ROWS_Z = 512
V0, IW0, DT0 = 0, 64, 68
SMALL = 76
ROPE_CHUNKS = 8
XBC_CHUNKS = 6

LAYERS = 2
RMS_EPS = 1e-6
GRID_W = 64
GRID_H = S // GRID_W
NA_HEADS = 4
NA_H = 8
NA_W = 16
MLA_HEADS = 6
MLA_D = 96
SWA_HEADS = 6
CAP = 128
HIDE = -1e30
TAKEN = -3e38
BLOCKS = (2 * S - EXPERTS) // P + EXPERTS


class Book:

    def __init__(self, nc):
        self.nc = nc
        self.before = None
        self.count = 0


class Stage:

    def __init__(self, book, *names):
        self.book = book
        self.names = names

    def __enter__(self):
        book = self.book
        nc = book.nc
        book.count += 1
        self.own = ExitStack()
        self.sems = [self.own.enter_context(nc.semaphore(f"{n}_{book.count}")) for n in self.names]
        self.opened = ExitStack()
        block = self.opened.enter_context(nc.Block(no_gpsimd_drain=False))
        old = book.before.sems if book.before else []

        @block.sync
        def _(sp):
            for s in old:
                sp.sem_clear(s)

        return (block, *self.sems)

    def __exit__(self, kind, value, trace):
        if kind is not None:
            return False
        self.opened.close()
        if self.book.before:
            self.book.before.own.close()
        self.book.before = self
        return False


class Chain:

    def __init__(self, eng, sem):
        self.eng, self.sem, self.n = eng, sem, 0

    def step(self, ins):
        ins.then_inc(self.sem, 1)
        self.n += 1
        self.eng.wait_ge(self.sem, self.n)


def tile(t, size=P):
    return slice(t * size, (t + 1) * size)


def spread(ap, shape):
    return ap.unsqueeze(len(shape) - 1).broadcast_to(shape)




def turn(book, ps, ident, rows, turned, width, gain=None):
    nc = book.nc
    chunks = width // P
    groups = [(c, h) for c in range(chunks) for h in range(2)]
    with Stage(book, "turned_full", "read_by_act", "read_by_dve") as (block, full, by_act, by_dve):

        @block.tensor
        def _(pe):
            for g, (c, h) in enumerate(groups):
                if g >= 8:
                    if g % 2:
                        pe.wait_ge(by_dve, g // 2 - 3)
                    else:
                        pe.wait_ge(by_act, g // 2 - 3)
                for j in range(4):
                    t = 4 * h + j
                    last = nc.tensor.transpose(ps[:, g % 8, tile(j)], rows[:, t, tile(c)], ident[:, :])
                last.then_inc(full, 1)

        @block.scalar
        def _(act):
            for g, (c, h) in enumerate(groups):
                if g % 2 == 0:
                    act.wait_ge(full, g + 1)
                    out = turned[:, c, tile(h, HALF)]
                    if gain is None:
                        nc.scalar.activation(out, ps[:, g % 8, :], ACT.Copy).then_inc(by_act, 1)
                    else:
                        nc.scalar.activation(out, ps[:, g % 8, :], ACT.Copy, scale=gain[:, c:c + 1]).then_inc(by_act, 1)

        @block.vector
        def _(dve):
            for g, (c, h) in enumerate(groups):
                if g % 2 == 1:
                    dve.wait_ge(full, g + 1)
                    out = turned[:, c, tile(h, HALF)]
                    if gain is None:
                        nc.vector.tensor_copy(out, ps[:, g % 8, :]).then_inc(by_dve, 1)
                    else:
                        nc.vector.tensor_scalar(out, ps[:, g % 8, :], gain[:, c:c + 1], None, ALU.mult).then_inc(by_dve, 1)


def root_mean_squares(book, rows, segments, eps, stats, junk, out=None):
    nc = book.nc
    n = len(segments)
    if out is None:
        out = rows
    ss = stats[:, 0, 0:T * n].rearrange("p (t n) -> p t n", n=n)
    root = stats[:, 1, 0:T * n].rearrange("p (t n) -> p t n", n=n)
    with Stage(book, "squares", "means", "roots", "dve_steps") as (block, squares, means, roots, steps):

        @block.scalar
        def _(act):
            for t in range(T):
                for j, (a, b) in enumerate(segments):
                    if t * n + j >= 2:
                        act.wait_ge(squares, t * n + j - 1)
                    nc.scalar.activation(junk[:, (t * n + j) % 2, 0:b - a], rows[:, t, a:b], ACT.Square,
                                         accum_out=ss[:, t, j:j + 1]).then_inc(squares, 1)
            act.wait_ge(means, 1)
            act.wait_ge(squares, T * n)
            nc.scalar.activation(root, ss, ACT.Sqrt).then_inc(roots, 1)

        @block.vector
        def _(dve):
            chain = Chain(dve, steps)
            dve.wait_ge(squares, T * n)
            for j, (a, b) in enumerate(segments):
                ins = nc.vector.tensor_scalar(ss[:, :, j], ss[:, :, j], 1.0 / (b - a), eps, ALU.mult, ALU.add)
                if j == n - 1:
                    ins.then_inc(means, 1)
                else:
                    chain.step(ins)
            dve.wait_ge(roots, 1)
            chain.step(nc.vector.reciprocal(root, root))
            for t in range(T):
                for j, (a, b) in enumerate(segments):
                    nc.vector.tensor_scalar(out[:, t, a:b], rows[:, t, a:b], root[:, t, j:j + 1], None, ALU.mult)


def layer_norm(book, rows, gain, shift, stats, after=None):
    nc = book.nc
    with ExitStack() as ctx, Stage(book, "moments", "roots", "dve_steps", "scaled", "stored") as (
            block, moments, roots, steps, scaled, stored):
        bn = ctx.enter_context(nc.sbuf_tensor(f"bn{book.count}", [P, T, 2, 6], F32))
        mv = ctx.enter_context(nc.sbuf_tensor(f"mv{book.count}", [P, T, 2], F32))
        var, root = stats[:, 0, 0:T], stats[:, 1, 0:T]

        @block.vector
        def _(dve):
            chain = Chain(dve, steps)
            for t in range(T):
                for h in range(2):
                    ins = nc.vector.bn_stats(bn[:, t, h, :], rows[:, t, tile(h, HALF)])
            chain.step(ins)
            for t in range(T):
                ins = nc.vector.bn_aggr(mv[:, t, :], bn[:, t, :, :])
            chain.step(ins)
            nc.vector.tensor_scalar(var, mv[:, :, 1], LN_EPS, None, ALU.add).then_inc(moments, 1)
            dve.wait_ge(roots, 1)
            chain.step(nc.vector.reciprocal(root, root))
            for t in range(T):
                chain.step(nc.vector.tensor_scalar(rows[:, t, :], rows[:, t, :], mv[:, t, 0:1], root[:, t:t + 1],
                                                   ALU.subtract, ALU.mult))
                chain.step(nc.vector.tensor_tensor(rows[:, t, :], rows[:, t, :], gain[:, :], ALU.mult))
                nc.vector.tensor_tensor(rows[:, t, :], rows[:, t, :], shift[:, :], ALU.add).then_inc(scaled, 1)

        @block.scalar
        def _(act):
            act.wait_ge(moments, 1)
            nc.scalar.activation(root, var, ACT.Sqrt).then_inc(roots, 1)

        if after is not None:
            @block.sync
            def _(sp):
                sp.wait_ge(scaled, T)
                sp.dma_start(after, rows[:, :, :]).then_inc(stored, 16)
                sp.wait_ge(stored, 16)


def rotate(book, ps, turner, cos, sin, raw, chunks, parts=P):
    nc = book.nc
    with ExitStack() as ctx, Stage(book, "turned_full", "cos_done", "sin_done", "rotated") as (
            block, full, cos_done, sin_done, rotated):
        by_cos = ctx.enter_context(nc.sbuf_tensor(f"by_cos{book.count}", [P, 2, S], F32))
        by_sin = ctx.enter_context(nc.sbuf_tensor(f"by_sin{book.count}", [P, 2, S], F32))

        @block.tensor
        def _(pe):
            for n in range(chunks):
                if n >= 4:
                    pe.wait_ge(sin_done, n - 3)
                for h in range(2):
                    last = nc.tensor.matmul(ps[0:parts, 2 * (n % 4) + h, :], turner[0:parts, 0:parts],
                                            raw[0:parts, n, tile(h, HALF)], start=True, stop=True)
                last.then_inc(full, 1)

        @block.gpsimd
        def _(pool):
            for n in range(chunks):
                if n >= 2:
                    pool.wait_ge(rotated, n - 1)
                nc.gpsimd.tensor_tensor(by_cos[0:parts, n % 2, :], raw[0:parts, n, :], cos[0:parts, :],
                                        ALU.mult).then_inc(cos_done, 1)

        @block.vector
        def _(dve):
            for n in range(chunks):
                dve.wait_ge(full, n + 1)
                if n >= 2:
                    dve.wait_ge(rotated, n - 1)
                nc.vector.tensor_tensor(by_sin[0:parts, n % 2, :],
                                        ps[0:parts, 2 * (n % 4):2 * (n % 4) + 2, :].rearrange("p a b -> p (a b)"),
                                        sin[0:parts, :], ALU.mult).then_inc(sin_done, 1)
                dve.wait_ge(cos_done, n + 1)
                dve.wait_ge(sin_done, n + 1)
                nc.vector.tensor_tensor(raw[0:parts, n, :], by_cos[0:parts, n % 2, :], by_sin[0:parts, n % 2, :],
                                        ALU.add).then_inc(rotated, 1)


def attend(book, ps, ident, items, scale, widest):
    nc = book.nc
    N = len(items)
    groups = [(n, j) for n, item in enumerate(items) for j in range((item["keys"] // P + 3) // 4)]
    count = [len([1 for m, _ in groups if m == n]) for n in range(N)]
    first = [sum(count[:n]) for n in range(N)]
    by_act = [items[n]["add"] is not None or g % 2 == 0 for g, (n, _) in enumerate(groups)]

    def copied(eng, act_copied, dve_copied, g):
        if by_act[g]:
            eng.wait_ge(act_copied, sum(by_act[:g + 1]))
        else:
            eng.wait_ge(dve_copied, g + 1 - sum(by_act[:g + 1]))

    with ExitStack() as ctx, Stage(
            book, "scores_full", "logits_ready", "probs_ready", "turned_full", "act_copied", "dve_copied",
            "values_used", "dve_steps", "sink_done", "written") as (
            block, scores_full, logits_ready, probs_ready, turned_full, act_copied, dve_copied,
            values_used, steps, sink_done, written):
        sb = lambda name, shape: ctx.enter_context(nc.sbuf_tensor(f"{name}{book.count}", shape, F32))
        logits = sb("logits", [P, 2, widest])
        probs = sb("probs", [P, 2, widest])
        turned = sb("turned", [P, 4, BANK])
        top = sb("top", [P, 4])
        less = sb("less", [P, 4])
        total = sb("total", [P, 4])
        sunk = sb("sunk", [P, 4])
        over = sb("over", [P, 4])

        def raw(n, a=0, b=P):
            flat = ps[:, 2 * (n % 2):2 * (n % 2) + 2, :].rearrange("p a b -> p (a b)")
            return flat[a:b, 0:items[n]["keys"]]

        @block.tensor
        def _(pe):
            def score(n):
                item = items[n]
                if n >= 2:
                    pe.wait_ge(probs_ready, n - 1)
                for a, b, q, k in item["scores"]:
                    for h in range((item["keys"] + BANK - 1) // BANK):
                        lo, hi = h * BANK, min((h + 1) * BANK, item["keys"])
                        last = nc.tensor.matmul(ps[a:b, 2 * (n % 2) + h, 0:hi - lo], q, k[:, lo:hi],
                                                start=True, stop=True)
                last.then_inc(scores_full, 1)

            score(0)
            score(1)
            for n, item in enumerate(items):
                pe.wait_ge(probs_ready, n + 1)
                chunks = item["keys"] // P
                for j in range(count[n]):
                    g = first[n] + j
                    if g >= 2:
                        copied(pe, act_copied, dve_copied, g - 2)
                    for i in range(min(4, chunks - 4 * j)):
                        last = nc.tensor.transpose(ps[:, 4 + g % 2, tile(i)], probs[:, n % 2, tile(4 * j + i)],
                                                   ident[:, :])
                    last.then_inc(turned_full, 1)
                if n + 2 < N:
                    score(n + 2)
                if n >= 2:
                    pe.wait_ge(written, n - 1)
                for j in range(count[n]):
                    g = first[n] + j
                    copied(pe, act_copied, dve_copied, g)
                    for i in range(min(4, chunks - 4 * j)):
                        c = 4 * j + i
                        for a, b, values in item["values"]:
                            last = nc.tensor.matmul(ps[a:b, 6 + n % 2, 0:HD], turned[:, g % 4, i * P + a:i * P + b],
                                                    values[c], start=(c == 0), stop=(c == chunks - 1))
                    last.then_inc(values_used, 1)

        @block.scalar
        def _(act):
            def exponentials(n):
                item = items[n]
                s4 = slice(n % 4, n % 4 + 1)
                act.wait_ge(logits_ready, n + 1)
                if n >= 2:
                    act.wait_ge(turned_full, first[n - 1])
                if n >= 4:
                    act.wait_ge(written, n - 3)
                source = logits[:, n % 2, 0:item["keys"]] if item["add"] else raw(n)
                nc.scalar.activation(probs[:, n % 2, 0:item["keys"]], source, ACT.Exp, scale=scale,
                                     bias=less[:, s4], accum_out=total[:, s4]).then_inc(probs_ready, 1)
                if item["sink"] is not None:
                    nc.scalar.activation(sunk[:, s4], item["sink"], ACT.Exp, bias=less[:, s4]).then_inc(sink_done, 1)

            exponentials(0)
            exponentials(1)
            for n, item in enumerate(items):
                for j in range(count[n]):
                    g = first[n] + j
                    if by_act[g]:
                        act.wait_ge(turned_full, g + 1)
                        if g >= 4:
                            act.wait_ge(values_used, g - 3)
                        w = min(4, item["keys"] // P - 4 * j) * P
                        nc.scalar.activation(turned[:, g % 4, 0:w], ps[:, 4 + g % 2, 0:w],
                                             ACT.Copy).then_inc(act_copied, 1)
                if n + 2 < N:
                    exponentials(n + 2)

        @block.vector
        def _(dve):
            chain = Chain(dve, steps)

            def maxima(n):
                item = items[n]
                dve.wait_ge(scores_full, n + 1)
                if n >= 2:
                    dve.wait_ge(probs_ready, n - 1)
                if item["sink"] is not None and n >= 4:
                    dve.wait_ge(sink_done, n - 3)
                m = top[:, n % 4:n % 4 + 1]
                if item["add"]:
                    for a, b, add in item["add"]:
                        ins = nc.vector.tensor_tensor_reduce(
                            logits[a:b, n % 2, 0:item["keys"]], raw(n, a, b), add, 1.0, -3e38, ALU.add, ALU.max,
                            m[a:b, :])
                        if b < P:
                            ins.then_inc(steps, 1)
                            chain.n += 1
                    chain.step(ins)
                else:
                    chain.step(nc.vector.tensor_reduce(m, raw(n), AX.X, ALU.max))
                if item["sink"] is not None:
                    chain.step(nc.vector.tensor_scalar(m, m, scale, item["sink"], ALU.mult, ALU.max))
                nc.vector.tensor_scalar(less[:, n % 4:n % 4 + 1], m, -1.0 if item["sink"] is not None else -scale,
                                        None, ALU.mult).then_inc(logits_ready, 1)

            def write(n):
                item = items[n]
                dve.wait_ge(probs_ready, n + 1)
                s4 = slice(n % 4, n % 4 + 1)
                if item["sink"] is not None:
                    dve.wait_ge(sink_done, n + 1)
                    chain.step(nc.vector.tensor_tensor(total[:, s4], total[:, s4], sunk[:, s4], ALU.add))
                chain.step(nc.vector.reciprocal(over[:, s4], total[:, s4]))
                dve.wait_ge(values_used, first[n] + count[n])
                nc.vector.tensor_scalar(item["out"], ps[:, 6 + n % 2, 0:HD], over[:, s4], None,
                                        ALU.mult).then_inc(written, 1)

            maxima(0)
            maxima(1)
            for n, item in enumerate(items):
                for j in range(count[n]):
                    g = first[n] + j
                    if not by_act[g]:
                        dve.wait_ge(turned_full, g + 1)
                        if g >= 4:
                            dve.wait_ge(values_used, g - 3)
                        w = min(4, item["keys"] // P - 4 * j) * P
                        nc.vector.tensor_copy(turned[:, g % 4, 0:w], ps[:, 4 + g % 2, 0:w]).then_inc(dve_copied, 1)
                if n + 2 < N:
                    maxima(n + 2)
                write(n)




def project_one(book, ps, A, raw, xbc, z, small):
    nc = book.nc
    chunks = ROPE_CHUNKS + XBC_CHUNKS
    pieces = [(0, 2), (2, 8), (8, 14)]
    piece_of = [n for n, (a, b) in enumerate(pieces) for _ in range(a, b)]
    with ExitStack() as ctx, Stage(book, "x_in", "w_in0", "w_in1", "w_in2", "w_rows_in", "full", "read",
                                   "edge_zero") as (
            block, x_in, w_in0, w_in1, w_in2, w_rows_in, full, read, edge_zero):
        w_in = [w_in0, w_in1, w_in2]
        sb = lambda name, shape: ctx.enter_context(nc.sbuf_tensor(name, shape, F32))
        xt = sb("xt", [P, KD, S])
        wt = sb("wt", [P, chunks, KD, P])
        wr = sb("wr", [P, KD, ROWS_Z + SMALL])

        @block.sync
        def _(sp):
            a, b = pieces[0]
            sp.dma_start(wt[:, a:b], A["w_turned"][:, a:b]).then_inc(w_in[0], 16)
            sp.dma_start(xt[:, :, :], A["xt"].rearrange("(k p) s -> p k s", p=P)).then_inc(x_in, 16)
            for n, (a, b) in enumerate(pieces[1:]):
                sp.dma_start(wt[:, a:b], A["w_turned"][:, a:b]).then_inc(w_in[n + 1], 16)
            sp.dma_start(wr[:, :, :], A["w_rows"]).then_inc(w_rows_in, 16)

        @block.gpsimd
        def _(pool):
            nc.gpsimd.memset(xbc[:, :, 0:CONV - 1], 0.0).then_inc(edge_zero, 1)

        @block.tensor
        def _(pe):
            g = 0
            pe.wait_ge(x_in, 16)
            for m in range(chunks):
                pe.wait_ge(w_in[piece_of[m]], 16)
                for h in range(2):
                    if g >= 8:
                        pe.wait_ge(read, g - 7)
                    for k in range(KD):
                        last = nc.tensor.matmul(ps[:, g % 8, :], wt[:, m, k, :], xt[:, k, tile(h, HALF)],
                                                start=(k == 0), stop=(k == KD - 1))
                    last.then_inc(full, 1)
                    g += 1
            pe.wait_ge(w_rows_in, 16)
            for t in range(T):
                for a, b in ((0, ROWS_Z), (ROWS_Z, ROWS_Z + SMALL)):
                    pe.wait_ge(read, g - 7)
                    for k in range(KD):
                        last = nc.tensor.matmul(ps[:, g % 8, 0:b - a], xt[:, k, tile(t)], wr[:, k, a:b],
                                                start=(k == 0), stop=(k == KD - 1))
                    last.then_inc(full, 1)
                    g += 1

        @block.scalar
        def _(act):
            g = 0
            for m in range(chunks):
                for h in range(2):
                    act.wait_ge(full, g + 1)
                    if m < ROPE_CHUNKS:
                        out = raw[:, m, tile(h, HALF)]
                    else:
                        out = xbc[:, m - ROPE_CHUNKS, CONV - 1 + h * HALF:CONV - 1 + (h + 1) * HALF]
                    nc.scalar.activation(out, ps[:, g % 8, :], ACT.Copy).then_inc(read, 1)
                    g += 1
            for t in range(T):
                for out, w in ((z[:, t, :], ROWS_Z), (small[:, t, :], SMALL)):
                    act.wait_ge(full, g + 1)
                    nc.scalar.activation(out, ps[:, g % 8, 0:w], ACT.Copy).then_inc(read, 1)
                    g += 1


def convolve(book, A, xbc, mixed):
    nc = book.nc
    with ExitStack() as ctx, Stage(book, "taps_in", "dve_steps", "summed", "done") as (
            block, taps_in, steps, summed, done):
        taps = ctx.enter_context(nc.sbuf_tensor("taps", [P, XBC_CHUNKS, CONV], F32))
        bias = ctx.enter_context(nc.sbuf_tensor("conv_bias", [P, XBC_CHUNKS], F32))
        acc = ctx.enter_context(nc.sbuf_tensor("conv_acc", [P, 2, S], F32))

        @block.sync
        def _(sp):
            sp.dma_start(taps[:, :, :], A["conv_w"]).then_inc(taps_in, 16)
            sp.dma_start(bias[:, :], A["conv_b"]).then_inc(taps_in, 16)

        @block.vector
        def _(dve):
            chain = Chain(dve, steps)
            dve.wait_ge(taps_in, 32)
            for m in range(XBC_CHUNKS):
                if m >= 2:
                    dve.wait_ge(done, m - 1)
                a = acc[:, m % 2, :]
                chain.step(nc.vector.tensor_scalar(a, xbc[:, m, 0:S], taps[:, m, 0:1], None, ALU.mult))
                for j in range(1, CONV):
                    ins = nc.vector.scalar_tensor_tensor(out=a, in0=xbc[:, m, j:j + S], scalar=taps[:, m, j:j + 1],
                                                         in1=a, op0=ALU.mult, op1=ALU.add)
                    if j < CONV - 1:
                        chain.step(ins)
                ins.then_inc(summed, 1)

        @block.scalar
        def _(act):
            act.wait_ge(taps_in, 32)
            for m in range(XBC_CHUNKS):
                act.wait_ge(summed, m + 1)
                nc.scalar.activation(mixed[:, m, :], acc[:, m % 2, :], ACT.Silu,
                                     bias=bias[:, m:m + 1]).then_inc(done, 1)


def state_space(book, ps, A, ident, ones, mixed, small, z, ssd):
    nc = book.nc
    H = SSD_HEADS
    G = H // 2
    with ExitStack() as ctx:
        sb = lambda name, shape: ctx.enter_context(nc.sbuf_tensor(name, shape, F32))
        xs = sb("xs", [P, T, 5 * P])
        upto = sb("upto", [P, P])
        hidden = sb("hidden", [P, 4, P])
        bias = sb("dt_bias", [P, H])
        a_log = sb("a_log", [P, H])
        skip = sb("skip", [P, H])
        norm_w = sb("norm_w", [P, BANK])
        dt = sb("dt", [P, T, H])
        u1 = sb("u1", [P, T, H])
        u2 = sb("u2", [P, T, H])
        u3 = sb("u3", [P, T, H])
        adt = sb("adt", [P, T, H])
        cum = sb("cum", [P, T, H])
        less_cum = sb("less_cum", [P, T, H])
        grown = sb("grown", [P, T, H])
        fade = sb("fade", [P, T, H])
        last_fade = sb("last_fade", [P, T, H])
        ss = sb("ss_ssd", [P, T])
        root = sb("root_ssd", [P, T])

        with Stage(book, "consts_in", "full", "read", "exp_a", "exp_x", "one_more", "logged", "dt_ready",
                   "adt_ready", "cum_full", "cum_read", "fades", "dve_steps") as (
                block, consts_in, full, read, exp_a, exp_x, one_more, logged, dt_ready, adt_ready, cum_full,
                cum_read, fades, steps):
            raw_dt = small[:, :, DT0:DT0 + H]

            @block.sync
            def _(sp):
                for to, what in ((upto, A["upto"]), (bias, A["dt_bias"].broadcast_to([P, H])),
                                 (a_log, A["a_log"].broadcast_to([P, H])), (skip, A["d_skip"].broadcast_to([P, H])),
                                 (norm_w, A["ssd_norm_w"].broadcast_to([P, BANK]))):
                    sp.dma_start(to[:, :], what).then_inc(consts_in, 16)
                sp.dma_start(hidden[:, :, :], A["hidden"]).then_inc(consts_in, 16)

            @block.tensor
            def _(pe):
                for g in range(T * 2):
                    t, part = divmod(g, 2)
                    if g >= 8:
                        pe.wait_ge(read, g - 7)
                    for j in range(4 if part == 0 else 1):
                        c = 4 * part + j
                        last = nc.tensor.transpose(ps[:, g % 8, tile(j)], mixed[:, c, tile(t)], ident[:, :])
                    last.then_inc(full, 1)
                pe.wait_ge(read, T * 2)
                pe.wait_ge(adt_ready, 1)
                nc.tensor.matmul(ps[:, 0, 0:T * H], upto[:, :], adt[:, :, :].rearrange("p t h -> p (t h)"),
                                 start=True, stop=True).then_inc(cum_full, 1)
                nc.tensor.matmul(ps[:, 1, 0:T * H], ones[:, :], adt[:, :, :].rearrange("p t h -> p (t h)"),
                                 start=True, stop=True).then_inc(cum_full, 1)

            @block.scalar
            def _(act):
                act.wait_ge(consts_in, 96)
                nc.scalar.activation(a_log[:, :], a_log[:, :], ACT.Exp).then_inc(exp_a, 1)
                act.wait_ge(exp_x, 1)
                nc.scalar.activation(u1[:, :, :], u1[:, :, :], ACT.Exp, scale=-1.0).then_inc(exp_a, 1)
                act.wait_ge(one_more, 1)
                nc.scalar.activation(u3[:, :, :], u2[:, :, :], ACT.Ln).then_inc(logged, 1)
                for g in range(T * 2):
                    t, part = divmod(g, 2)
                    act.wait_ge(full, g + 1)
                    w = HALF if part == 0 else P
                    nc.scalar.activation(xs[:, t, part * HALF:part * HALF + w], ps[:, g % 8, 0:w],
                                         ACT.Copy).then_inc(read, 1)
                act.wait_ge(cum_read, 1)
                nc.scalar.activation(grown[:, :, :], cum[:, :, :], ACT.Exp).then_inc(fades, 1)
                nc.scalar.activation(fade[:, :, :], u1[:, :, :], ACT.Exp).then_inc(fades, 1)
                nc.scalar.activation(last_fade[:, :, :], u2[:, :, :], ACT.Exp).then_inc(fades, 1)

            @block.vector
            def _(dve):
                chain = Chain(dve, steps)
                dve.wait_ge(consts_in, 96)
                over = bias[:, :].unsqueeze(1).broadcast_to([P, T, H])
                chain.step(nc.vector.tensor_tensor(dt[:, :, :], raw_dt, over, ALU.add))
                chain.step(nc.vector.tensor_scalar(u1[:, :, :], dt[:, :, :], -1.0, None, ALU.mult))
                nc.vector.tensor_tensor(u1[:, :, :], u1[:, :, :], dt[:, :, :], ALU.max).then_inc(exp_x, 1)
                dve.wait_ge(exp_a, 2)
                nc.vector.tensor_scalar(u2[:, :, :], u1[:, :, :], 1.0, None, ALU.add).then_inc(one_more, 1)
                dve.wait_ge(one_more, 1)
                dve.wait_ge(logged, 1)
                chain.step(nc.vector.tensor_scalar(u2[:, :, :], u2[:, :, :], -1.0, None, ALU.add))
                chain.step(nc.vector.tensor_scalar(cum[:, :, :], u2[:, :, :], 0.0, None, ALU.is_equal))
                chain.step(nc.vector.tensor_tensor(u2[:, :, :], u2[:, :, :], cum[:, :, :], ALU.add))
                chain.step(nc.vector.tensor_tensor(u3[:, :, :], u3[:, :, :], cum[:, :, :], ALU.add))
                chain.step(nc.vector.reciprocal(u2[:, :, :], u2[:, :, :]))
                chain.step(nc.vector.tensor_tensor(u3[:, :, :], u3[:, :, :], u2[:, :, :], ALU.mult))
                chain.step(nc.vector.tensor_tensor(u3[:, :, :], u3[:, :, :], u1[:, :, :], ALU.mult))
                chain.step(nc.vector.tensor_scalar(dt[:, :, :], dt[:, :, :], 0.0, None, ALU.max))
                chain.step(nc.vector.tensor_tensor(dt[:, :, :], dt[:, :, :], u3[:, :, :], ALU.add))
                rate = a_log[:, :].unsqueeze(1).broadcast_to([P, T, H])
                chain.step(nc.vector.tensor_tensor(adt[:, :, :], dt[:, :, :], rate, ALU.mult))
                nc.vector.tensor_scalar(adt[:, :, :], adt[:, :, :], -1.0, None, ALU.mult).then_inc(adt_ready, 1)
                dve.wait_ge(cum_full, 2)
                cums = ps[:, 0, 0:T * H].rearrange("p (t h) -> p t h", t=T)
                lasts = ps[:, 1, 0:T * H].rearrange("p (t h) -> p t h", t=T)
                chain.step(nc.vector.tensor_copy(cum[:, :, :], cums))
                chain.step(nc.vector.tensor_scalar(less_cum[:, :, :], cum[:, :, :], -1.0, None, ALU.mult))
                chain.step(nc.vector.tensor_copy(u2[:, :, :], lasts))
                nc.vector.tensor_tensor(u1[:, :, :], u2[:, :, :], cum[:, :, :], ALU.subtract).then_inc(cum_read, 1)

        with Stage(book, "a_upto_ready", "spans_full", "spans_ready", "pairs_full", "pairs_ready", "x_ready",
                   "inner_full", "outer_full", "state_full", "state_ready", "decayed", "skip_ready", "y_ready",
                   "pool_steps", "dve_steps") as (
                block, a_upto_ready, spans_full, spans_ready, pairs_full, pairs_ready, x_ready, inner_full,
                outer_full, state_full, state_ready, decayed, skip_ready, y_ready, pool_steps, steps), \
                ExitStack() as inner:
            sb = lambda name, shape: inner.enter_context(nc.sbuf_tensor(name, shape, F32))
            a_upto = sb("a_upto", [P, H, P])
            spans = sb("spans", [P, H, P])
            pairs = sb("pairs", [P, H, P])
            xdt = sb("xdt", [P, 2, H * HD])
            xdec = sb("xdec", [P, 2, H * HD])
            state = sb("state", [P, G * HD])
            state_new = sb("state_new", [P, G * HD])
            fade_pair = sb("fade_pair", [P, T, G])
            skipped = sb("skipped", [P, 2, H * HD])
            yo = sb("yo", [P, H * HD])

            @block.tensor
            def _(pe):
                for c in range(T):
                    pe.wait_ge(a_upto_ready, c + 1)
                    for h in range(2):
                        if c >= 1 and h == 0:
                            pe.wait_ge(spans_ready, c)
                        nc.tensor.matmul(ps[:, h, :], ident[:, :], hidden[:, :, :].rearrange("p a b -> p (a b)"),
                                         start=True, stop=False)
                        last = nc.tensor.matmul(ps[:, h, :], ones[:, :],
                                                a_upto[:, 4 * h:4 * h + 4, :].rearrange("p a b -> p (a b)"),
                                                start=False, stop=True)
                    last.then_inc(spans_full, 1)
                    if c >= 1:
                        pe.wait_ge(pairs_ready, 2 * c)
                    for g in range(2):
                        half = slice(g * STATE, (g + 1) * STATE)
                        last = nc.tensor.matmul(ps[:, 2 + g, 0:P], mixed[half, 4, tile(c)], mixed[half, 5, tile(c)],
                                                start=True, stop=True)
                    last.then_inc(pairs_full, 1)
                    if c >= 1:
                        pe.wait_ge(state_ready, c)
                        pe.wait_ge(y_ready, c)
                        for g in range(2):
                            half = slice(g * STATE, (g + 1) * STATE)
                            last = nc.tensor.matmul(ps[:, 5 + 2 * g, 0:256], mixed[half, 5, tile(c)],
                                                    state[half, :], start=True, stop=True)
                        last.then_inc(outer_full, 1)
                    pe.wait_ge(x_ready, c + 1)
                    if c >= 1:
                        pe.wait_ge(state_ready, c)
                    for g in range(2):
                        last = nc.tensor.matmul(ps[g * STATE:(g + 1) * STATE, 6, 0:256],
                                                xs[:, c, HALF + g * STATE:HALF + (g + 1) * STATE],
                                                xdec[:, c % 2, g * 256:(g + 1) * 256], start=True, stop=True)
                    last.then_inc(state_full, 1)
                    pe.wait_ge(pairs_ready, 2 * c + 2)
                    if c >= 1:
                        pe.wait_ge(y_ready, c)
                    for h in range(H):
                        last = nc.tensor.matmul(ps[:, 4, h * HD:(h + 1) * HD], pairs[:, h, :],
                                                xdt[:, c % 2, h * HD:(h + 1) * HD], start=True, stop=True,
                                                skip_group_check=True)
                    last.then_inc(inner_full, 1)

            @block.scalar
            def _(act):
                for c in range(T):
                    act.wait_ge(spans_full, c + 1)
                    if c >= 1:
                        act.wait_ge(pairs_ready, 2 * c)
                    for h in range(H):
                        ins = nc.scalar.activation(spans[:, h, :], ps[:, h // 4, tile(h % 4)], ACT.Exp,
                                                   bias=less_cum[:, c, h:h + 1])
                    ins.then_inc(spans_ready, 1)

            @block.gpsimd
            def _(pool):
                def heads(ap):
                    return ap.rearrange("p (h d) -> p h d", d=HD)

                for g in range(2):
                    half = slice(g * STATE, (g + 1) * STATE)
                    nc.gpsimd.tensor_copy(fade_pair[half, :, :], last_fade[half, :, g * G:(g + 1) * G])\
                        .then_inc(decayed, 1)
                pool.wait_ge(decayed, 2)
                for c in range(T):
                    if c >= 2:
                        pool.wait_ge(inner_full, c - 1)
                        pool.wait_ge(y_ready, c - 1)
                    nc.gpsimd.tensor_tensor(heads(xdt[:, c % 2, :]), heads(xs[:, c, 0:HALF]),
                                            spread(dt[:, c, :], [P, H, HD]), ALU.mult).then_inc(pool_steps, 1)
                    pool.wait_ge(pool_steps, c + 1)
                    nc.gpsimd.tensor_tensor(heads(xdec[:, c % 2, :]), heads(xdt[:, c % 2, :]),
                                            spread(fade[:, c, :], [P, H, HD]), ALU.mult).then_inc(x_ready, 1)
                    nc.gpsimd.tensor_tensor(heads(skipped[:, c % 2, :]), heads(xs[:, c, 0:HALF]),
                                            spread(skip[:, :], [P, H, HD]), ALU.mult).then_inc(skip_ready, 1)

            @block.vector
            def _(dve):
                def heads(ap):
                    return ap.rearrange("p (h d) -> p h d", d=HD)

                chain = Chain(dve, steps)
                for c in range(T):
                    if c >= 1:
                        dve.wait_ge(spans_full, c)
                    nc.vector.tensor_tensor(a_upto[:, :, :], upto[:, :].unsqueeze(1).broadcast_to([P, H, P]),
                                            spread(adt[:, c, :], [P, H, P]), ALU.mult).then_inc(a_upto_ready, 1)
                    dve.wait_ge(spans_ready, c + 1)
                    dve.wait_ge(pairs_full, c + 1)
                    if c >= 1:
                        dve.wait_ge(inner_full, c)
                    for g in range(2):
                        nc.vector.tensor_tensor(pairs[:, 4 * g:4 * g + 4, :], spans[:, 4 * g:4 * g + 4, :],
                                                ps[:, 2 + g, 0:P].unsqueeze(1).broadcast_to([P, 4, P]),
                                                ALU.mult).then_inc(pairs_ready, 1)
                    dve.wait_ge(state_full, c + 1)
                    if c == 0:
                        dve.wait_ge(decayed, 2)
                        nc.vector.tensor_copy(state[:, :], ps[:, 6, 0:256]).then_inc(state_ready, 1)
                    else:
                        dve.wait_ge(outer_full, c)
                        chain.step(nc.vector.tensor_tensor(heads(state_new[:, :]), heads(state[:, :]),
                                                           spread(fade_pair[:, c, :], [P, G, HD]), ALU.mult))
                        nc.vector.tensor_tensor(state[:, :], state_new[:, :], ps[:, 6, 0:256],
                                                ALU.add).then_inc(state_ready, 1)
                    dve.wait_ge(skip_ready, c + 1)
                    dve.wait_ge(inner_full, c + 1)
                    y = ssd[:, c, :]
                    if c >= 1:
                        for g in range(2):
                            part = slice(g * 256, (g + 1) * 256)
                            ins = nc.vector.tensor_tensor(heads(yo[:, part]), heads(ps[:, 5 + 2 * g, 0:256]),
                                                          spread(grown[:, c, g * G:(g + 1) * G], [P, G, HD]),
                                                          ALU.mult)
                        chain.step(ins)
                        chain.step(nc.vector.tensor_tensor(yo[:, :], yo[:, :], ps[:, 4, :], ALU.add))
                        nc.vector.tensor_tensor(y, yo[:, :], skipped[:, c % 2, :], ALU.add).then_inc(y_ready, 1)
                    else:
                        nc.vector.tensor_tensor(y, ps[:, 4, :], skipped[:, c % 2, :], ALU.add).then_inc(y_ready, 1)
        with Stage(book, "gates", "gated", "squares", "means", "roots", "dve_steps") as (
                block, gates, gated, squares, means, roots, steps), ExitStack() as inner:
            junk = inner.enter_context(nc.sbuf_tensor("junk2_ssd", [P, HALF], F32))

            @block.scalar
            def _(act):
                for c in range(T):
                    nc.scalar.activation(z[:, c, :], z[:, c, :], ACT.Silu).then_inc(gates, 1)
                for c in range(T):
                    act.wait_ge(gated, c + 1)
                    nc.scalar.activation(junk[:, :], ssd[:, c, :], ACT.Square,
                                         accum_out=ss[:, c:c + 1]).then_inc(squares, 1)
                    act.wait_ge(squares, c + 1)
                act.wait_ge(means, 1)
                nc.scalar.activation(root[:, :], ss[:, :], ACT.Sqrt).then_inc(roots, 1)

            @block.vector
            def _(dve):
                chain = Chain(dve, steps)
                for c in range(T):
                    dve.wait_ge(gates, c + 1)
                    nc.vector.tensor_tensor(ssd[:, c, :], ssd[:, c, :], z[:, c, :], ALU.mult).then_inc(gated, 1)
                dve.wait_ge(gated, T)
                dve.wait_ge(squares, T)
                nc.vector.tensor_scalar(ss[:, :], ss[:, :], 1.0 / HALF, LN_EPS, ALU.mult, ALU.add).then_inc(means, 1)
                dve.wait_ge(roots, 1)
                chain.step(nc.vector.reciprocal(root[:, :], root[:, :]))
                for c in range(T):
                    nc.vector.scalar_tensor_tensor(out=ssd[:, c, :], in0=ssd[:, c, :], scalar=root[:, c:c + 1],
                                                   in1=norm_w[:, :], op0=ALU.mult, op1=ALU.mult)


def index_keys(book, ps, A, raw, small, masks, moff):
    nc = book.nc
    rounds = TOPK // 8
    with ExitStack() as ctx, Stage(book, "causal_in", "full", "positive", "scored", "dve_steps", "weights") as (
            block, causal_in, full, positive, scored, steps, weights):
        sb = lambda name, shape: ctx.enter_context(nc.sbuf_tensor(name, shape, F32))
        causal = sb("causal", [P, P])
        iw = sb("iw", [P, T, IDX_HEADS])
        relu = sb("relu", [P, 4, S])
        score = sb("score", [P, S])
        best = sb("best", [P, 8])

        @block.sync
        def _(sp):
            sp.dma_start(causal[:, :], A["causal"]).then_inc(causal_in, 16)

        @block.tensor
        def _(pe):
            n = 0
            for t in range(2, T):
                keys = (t + 1) * P
                for h in range(IDX_HEADS):
                    half = slice((h % 2) * HD, (h % 2 + 1) * HD)
                    if n >= 4:
                        pe.wait_ge(positive, n - 3)
                    for b in range((keys + BANK - 1) // BANK):
                        lo, hi = b * BANK, min((b + 1) * BANK, keys)
                        last = nc.tensor.matmul(ps[:, 2 * (n % 4) + b, 0:hi - lo], raw[half, 4 + h // 2, tile(t)],
                                                raw[half, 7, lo:hi], start=True, stop=True)
                    last.then_inc(full, 1)
                    n += 1

        @block.scalar
        def _(act):
            n = 0
            for t in range(2, T):
                keys = (t + 1) * P
                for h in range(IDX_HEADS):
                    act.wait_ge(full, n + 1)
                    if n >= 4:
                        act.wait_ge(scored, n - 3)
                    flat = ps[:, 2 * (n % 4):2 * (n % 4) + 2, :].rearrange("p a b -> p (a b)")
                    nc.scalar.activation(relu[:, n % 4, 0:keys], flat[:, 0:keys], ACT.Relu).then_inc(positive, 1)
                    n += 1

        @block.vector
        def _(dve):
            chain = Chain(dve, steps)
            chain.step(nc.vector.tensor_scalar(iw[:, :, :], small[:, :, IW0:IW0 + IDX_HEADS], INDEXER_SCALE, None,
                                               ALU.mult))
            dve.wait_ge(causal_in, 16)
            n = 0
            for t in range(T):
                keys = (t + 1) * P
                mask = masks[:, moff[t]:moff[t] + keys]
                if t < 2:
                    if t:
                        nc.vector.memset(mask[:, 0:t * P], 0.0)
                    nc.vector.tensor_copy(mask[:, t * P:keys], causal[:, :])
                    continue
                sc = score[:, 0:keys]
                for h in range(IDX_HEADS):
                    dve.wait_ge(positive, n + 1)
                    if h == 0:
                        ins = nc.vector.tensor_scalar(sc, relu[:, n % 4, 0:keys], iw[:, t, h:h + 1], None, ALU.mult)
                    else:
                        ins = nc.vector.scalar_tensor_tensor(out=sc, in0=relu[:, n % 4, 0:keys],
                                                             scalar=iw[:, t, h:h + 1], in1=sc, op0=ALU.mult,
                                                             op1=ALU.add)
                    ins.then_inc(scored, 1)
                    n += 1
                    dve.wait_ge(scored, n)
                chain.step(nc.vector.tensor_tensor(sc[:, t * P:keys], sc[:, t * P:keys], causal[:, :], ALU.add))
                for _ in range(rounds):
                    chain.step(nc.vector.max(best[:, :], sc))
                    chain.step(nc.vector.match_replace(sc, best[:, :], sc, TAKEN))
                chain.step(nc.vector.tensor_scalar(mask, sc, TAKEN / 2, HIDE, ALU.is_ge, ALU.mult))


def mix_out(book, ps, A, weights, turned, residual_scale, rows, source, chunks=KD):
    nc = book.nc
    with ExitStack() as ctx, Stage(book, "w_in", "rows_in", "full", "read") as (block, w_in, rows_in, full, read):
        w = ctx.enter_context(nc.sbuf_tensor(f"w_mix{book.count}", [P, chunks, D], F32))

        @block.sync
        def _(sp):
            sp.dma_start(w[:, :, :], weights).then_inc(w_in, 16)
            if source is not None:
                sp.dma_start(rows[:, :, :], source).then_inc(rows_in, 16)

        @block.tensor
        def _(pe):
            pe.wait_ge(w_in, 16)
            for g in range(2 * T):
                t, h = divmod(g, 2)
                if g >= 8:
                    pe.wait_ge(read, g - 7)
                for k in range(chunks):
                    last = nc.tensor.matmul(ps[:, g % 8, :], turned[:, k, tile(t)], w[:, k, tile(h, HALF)],
                                            start=(k == 0), stop=(k == chunks - 1))
                last.then_inc(full, 1)

        @block.vector
        def _(dve):
            if source is not None:
                dve.wait_ge(rows_in, 16)
            for g in range(2 * T):
                t, h = divmod(g, 2)
                dve.wait_ge(full, g + 1)
                out = rows[:, t, tile(h, HALF)]
                if residual_scale == 1.0:
                    nc.vector.tensor_tensor(out, out, ps[:, g % 8, :], ALU.add).then_inc(read, 1)
                else:
                    nc.vector.scalar_tensor_tensor(out=out, in0=out, scalar=residual_scale, in1=ps[:, g % 8, :],
                                                   op0=ALU.mult, op1=ALU.add).then_inc(read, 1)


def route_one(book, ps, A, turned, picked, weights):
    nc = book.nc
    GR, PER = 4, 4
    W = GR + EXPERTS
    with ExitStack() as ctx, Stage(book, "w_in", "bias_in", "full", "shifted", "exps", "dve_steps") as (
            block, w_in, bias_in, full, shifted, exps, steps):
        sb = lambda name, shape: ctx.enter_context(nc.sbuf_tensor(name, shape, F32))
        w = sb("w_route", [P, KD, W])
        bias = sb("b_route", [P, W])
        logit = sb("logit", [P, T, W])
        a = sb("route_a", [P, T, GR])
        b = sb("route_b", [P, T, GR])
        onehot = sb("onehot", [P, T, GR])
        free = sb("free", [P, T])
        m = sb("route_m", [P, T])
        m2 = sb("route_m2", [P, T])
        prob = sb("route_prob", [P, T])
        pick = sb("pick", [P, T, PER])
        both = sb("both", [P, T, PER])
        inner = sb("inner", [P, T, PER])
        tmp = sb("route_tmp", [P, T, PER])
        first_w, second_w = weights[:, 0, :], weights[:, 1, :]

        @block.sync
        def _(sp):
            sp.dma_start(w[:, :, :], A["w_route"]).then_inc(w_in, 16)
            sp.dma_start(bias[:, :], A["b_route"].broadcast_to([P, W])).then_inc(bias_in, 16)

        @block.tensor
        def _(pe):
            pe.wait_ge(w_in, 16)
            for t in range(T):
                for k in range(KD):
                    last = nc.tensor.matmul(ps[:, t, 0:W], turned[:, k, tile(t)], w[:, k, :], start=(k == 0),
                                            stop=(k == KD - 1))
                last.then_inc(full, 1)

        @block.scalar
        def _(act):
            act.wait_ge(shifted, 1)
            nc.scalar.activation(b[:, :, :], b[:, :, :], ACT.Exp).then_inc(exps, 1)
            act.wait_ge(shifted, 2)
            nc.scalar.activation(second_w, second_w, ACT.Exp).then_inc(exps, 1)

        @block.vector
        def _(dve):
            chain = Chain(dve, steps)

            def first_of(out, values, top):
                chain.step(nc.vector.tensor_tensor(out[:, :, :], values, spread(top, [P, T, 4]), ALU.is_equal))
                chain.step(nc.vector.tensor_scalar(free[:, :], out[:, :, 0], -1.0, 1.0, ALU.mult, ALU.add))
                for j in range(1, 4):
                    chain.step(nc.vector.tensor_tensor(out[:, :, j], out[:, :, j], free[:, :], ALU.mult))
                    if j < 3:
                        chain.step(nc.vector.tensor_tensor(free[:, :], free[:, :], out[:, :, j], ALU.subtract))

            dve.wait_ge(bias_in, 16)
            for t in range(T):
                dve.wait_ge(full, t + 1)
                ins = nc.vector.tensor_tensor(logit[:, t, :], ps[:, t, 0:W], bias[:, :], ALU.add)
            chain.step(ins)
            groups = logit[:, :, 0:GR]
            chain.step(nc.vector.tensor_reduce(m[:, :], groups, AX.X, ALU.max))
            nc.vector.tensor_tensor(b[:, :, :], groups, spread(m[:, :], [P, T, GR]), ALU.subtract).then_inc(shifted, 1)
            first_of(onehot, groups, m[:, :])
            dve.wait_ge(exps, 1)
            chain.step(nc.vector.tensor_reduce(prob[:, :], b[:, :, :], AX.X, ALU.add))
            chain.step(nc.vector.reciprocal(prob[:, :], prob[:, :]))
            for g in range(GR):
                of_group = logit[:, :, GR + g * PER:GR + (g + 1) * PER]
                to = inner if g == 0 else tmp
                chain.step(nc.vector.tensor_tensor(to[:, :, :], of_group, spread(onehot[:, :, g], [P, T, PER]),
                                                   ALU.mult))
                if g:
                    chain.step(nc.vector.tensor_tensor(inner[:, :, :], inner[:, :, :], tmp[:, :, :], ALU.add))
            chain.step(nc.vector.tensor_reduce(m[:, :], inner[:, :, :], AX.X, ALU.max))
            first_of(pick, inner[:, :, :], m[:, :])
            chain.step(nc.vector.scalar_tensor_tensor(out=tmp[:, :, :], in0=pick[:, :, :], scalar=HIDE,
                                                      in1=inner[:, :, :], op0=ALU.mult, op1=ALU.add))
            chain.step(nc.vector.tensor_reduce(m2[:, :], tmp[:, :, :], AX.X, ALU.max))
            nc.vector.tensor_tensor(second_w, m2[:, :], m[:, :], ALU.subtract).then_inc(shifted, 1)
            first_of(both, tmp[:, :, :], m2[:, :])
            dve.wait_ge(exps, 2)
            chain.step(nc.vector.tensor_scalar(first_w, second_w, 1.0, None, ALU.add))
            chain.step(nc.vector.reciprocal(first_w, first_w))
            chain.step(nc.vector.tensor_tensor(first_w, first_w, prob[:, :], ALU.mult))
            chain.step(nc.vector.tensor_tensor(second_w, second_w, first_w, ALU.mult))
            for n, of_four in enumerate((pick, both)):
                for g in range(GR):
                    nc.vector.tensor_tensor(picked[:, n, :, g * PER:(g + 1) * PER], of_four[:, :, :],
                                            spread(onehot[:, :, g], [P, T, PER]), ALU.mult)


def place_tokens(book, ps, A, picked, ones, slots, block_tokens, block_expert):
    nc = book.nc
    E = EXPERTS
    with ExitStack() as ctx, Stage(book, "consts_in", "counted_ready", "sums_full", "onehots_ready", "tokens_full",
                                   "dve_steps") as (block, consts_in, counted_ready, sums_full, onehots_ready,
                                                    tokens_full, steps):
        sb = lambda name, shape: ctx.enter_context(nc.sbuf_tensor(name, shape, F32))
        upto = sb("upto_p", [P, P])
        count = sb("count", [P, P])
        eights = sb("eights", [P, 8])
        token = sb("token", [P, T])
        both = sb("both_picked", [P, T, E])
        before = sb("before", [P, T, E])
        pos = sb("pos", [P, T, E])
        n_e = sb("n_e", [P, E])
        over = sb("over_e", [P, E, 8])
        blocks = sb("blocks_e", [P, E])
        ends = sb("ends_e", [P, E])
        starts = sb("starts_e", [P, E])
        past = sb("past", [P, BLOCKS, E])
        expert = sb("expert_b", [P, BLOCKS])
        prod = sb("prod", [P, 2, T, E])
        at = sb("at", [P, 2 * T])
        start = sb("start_t", [P, 2 * T])
        ge = sb("ge", [P, 2 * T, 7])
        q = sb("q_t", [P, 2 * T])
        within = sb("within", [P, 2 * T])
        blk = sb("blk", [P, 2 * T])
        slot = sb("slot", [P, 2 * T])
        hot_slot = sb("hot_slot", [P, 2 * T, P])
        hot_block = sb("hot_block", [P, 2 * T, BLOCKS])
        flat = lambda ap: ap.rearrange("p a b -> p (a b)")
        flat2 = lambda ap: ap.rearrange("p a b c -> p (a b) c")

        @block.sync
        def _(sp):
            for to, what in ((upto, A["upto"]), (count, A["count"]), (eights, A["eights"]), (token, A["token"])):
                sp.dma_start(to[:, :], what).then_inc(consts_in, 16)

        @block.tensor
        def _(pe):
            pe.wait_ge(consts_in, 64)
            pe.wait_ge(counted_ready, 1)
            nc.tensor.matmul(ps[:, 0, 0:T * E], upto[:, :], flat(both[:, :, :]), start=True, stop=True)\
                .then_inc(sums_full, 1)
            nc.tensor.matmul(ps[:, 1, 0:T * E], ones[:, :], flat(both[:, :, :]), start=True, stop=True)\
                .then_inc(sums_full, 1)
            pe.wait_ge(onehots_ready, 1)
            for n in range(2 * T):
                last = nc.tensor.matmul(ps[:, 2, 0:BLOCKS], hot_slot[:, n, :], hot_block[:, n, :], start=(n == 0),
                                        stop=(n == 2 * T - 1))
            last.then_inc(tokens_full, 1)

        @block.vector
        def _(dve):
            chain = Chain(dve, steps)
            tt, ts = nc.vector.tensor_tensor, nc.vector.tensor_scalar
            tt(both[:, :, :], picked[:, 0, :, :], picked[:, 1, :, :], ALU.add).then_inc(counted_ready, 1)
            dve.wait_ge(counted_ready, 1)
            dve.wait_ge(consts_in, 64)
            dve.wait_ge(sums_full, 2)
            inclusive = ps[:, 0, 0:T * E].rearrange("p (t e) -> p t e", t=T)
            totals = ps[:, 1, 0:T * E].rearrange("p (t e) -> p t e", t=T)
            chain.step(nc.vector.memset(before[:, 0, :], 0.0))
            for t in range(1, T):
                chain.step(tt(before[:, t, :], before[:, t - 1, :], totals[:, t - 1, :], ALU.add))
            chain.step(tt(n_e[:, :], before[:, T - 1, :], totals[:, T - 1, :], ALU.add))
            chain.step(tt(pos[:, :, :], inclusive, both[:, :, :], ALU.subtract))
            chain.step(tt(pos[:, :, :], pos[:, :, :], before[:, :, :], ALU.add))
            chain.step(tt(over[:, :, :], spread(n_e[:, :], [P, E, 8]), eights[:, :].unsqueeze(1).broadcast_to([P, E, 8]),
                          ALU.is_gt))
            chain.step(nc.vector.tensor_reduce(blocks[:, :], over[:, :, :], AX.X, ALU.add))
            chain.step(nc.vector.tensor_copy(ends[:, 0:1], blocks[:, 0:1]))
            for e in range(1, E):
                chain.step(tt(ends[:, e:e + 1], ends[:, e - 1:e], blocks[:, e:e + 1], ALU.add))
            chain.step(tt(starts[:, :], ends[:, :], blocks[:, :], ALU.subtract))
            chain.step(tt(past[:, :, :], spread(count[:, 0:BLOCKS], [P, BLOCKS, E]),
                          ends[:, :].unsqueeze(1).broadcast_to([P, BLOCKS, E]), ALU.is_ge))
            chain.step(nc.vector.tensor_reduce(expert[:, :], past[:, :, :], AX.X, ALU.add))
            chain.step(ts(block_expert[:, :], expert[:, :], float(E - 1), None, ALU.min))
            for n in range(2):
                chain.step(tt(prod[:, n, :, :], picked[:, n, :, :], pos[:, :, :], ALU.mult))
            chain.step(nc.vector.tensor_reduce(at[:, :], flat2(prod[:, :, :, :]), AX.X, ALU.add))
            for n in range(2):
                chain.step(tt(prod[:, n, :, :], picked[:, n, :, :],
                              starts[:, :].unsqueeze(1).broadcast_to([P, T, E]), ALU.mult))
            chain.step(nc.vector.tensor_reduce(start[:, :], flat2(prod[:, :, :, :]), AX.X, ALU.add))
            chain.step(tt(ge[:, :, :], spread(at[:, :], [P, 2 * T, 7]),
                          eights[:, 1:8].unsqueeze(1).broadcast_to([P, 2 * T, 7]), ALU.is_ge))
            chain.step(nc.vector.tensor_reduce(q[:, :], ge[:, :, :], AX.X, ALU.add))
            chain.step(nc.vector.scalar_tensor_tensor(out=within[:, :], in0=q[:, :], scalar=-float(P), in1=at[:, :],
                                                      op0=ALU.mult, op1=ALU.add))
            chain.step(tt(blk[:, :], start[:, :], q[:, :], ALU.add))
            chain.step(nc.vector.scalar_tensor_tensor(out=slot[:, :], in0=blk[:, :], scalar=float(P),
                                                      in1=within[:, :], op0=ALU.mult, op1=ALU.add))
            nc.vector.tensor_copy(slots.rearrange("p a b -> p (a b)"), slot[:, :])
            chain.step(tt(hot_slot[:, :, :], count[:, :].unsqueeze(1).broadcast_to([P, 2 * T, P]),
                          spread(within[:, :], [P, 2 * T, P]), ALU.is_equal))
            chain.step(tt(hot_block[:, :, :], count[:, 0:BLOCKS].unsqueeze(1).broadcast_to([P, 2 * T, BLOCKS]),
                          spread(blk[:, :], [P, 2 * T, BLOCKS]), ALU.is_equal))
            for n in range(2):
                ins = tt(hot_block[:, n * T:(n + 1) * T, :], hot_block[:, n * T:(n + 1) * T, :],
                         spread(token[:, :], [P, T, BLOCKS]), ALU.mult)
                if n == 0:
                    chain.step(ins)
            ins.then_inc(onehots_ready, 1)
            dve.wait_ge(tokens_full, 1)
            nc.vector.tensor_copy(block_tokens[:, :], ps[:, 2, 0:BLOCKS])


def experts_one(book, ps, A, ident, block_tokens, block_expert):
    nc = book.nc
    UP, DOWN = 4, 2
    UNITS = UP + DOWN
    with ExitStack() as ctx:
        sb = lambda name, shape, dt=F32: ctx.enter_context(nc.sbuf_tensor(name, shape, dt))
        w_up = sb("w_up_ring", [P, UP, KD // UP, 2 * FF])
        w_down = sb("w_down_ring", [P, DOWN, D])
        taken = sb("taken_1", [P, D])
        xs = sb("xs_1", [P, KD, P])
        silu = sb("silu_1", [P, FF])
        hid = sb("hid_1", [P, FF])
        hidt = sb("hidt_1", [P, 2, P])
        out = sb("out_1", [P, D])
        take_from = sb("take_from_1", [P, 1], U32)
        unit_sems = [f"unit{n}_in" for n in range(UNITS)]
        with Stage(book, *unit_sems, "x_turned", "x_read", "silu_done", "hid_ready", "hid_turned",
                   "hid_read", "out_ready", "stored", "unit_used", "first_ready", "from_ready") as (block, *sems):
            unit_in = sems[:UNITS]
            (x_turned, x_read, silu_done, hid_ready, hid_turned, hid_read, out_ready, stored, unit_used, first_ready,
             from_ready) = sems[UNITS:]
            taken_in = A["taken_one"]

            @block.sync
            def _(sp):
                def units(b, later):
                    expert = sp.value_load(block_expert[0:1, bass.ds(b, 1)], min_val=0, max_val=EXPERTS - 1)
                    one = bass.ds(expert, 1)
                    up = A["w_gate_up"][one].rearrange("a (k p) f -> p (a k) f", p=P)
                    down = A["w_down"][one].rearrange("a (k p) f -> p (a k) f", p=P)
                    for n in range(UNITS):
                        if later:
                            sp.wait_ge(unit_used, (b - 1) * UNITS + n + 1)
                        if n < UP:
                            sp.dma_start(w_up[:, n, :, :], up[:, 2 * n:2 * n + 2, :]).then_inc(unit_in[n], 16)
                        else:
                            sp.dma_start(w_down[:, n - UP, :], down[:, n - UP, :]).then_inc(unit_in[n], 16)

                def store(b):
                    sp.wait_ge(out_ready, 2 * b + 2)
                    sp.dma_start(A["expert_out"][bass.ds(b * P, P), :], out[:, :]).then_inc(stored, 16)

                units(0, False)
                with sp.Fori(1, BLOCKS) as b:
                    units(b, True)
                    store(b - 1)
                store(BLOCKS - 1)
                sp.wait_ge(stored, 16 * BLOCKS)

            @block.gpsimd
            def _(pool):
                def gather(b, ready):
                    nc.gpsimd.tensor_copy(take_from[:, :], block_tokens[:, bass.ds(b, 1)]).then_inc(ready, 1)
                    pool.wait_ge(ready, 1)
                    pool.wait_ge(ready, 1 if isinstance(b, int) else b)
                    pool.indirect_dma_start(taken[:, :], None, A["normed"],
                                            bass.IndirectOffsetOnAxis(ap=take_from[:, 0:1], axis=0))\
                        .then_inc(taken_in, 16)

                gather(0, first_ready)
                with pool.Fori(0, BLOCKS - 1) as b:
                    pool.wait_ge(x_turned, 2 * b + 2)
                    gather(b + 1, from_ready)

            @block.tensor
            def _(pe):
                def turn_rows(b):
                    pe.wait_ge(taken_in, 16 * b + 16)
                    for h in range(2):
                        for j in range(4):
                            last = nc.tensor.transpose(ps[:, 2 + h, tile(j)], taken[:, tile(4 * h + j)], ident[:, :])
                        last.then_inc(x_turned, 1)

                def up(b, later):
                    pe.wait_ge(x_read, 2 * b + 2)
                    for n in range(UP):
                        pe.wait_ge(unit_in[n], 16 * b + 16)
                        for k in range(2):
                            last = nc.tensor.matmul(ps[:, 0, :], xs[:, 2 * n + k, :], w_up[:, n, k, :],
                                                    start=(n == 0 and k == 0), stop=(n == UP - 1 and k == 1))
                        last.then_inc(unit_used, 1)

                def down(b, later):
                    pe.wait_ge(hid_ready, b + 1)
                    for j in range(2):
                        last = nc.tensor.transpose(ps[:, 1, tile(j)], hid[:, tile(j)], ident[:, :])
                    last.then_inc(hid_turned, 1)
                    if later:
                        pe.wait_ge(out_ready, 2 * b)
                    pe.wait_ge(hid_read, b + 1)
                    for n in range(DOWN):
                        pe.wait_ge(unit_in[UP + n], 16 * b + 16)
                        for h in range(2):
                            last = nc.tensor.matmul(ps[:, 4 + h, :], hidt[:, n, :], w_down[:, n, tile(h, HALF)],
                                                    start=(n == 0), stop=(n == DOWN - 1))
                        last.then_inc(unit_used, 1)

                turn_rows(0)
                up(0, False)
                turn_rows(1)
                down(0, False)
                with pe.Fori(1, BLOCKS - 1) as b:
                    up(b, True)
                    turn_rows(b + 1)
                    down(b, True)
                up(BLOCKS - 1, True)
                down(BLOCKS - 1, True)

            @block.scalar
            def _(act):
                def copy_x(b):
                    for h in range(2):
                        act.wait_ge(x_turned, 2 * b + h + 1)
                        nc.scalar.activation(xs[:, 4 * h:4 * h + 4, :].rearrange("p a b -> p (a b)"), ps[:, 2 + h, :],
                                             ACT.Copy).then_inc(x_read, 1)

                def gate(b):
                    act.wait_ge(unit_used, b * UNITS + UP)
                    nc.scalar.activation(silu[:, :], ps[:, 0, 0:FF], ACT.Silu).then_inc(silu_done, 1)

                copy_x(0)
                with act.Fori(0, BLOCKS - 1) as b:
                    gate(b)
                    copy_x(b + 1)
                gate(BLOCKS - 1)

            @block.vector
            def _(dve):
                def finish(b, later):
                    dve.wait_ge(silu_done, b + 1)
                    nc.vector.tensor_tensor(hid[:, :], silu[:, :], ps[:, 0, FF:2 * FF], ALU.mult).then_inc(hid_ready, 1)
                    dve.wait_ge(hid_turned, b + 1)
                    nc.vector.tensor_copy(hidt[:, :, :].rearrange("p a b -> p (a b)"), ps[:, 1, 0:FF])\
                        .then_inc(hid_read, 1)
                    dve.wait_ge(unit_used, b * UNITS + UNITS)
                    if later:
                        dve.wait_ge(stored, 16 * b)
                    for h in range(2):
                        nc.vector.tensor_copy(out[:, tile(h, HALF)], ps[:, 4 + h, :]).then_inc(out_ready, 1)

                finish(0, False)
                with dve.Fori(1, BLOCKS) as b:
                    finish(b, True)



def combine_one(book, A, slots, weights, rows):
    nc = book.nc
    with ExitStack() as ctx, Stage(book, "scaled", "added", "dve_steps") as (block, scaled, added, steps):
        part = ctx.enter_context(nc.sbuf_tensor("part", [P, 4, D], F32))
        came_in = A["came_in"]

        @block.gpsimd
        def _(pool):
            for n in range(2 * T):
                if n >= 4:
                    pool.wait_ge(added, n - 3)
                pool.indirect_dma_start(part[:, n % 4, :], None, A["expert_out"],
                                        bass.IndirectOffsetOnAxis(ap=slots[:, n % 2, n // 2:n // 2 + 1], axis=0))\
                    .then_inc(came_in[n % 4], 16)

        @block.vector
        def _(dve):
            for t in range(T):
                nc.vector.tensor_scalar(rows[:, t, :], rows[:, t, :], ALPHA, None, ALU.mult).then_inc(scaled, 1)
            dve.wait_ge(scaled, T)
            for n in range(2 * T):
                dve.wait_ge(came_in[n % 4], 16 * (n // 4 + 1))
                if n % 2:
                    dve.wait_ge(added, n)
                out = rows[:, n // 2, :]
                nc.vector.scalar_tensor_tensor(out=out, in0=part[:, n % 4, :], scalar=weights[:, n % 2, n // 2:n // 2 + 1],
                                               in1=out, op0=ALU.mult, op1=ALU.add).then_inc(added, 1)


def project_two(book, ps, A, layer, turned, qk, rows_out):
    nc = book.nc
    M, W = 10, 768
    with ExitStack() as ctx, Stage(book, "w_in0", "w_in1", "w_in2", "w_rows_in", "full", "read") as (
            block, w_in0, w_in1, w_in2, w_rows_in, full, read):
        w_in = [w_in0, w_in1, w_in2]
        pieces = [(0, 2), (2, 6), (6, 10)]
        piece_of = [n for n, (a, b) in enumerate(pieces) for _ in range(a, b)]
        wt = ctx.enter_context(nc.sbuf_tensor("wt2", [P, M, KD, P], F32))
        wr = ctx.enter_context(nc.sbuf_tensor("wr2", [P, KD, W], F32))
        mine = bass.ds(layer * P, P)

        @block.sync
        def _(sp):
            for n, (a, b) in enumerate(pieces):
                sp.dma_start(wt[:, a:b], A["w_turned_2"][mine, a:b]).then_inc(w_in[n], 16)
            sp.dma_start(wr[:, :, :], A["w_rows_2"][mine]).then_inc(w_rows_in, 16)

        @block.tensor
        def _(pe):
            g = 0
            for m in range(M):
                pe.wait_ge(w_in[piece_of[m]], 16)
                for h in range(2):
                    if g >= 8:
                        pe.wait_ge(read, g - 7)
                    for k in range(KD):
                        last = nc.tensor.matmul(ps[:, g % 8, :], wt[:, m, k, :], turned[:, k, tile(h, HALF)],
                                                start=(k == 0), stop=(k == KD - 1))
                    last.then_inc(full, 1)
                    g += 1
            pe.wait_ge(w_rows_in, 16)
            for t in range(T):
                for a, b in ((0, BANK), (BANK, W)):
                    pe.wait_ge(read, g - 7)
                    for k in range(KD):
                        last = nc.tensor.matmul(ps[:, g % 8, 0:b - a], turned[:, k, tile(t)], wr[:, k, a:b],
                                                start=(k == 0), stop=(k == KD - 1))
                    last.then_inc(full, 1)
                    g += 1

        @block.scalar
        def _(act):
            g = 0
            for m in range(M):
                for h in range(2):
                    act.wait_ge(full, g + 1)
                    nc.scalar.activation(qk[:, m, tile(h, HALF)], ps[:, g % 8, :], ACT.Copy).then_inc(read, 1)
                    g += 1
            for t in range(T):
                for a, b in ((0, BANK), (BANK, W)):
                    act.wait_ge(full, g + 1)
                    nc.scalar.activation(rows_out[:, t, a:b], ps[:, g % 8, 0:b - a], ACT.Copy).then_inc(read, 1)
                    g += 1


def expand_latents(book, ps, A, layer, latents, k_rope, q, k, v):
    nc = book.nc
    H = MLA_HEADS
    with ExitStack() as ctx, Stage(book, "w_in", "full", "read", "shared") as (block, w_in, full, read, shared):
        wq = ctx.enter_context(nc.sbuf_tensor("w_uq", [P, 2, H * MLA_D], F32))
        wkv = ctx.enter_context(nc.sbuf_tensor("w_ukv", [P, 2 * H * HD], F32))
        mine = bass.ds(layer * P, P)

        @block.sync
        def _(sp):
            sp.dma_start(wq[:, :, :], A["mla_w_uq"][mine]).then_inc(w_in, 16)
            sp.dma_start(wkv[:, :], A["mla_w_ukv"][mine]).then_inc(w_in, 16)

        @block.tensor
        def _(pe):
            pe.wait_ge(w_in, 32)
            g = 0
            for h in range(H):
                for s in range(2):
                    if g >= 8:
                        pe.wait_ge(read, g - 7)
                    for c in range(2):
                        last = nc.tensor.matmul(ps[0:MLA_D, g % 8, :], wq[:, c, h * MLA_D:(h + 1) * MLA_D],
                                                latents[:, c, tile(s, HALF)], start=(c == 0), stop=(c == 1))
                    last.then_inc(full, 1)
                    g += 1
            for h in range(H):
                for s in range(2):
                    pe.wait_ge(read, g - 7)
                    nc.tensor.matmul(ps[0:HD, g % 8, :], wkv[:, h * HD:(h + 1) * HD], latents[:, 2, tile(s, HALF)],
                                     start=True, stop=True).then_inc(full, 1)
                    g += 1
            for t in range(T):
                pe.wait_ge(read, g - 7)
                nc.tensor.matmul(ps[:, g % 8, 0:H * HD], latents[:, 2, tile(t)], wkv[:, H * HD:2 * H * HD],
                                 start=True, stop=True).then_inc(full, 1)
                g += 1

        @block.scalar
        def _(act):
            g = 0
            for h in range(H):
                for s in range(2):
                    act.wait_ge(full, g + 1)
                    nc.scalar.activation(q[0:MLA_D, h, tile(s, HALF)], ps[0:MLA_D, g % 8, :], ACT.Copy)\
                        .then_inc(read, 1)
                    g += 1
            for h in range(H):
                for s in range(2):
                    act.wait_ge(full, g + 1)
                    nc.scalar.activation(k[0:HD, h, tile(s, HALF)], ps[0:HD, g % 8, :], ACT.Copy).then_inc(read, 1)
                    g += 1
            for t in range(T):
                act.wait_ge(full, g + 1)
                nc.scalar.activation(v[:, t, :], ps[:, g % 8, 0:H * HD], ACT.Copy).then_inc(read, 1)
                g += 1

        @block.vector
        def _(dve):
            for h in range(H):
                nc.vector.tensor_copy(k[HD:MLA_D, h, :], k_rope[HD:MLA_D, :])


def choose_tokens(book, ps, A, layer, ident, turned, gates, index):
    nc = book.nc
    rounds = CAP // 8
    with ExitStack() as ctx, Stage(book, "w_in", "full", "shifted", "exps", "aff_ready", "aff_turned", "dve_steps",
                                   "chosen", "slots_full") as (
            block, w_in, full, shifted, exps, aff_ready, aff_turned, steps, chosen, slots_full):
        sb = lambda name, shape, dt=F32: ctx.enter_context(nc.sbuf_tensor(name, shape, dt))
        w = sb("w_router", [P, KD, EXPERTS])
        aff = sb("aff", [P, T, EXPERTS])
        m = sb("aff_m", [P, T])
        total = sb("aff_total", [P, T])
        byexp = sb("byexp", [EXPERTS, S])
        best = sb("best_aff", [EXPERTS, CAP])
        where = sb("where", [EXPERTS, CAP], U32)
        wheref = sb("wheref", [EXPERTS, CAP])

        @block.sync
        def _(sp):
            sp.dma_start(w[:, :, :], A["w_router"][bass.ds(layer * P, P)]).then_inc(w_in, 16)

        @block.tensor
        def _(pe):
            pe.wait_ge(w_in, 16)
            for t in range(T):
                for k in range(KD):
                    last = nc.tensor.matmul(ps[:, t, 0:EXPERTS], turned[:, k, tile(t)], w[:, k, :], start=(k == 0),
                                            stop=(k == KD - 1))
                last.then_inc(full, 1)
            pe.wait_ge(aff_ready, 1)
            for t in range(T):
                last = nc.tensor.transpose(ps[0:EXPERTS, t // 4, tile(t % 4)], aff[:, t, :], ident[:, :])
            last.then_inc(aff_turned, 1)
            pe.wait_ge(chosen, 1)
            nc.tensor.transpose(ps[:, 2, 0:EXPERTS], best[:, :], ident[0:EXPERTS, 0:EXPERTS])
            nc.tensor.transpose(ps[:, 3, 0:EXPERTS], wheref[:, :], ident[0:EXPERTS, 0:EXPERTS]).then_inc(slots_full, 1)

        @block.scalar
        def _(act):
            act.wait_ge(shifted, 1)
            nc.scalar.activation(aff[:, :, :], aff[:, :, :], ACT.Exp).then_inc(exps, 1)

        @block.vector
        def _(dve):
            chain = Chain(dve, steps)
            dve.wait_ge(full, T)
            logit = ps[:, 0:T, 0:EXPERTS]
            chain.step(nc.vector.tensor_reduce(m[:, :], logit, AX.X, ALU.max))
            nc.vector.tensor_tensor(aff[:, :, :], logit, spread(m[:, :], [P, T, EXPERTS]), ALU.subtract)\
                .then_inc(shifted, 1)
            dve.wait_ge(exps, 1)
            chain.step(nc.vector.tensor_reduce(total[:, :], aff[:, :, :], AX.X, ALU.add))
            chain.step(nc.vector.reciprocal(total[:, :], total[:, :]))
            nc.vector.tensor_tensor(aff[:, :, :], aff[:, :, :], spread(total[:, :], [P, T, EXPERTS]), ALU.mult)\
                .then_inc(aff_ready, 1)
            dve.wait_ge(aff_turned, 1)
            chain.step(nc.vector.tensor_copy(byexp[:, :].rearrange("p (a b) -> p a b", a=2), ps[0:EXPERTS, 0:2, :]))
            for r in range(rounds):
                top = best[:, 8 * r:8 * r + 8]
                chain.step(nc.vector.max(top, byexp[:, :]))
                nc.vector.max_index(where[:, 8 * r:8 * r + 8], top, byexp[:, :])
                chain.step(nc.vector.match_replace(byexp[:, :], top, byexp[:, :], -1.0))
            nc.vector.tensor_copy(wheref[:, :], where[:, :]).then_inc(chosen, 1)
            dve.wait_ge(slots_full, 1)
            nc.vector.tensor_copy(gates[:, :], ps[:, 2, 0:EXPERTS])
            nc.vector.tensor_copy(index[:, :], ps[:, 3, 0:EXPERTS])


def experts_two(book, ps, A, layer, taken_in, summed, ident, gain, gates, index, rows_dram, sum_dram):
    nc = book.nc
    UNITS = 12
    with ExitStack() as ctx:
        sb = lambda name, shape, dt=F32: ctx.enter_context(nc.sbuf_tensor(name, shape, dt))
        ring = [sb(f"ring{n}", [P, 2048]) for n in range(UNITS)]
        taken = sb("taken", [P, D])
        xs = sb("xs_e", [P, KD, P])
        silu = sb("silu_e", [P, D])
        hid = sb("hid_e", [P, D])
        hidt = sb("hidt_e", [P, KD, P])
        out = sb("out_e", [P, D])
        take_from = sb("take_from", [P, 1], U32)
        add_to = sb("add_to", [P, 1], U32)
        gcol = sb("gcol", [P, 1])
        base = 16 * EXPERTS * layer
        unit_sems = [f"unit{n}_in" for n in range(UNITS)]
        wg, wu, wd = A["w_gate_2"], A["w_up_2"], A["w_down_2"]

        def unit_source(e, n):
            row = layer * EXPERTS + e
            if n < 8:
                h, kind, q = n // 4, (n // 2) % 2, n % 2
                w = (wg, wu)[kind]
                return w[bass.ds(row, 1)].rearrange("a (k p) f -> p (a k) f", p=P)[:, 4 * q:4 * q + 4, tile(h, HALF)]
            q = n - 8
            return wd[bass.ds(row, 1)].rearrange("a (k p) f -> p (a k) f", p=P)[:, 2 * q:2 * q + 2, :]

        def unit_view(n):
            return ring[n][:, :].rearrange("p (k f) -> p k f", k=4 if n < 8 else 2)

        with Stage(book, *unit_sems, "x_turned", "x_read", "silu_done", "hid_ready", "hid_turned",
                   "hid_read", "out_ready", "unit_used", "first_ready", "from_ready", "to_ready", "gate_ready") as (
                block, *sems):
            unit_in = sems[:UNITS]
            (x_turned, x_read, silu_done, hid_ready, hid_turned, hid_read, out_ready, unit_used,
             first_ready, from_ready, to_ready, gate_ready) = sems[UNITS:]

            @block.sync
            def _(sp):
                for n in range(UNITS):
                    sp.dma_start(unit_view(n), unit_source(0, n)).then_inc(unit_in[n], 16)
                with sp.Fori(1, EXPERTS) as e:
                    for n in range(UNITS):
                        sp.wait_ge(unit_used, (e - 1) * UNITS + n + 1)
                        sp.dma_start(unit_view(n), unit_source(e, n)).then_inc(unit_in[n], 16)

            @block.gpsimd
            def _(pool):
                def gather(e, ready):
                    nc.gpsimd.tensor_copy(take_from[:, :], index[:, bass.ds(e, 1)]).then_inc(ready, 1)
                    pool.wait_ge(ready, 1)
                    pool.wait_ge(ready, 1 if isinstance(e, int) else e)
                    pool.indirect_dma_start(taken[:, :], None, rows_dram,
                                            bass.IndirectOffsetOnAxis(ap=take_from[:, 0:1], axis=0))\
                        .then_inc(taken_in, 16)

                def scatter(e):
                    nc.gpsimd.tensor_copy(add_to[:, :], index[:, bass.ds(e, 1)]).then_inc(to_ready, 1)
                    pool.wait_ge(to_ready, 1)
                    pool.wait_ge(to_ready, e + 1)
                    pool.wait_ge(out_ready, 2 * e + 2)
                    pool.indirect_dma_start(sum_dram, bass.IndirectOffsetOnAxis(ap=add_to[:, 0:1], axis=0),
                                            out[:, :], None, compute_op=ALU.add).then_inc(summed, 16)
                    pool.wait_ge(summed, base + 16 * e + 16)

                gather(0, first_ready)
                with pool.Fori(0, EXPERTS - 1) as e:
                    pool.wait_ge(x_turned, 2 * e + 2)
                    gather(e + 1, from_ready)
                    scatter(e)
                scatter(EXPERTS - 1)

            @block.tensor
            def _(pe):
                def expert(e, later):
                    pe.wait_ge(taken_in, base + 16 * e + 16)
                    for h in range(2):
                        for j in range(4):
                            last = nc.tensor.transpose(ps[:, 4 + h, tile(j)], taken[:, tile(4 * h + j)], ident[:, :])
                        last.then_inc(x_turned, 1)
                    pe.wait_ge(x_read, 2 * e + 2)
                    for h in range(2):
                        for kind in range(2):
                            for q in range(2):
                                n = 4 * h + 2 * kind + q
                                pe.wait_ge(unit_in[n], 16 * e + 16)
                                for k in range(4):
                                    last = nc.tensor.matmul(ps[:, 2 * h + kind, :], xs[:, 4 * q + k, :],
                                                            unit_view(n)[:, k, :], start=(q == 0 and k == 0),
                                                            stop=(q == 1 and k == 3))
                                last.then_inc(unit_used, 1)
                    for h in range(2):
                        pe.wait_ge(hid_ready, 2 * e + h + 1)
                        for j in range(4):
                            last = nc.tensor.transpose(ps[:, 4 + h, tile(j)], hid[:, tile(4 * h + j)], ident[:, :])
                        last.then_inc(hid_turned, 1)
                    if later:
                        pe.wait_ge(out_ready, 2 * e)
                    for n in range(8, UNITS):
                        q = n - 8
                        pe.wait_ge(unit_in[n], 16 * e + 16)
                        if q % 2 == 0:
                            pe.wait_ge(hid_read, 2 * e + q // 2 + 1)
                        for k in range(2):
                            for h in range(2):
                                last = nc.tensor.matmul(ps[:, 6 + h, :], hidt[:, 2 * q + k, :],
                                                        unit_view(n)[:, k, tile(h, HALF)], start=(q == 0 and k == 0),
                                                        stop=(q == 3 and k == 1))
                        last.then_inc(unit_used, 1)

                expert(0, False)
                with pe.Fori(1, EXPERTS) as e:
                    expert(e, True)

            @block.scalar
            def _(act):
                with act.Fori(0, EXPERTS) as e:
                    for h in range(2):
                        act.wait_ge(x_turned, 2 * e + h + 1)
                        for j in range(4):
                            c = 4 * h + j
                            ins = nc.scalar.activation(xs[:, c, :], ps[:, 4 + h, tile(j)], ACT.Copy,
                                                       scale=gain[:, c:c + 1])
                        ins.then_inc(x_read, 1)
                    for h in range(2):
                        act.wait_ge(unit_used, e * UNITS + 4 * h + 2)
                        nc.scalar.activation(silu[:, tile(h, HALF)], ps[:, 2 * h, :], ACT.Silu).then_inc(silu_done, 1)
                    for h in range(2):
                        act.wait_ge(hid_turned, 2 * e + h + 1)
                        nc.scalar.activation(hidt[:, 4 * h:4 * h + 4, :].rearrange("p a b -> p (a b)"),
                                             ps[:, 4 + h, :], ACT.Copy).then_inc(hid_read, 1)

            @block.vector
            def _(dve):
                def expert(e, later):
                    if later:
                        dve.wait_ge(out_ready, 2 * e)
                    nc.vector.tensor_copy(gcol[:, :], gates[:, bass.ds(e, 1)]).then_inc(gate_ready, 1)
                    for h in range(2):
                        dve.wait_ge(silu_done, 2 * e + h + 1)
                        dve.wait_ge(unit_used, e * UNITS + 4 * h + 4)
                        nc.vector.tensor_tensor(hid[:, tile(h, HALF)], silu[:, tile(h, HALF)], ps[:, 2 * h + 1, :],
                                                ALU.mult).then_inc(hid_ready, 1)
                    dve.wait_ge(gate_ready, e + 1)
                    dve.wait_ge(unit_used, e * UNITS + UNITS)
                    if later:
                        dve.wait_ge(summed, base + 16 * e)
                    for h in range(2):
                        nc.vector.tensor_scalar(out[:, tile(h, HALF)], ps[:, 6 + h, :], gcol[:, :], None,
                                                ALU.mult).then_inc(out_ready, 1)

                expert(0, False)
                with dve.Fori(1, EXPERTS) as e:
                    expert(e, True)


def neighbourhood_items(qk, v, v_shifted, bias, out):
    items = []
    for t in range(T):
        for h in range(NA_HEADS):
            half = slice((h % 2) * HD, (h % 2 + 1) * HD)
            scores, add, values = [], [], []
            for j in range(2):
                r = 2 * t + j
                start = min(max(r - NA_H // 2, 0), GRID_H - NA_H)
                a, b = j * GRID_W, (j + 1) * GRID_W
                q = qk[half, h // 2, r * GRID_W:(r + 1) * GRID_W]
                k = qk[half, 2 + h // 2, start * GRID_W:(start + NA_H) * GRID_W]
                scores.append((a, b, q, k))
                dr = start - r + NA_H - 1
                add.append((a, b, bias[a:b, h, dr * GRID_W:(dr + NA_H) * GRID_W]))
                rows, first = (v, start // 2) if start % 2 == 0 else (v_shifted, (start - 1) // 2)
                values.append((a, b, [rows[:, first + c, h * HD:(h + 1) * HD] for c in range(4)]))
            items.append(dict(scores=scores, keys=NA_H * GRID_W, add=add, values=values,
                              out=out[:, t, h * HD:(h + 1) * HD], sink=None))
    return items


def sparse_items(raw, small, masks, moff, out):
    items = []
    for t in range(T):
        keys = (t + 1) * P
        for h in range(HEADS):
            half = slice((h % 2) * HD, (h % 2 + 1) * HD)
            items.append(dict(
                scores=[(0, P, raw[half, h // 2, tile(t)], raw[half, 6, 0:keys])], keys=keys,
                add=[(0, P, masks[:, moff[t]:moff[t] + keys])],
                values=[(0, P, [small[:, c, V0:V0 + HD] for c in range(t + 1)])],
                out=out[:, t, h * HD:(h + 1) * HD], sink=None))
    return items


def latent_items(q, k, v, out):
    return [dict(scores=[(0, P, q[0:MLA_D, h, tile(t)], k[0:MLA_D, h, :])], keys=S, add=None,
                 values=[(0, P, [v[:, c, h * HD:(h + 1) * HD] for c in range(T)])],
                 out=out[:, t, 256 + h * HD:256 + (h + 1) * HD], sink=None)
            for t in range(T) for h in range(MLA_HEADS)]


def window_items(qk, v, band, sink, out):
    items = []
    for t in range(T):
        lo, hi = max(t - 1, 0), min(t + 1, T - 1)
        keys = (hi - lo + 1) * P
        at = (lo - t + 1) * P
        for h in range(SWA_HEADS):
            half = slice((h % 2) * HD, (h % 2 + 1) * HD)
            kv = h // (SWA_HEADS // 2)
            items.append(dict(
                scores=[(0, P, qk[half, 4 + h // 2, tile(t)], qk[half, 7 + kv, lo * P:(hi + 1) * P])], keys=keys,
                add=[(0, P, band[:, at:at + keys])],
                values=[(0, P, [v[:, c, kv * HD:(kv + 1) * HD] for c in range(lo, hi + 1)])],
                out=out[:, t, 640 + h * HD:640 + (h + 1) * HD], sink=sink[:, h:h + 1]))
    return items


def block_one(book, ps, A, ident, ones, stats, stop=None):
    nc = book.nc
    moff = [P * t * (t + 1) // 2 for t in range(T)]
    with ExitStack() as outer:
        sb = lambda ctx, name, shape: ctx.enter_context(nc.sbuf_tensor(name, shape, F32))
        rows = None
        with ExitStack() as mid:
            raw = sb(mid, "raw", [P, ROPE_CHUNKS, S])
            small = sb(mid, "small", [P, T, SMALL])
            heads_out = sb(mid, "heads_out", [P, T, D])
            ssd = heads_out[:, :, HALF:D]
            with ExitStack() as early:
                xbc = sb(early, "xbc", [P, XBC_CHUNKS, S + CONV - 1])
                z = heads_out[:, :, 0:HALF]
                project_one(book, ps, A, raw, xbc, z, small)
                if stop == "proj": return
                with ExitStack() as part:
                    turner = sb(part, "turner", [P, P])
                    cos = sb(part, "cos", [P, S])
                    sin = sb(part, "sin", [P, S])
                    load(book, [(turner[:, :], A["turner64"]), (cos[:, :], A["cos64"]), (sin[:, :], A["sin64"])])
                    rotate(book, ps, turner, cos, sin, raw, ROPE_CHUNKS)
                mixed = sb(early, "mixed", [P, XBC_CHUNKS, S])
                convolve(book, A, xbc, mixed)
                if stop == "conv": return
                state_space(book, ps, A, ident, ones, mixed, small, z, ssd)
                if stop == "ssd": return
            masks = sb(mid, "masks", [P, moff[T - 1] + S])
            index_keys(book, ps, A, raw, small, masks, moff)
            if stop == "index": return
            attend(book, ps, ident, sparse_items(raw, small, masks, moff, heads_out), HD ** -0.5, S)
            if stop == "dsa": return
            turned = sb(mid, "turned_mix", [P, KD, S])
            turn(book, ps, ident, heads_out, turned, D)
            rows = heads_out
            mix_out(book, ps, A, A["w_out"], turned, ALPHA, rows, A["x"])
            gain = sb(mid, "ln_gain", [P, D])
            shift = sb(mid, "ln_shift", [P, D])
            load(book, [(gain[:, :], A["ln1_g"].broadcast_to([P, D])), (shift[:, :], A["ln1_b"].broadcast_to([P, D]))])
            layer_norm(book, rows, gain, shift, stats, after=A["normed_rows"])
            turn(book, ps, ident, rows, turned, D)
            if stop == "ln1": return
            picked = sb(mid, "picked", [P, 2, T, EXPERTS])
            weights = sb(mid, "pick_weights", [P, 2, T])
            slots = mid.enter_context(nc.sbuf_tensor("slots", [P, 2, T], U32))
            block_tokens = mid.enter_context(nc.sbuf_tensor("block_tokens", [P, BLOCKS], U32))
            block_expert = mid.enter_context(nc.sbuf_tensor("block_expert", [P, BLOCKS], U32))
            route_one(book, ps, A, turned, picked, weights)
            place_tokens(book, ps, A, picked, ones, slots[:, :, :], block_tokens, block_expert)
            if stop == "route": return
            load(book, [(gain[:, :], A["ln2_g"].broadcast_to([P, D])), (shift[:, :], A["ln2_b"].broadcast_to([P, D]))])
            A["taken_one"] = mid.enter_context(nc.semaphore("taken_one"))
            A["came_in"] = [mid.enter_context(nc.semaphore(f"came_in{n}")) for n in range(4)]
            experts_one(book, ps, A, ident, block_tokens, block_expert)
            combine_one(book, A, slots, weights, rows)
            if stop == "moe": return
            layer_norm(book, rows, gain, shift, stats, after=A["residual_rows"])
            if stop == "ln2": return


def load(book, pairs):
    nc = book.nc
    with Stage(book, "loaded") as (block, loaded):
        @block.sync
        def _(sp):
            for to, what in pairs:
                sp.dma_start(to, what).then_inc(loaded, 16)
            sp.wait_ge(loaded, 16 * len(pairs))


def block_two(book, ps, A, ident, stats, stop=None):
    nc = book.nc
    sb = lambda ctx, name, shape, dt=F32: ctx.enter_context(nc.sbuf_tensor(name, shape, dt))
    with ExitStack() as ctx:
        taken_in = ctx.enter_context(nc.semaphore("taken_in"))
        summed = ctx.enter_context(nc.semaphore("summed"))
        with nc.Fori(0, LAYERS) as layer:
            layer_two(book, ps, A, layer, taken_in, summed, ident, stats, sb, stop)
            with Stage(book) as (block,):
                pass
    if stop: return
    finish_two(book, A, stats, sb)


def layer_two(book, ps, A, layer, taken_in, summed, ident, stats, sb, stop):
    nc = book.nc
    with ExitStack() as whole:
        mine = bass.ds(layer * P, P)
        mix = sb(whole, "mix", [P, T, D])
        with ExitStack() as attention:
            qk = sb(attention, "qk", [P, 10, S])
            feats = sb(attention, "feats", [P, T, 768])
            with ExitStack() as part:
                xnt = sb(part, "xnt", [P, KD, S])
                gain = sb(part, "gain_a", [P, KD])
                junk = sb(part, "junk_a", [P, 2, D])
                load(book, [(mix[:, :, :], A["residual_rows"]), (gain[:, :], A["attn_norm"][mine])])
                root_mean_squares(book, mix, [(0, D)], RMS_EPS, stats, junk)
                turn(book, ps, ident, mix, xnt, D, gain)
                project_two(book, ps, A, layer, xnt, qk, feats)
            if stop == "proj2": return
            with ExitStack() as part:
                turner = sb(part, "turner2", [P, P])
                cos = sb(part, "cos2", [P, S])
                sin = sb(part, "sin2", [P, S])
                turner96 = sb(part, "turner96", [P, P])
                cos96 = sb(part, "cos96", [P, S])
                sin96 = sb(part, "sin96", [P, S])
                load(book, [(turner[:, :], A["turner64"]), (cos[:, :], A["cos64"]), (sin[:, :], A["sin64"]),
                            (turner96[:, :], A["turner96"]), (cos96[:, :], A["cos96"]), (sin96[:, :], A["sin96"])])
                rotate(book, ps, turner, cos, sin, qk[:, 4:9, :], 5)
                rotate(book, ps, turner96, cos96, sin96, qk[:, 9:10, :], 1, MLA_D)
            if stop == "rope2": return
            with ExitStack() as part:
                shifted = sb(part, "v_shifted", [P, T - 1, 256])
                bias = sb(part, "na_bias", [P, NA_HEADS, (2 * NA_H - 1) * GRID_W])
                outside = sb(part, "outside", [P, (2 * NA_H - 1) * GRID_W])
                band = sb(part, "band", [P, 3 * P])
                sink = sb(part, "sink", [P, SWA_HEADS])
                v = feats[:, :, 0:256]
                with Stage(book, "loaded", "masked", "scaled") as (block, loaded, masked, scaled):
                    @block.sync
                    def _(sp):
                        sp.dma_start(bias[0:GRID_W, :, :], A["na_rpb"][bass.ds(layer * GRID_W, GRID_W)]).then_inc(loaded, 16)
                        sp.dma_start(bias[GRID_W:P, :, :], A["na_rpb"][bass.ds(layer * GRID_W, GRID_W)]).then_inc(loaded, 16)
                        sp.dma_start(outside[:, :], A["na_outside"]).then_inc(loaded, 16)
                        sp.dma_start(band[:, :], A["swa_band"]).then_inc(loaded, 16)
                        sp.dma_start(sink[:, :], A["swa_sink"][bass.ds(layer, 1)].broadcast_to([P, SWA_HEADS])).then_inc(loaded, 16)
                        sp.dma_start(shifted[0:GRID_W, :, :], v[GRID_W:P, 0:T - 1, :]).then_inc(loaded, 16)
                        sp.dma_start(shifted[GRID_W:P, :, :], v[0:GRID_W, 1:T, :]).then_inc(loaded, 16)
                        sp.wait_ge(loaded, 16 * 7)

                    @block.vector
                    def _(dve):
                        dve.wait_ge(loaded, 16 * 7)
                        for h in range(NA_HEADS):
                            nc.vector.scalar_tensor_tensor(out=bias[:, h, :], in0=bias[:, h, :], scalar=HD ** 0.5,
                                                           in1=outside[:, :], op0=ALU.mult, op1=ALU.add)
                attend(book, ps, ident, neighbourhood_items(qk, v, shifted, bias, mix), HD ** -0.5, 512)
                if stop == "na": return
                attend(book, ps, ident, window_items(qk, feats[:, :, 640:768], band, sink, mix), HD ** -0.5, 3 * P)
            if stop == "swa": return
            with ExitStack() as part:
                q = sb(part, "q_mla", [P, MLA_HEADS, S])
                k = qk[:, 0:MLA_HEADS, :]
                v_mla = sb(part, "v_mla", [P, T, MLA_HEADS * HD])
                with ExitStack() as inner:
                    latents = sb(inner, "latents", [P, 3, S])
                    gain = sb(inner, "gain_l", [P, 3])
                    junk = sb(inner, "junk_l", [P, 2, 256])
                    load(book, [(gain[:, :], A["latent_gain"][mine])])
                    lat = feats[:, :, 256:640]
                    root_mean_squares(book, lat, [(0, 256), (256, 384)], RMS_EPS, stats, junk)
                    turn(book, ps, ident, lat, latents, 384, gain)
                    expand_latents(book, ps, A, layer, latents, qk[:, 9, :], q, k, v_mla)
                    turner96 = sb(inner, "turner96b", [P, P])
                    cos96 = sb(inner, "cos96b", [P, S])
                    sin96 = sb(inner, "sin96b", [P, S])
                    load(book, [(turner96[:, :], A["turner96"]), (cos96[:, :], A["cos96"]), (sin96[:, :], A["sin96"])])
                    rotate(book, ps, turner96, cos96, sin96, q, MLA_HEADS, MLA_D)
                attend(book, ps, ident, latent_items(q, k, v_mla, mix), MLA_D ** -0.5, S)
            if stop == "mla": return
        with ExitStack() as part:
            turned = sb(part, "mix_turned", [P, KD, S])
            gain = sb(part, "gain_g", [P, KD])
            gain_f = sb(part, "gain_f", [P, KD])
            junk = sb(part, "junk_g", [P, 2, D])
            load(book, [(gain[:, :], A["group_norm"][mine]), (gain_f[:, :], A["ffn_norm"][mine])])
            root_mean_squares(book, mix, [(0, 256), (256, 640), (640, 1024)], RMS_EPS, stats, junk)
            turn(book, ps, ident, mix, turned, D, gain)
            mix_out(book, ps, A, A["w_out_2"][mine], turned, 1.0, mix, A["residual_rows"])
            if stop == "mix2": return
            with Stage(book, "stored") as (block, stored):
                @block.sync
                def _(sp):
                    sp.dma_start(A["residual_rows"], mix[:, :, :]).then_inc(stored, 16)
                    sp.wait_ge(stored, 16)
            root_mean_squares(book, mix, [(0, D)], RMS_EPS, stats, junk)
            with Stage(book, "stored") as (block, stored):
                @block.sync
                def _(sp):
                    sp.dma_start(A["normed_rows"], mix[:, :, :]).then_inc(stored, 16)
                    sp.wait_ge(stored, 16)
            turn(book, ps, ident, mix, turned, D, gain_f)
            gates = sb(part, "slot_gates", [P, EXPERTS])
            index = sb(part, "slot_index", [P, EXPERTS], U32)
            choose_tokens(book, ps, A, layer, ident, turned, gates, index)
            if stop == "choose": return
            experts_two(book, ps, A, layer, taken_in, summed, ident, gain_f, gates, index, A["normed"], A["residual"])


def finish_two(book, A, stats, sb):
    nc = book.nc
    with ExitStack() as ctx:
        rows = sb(ctx, "final_rows", [P, T, D])
        gain = sb(ctx, "final_gain", [P, D])
        junk = sb(ctx, "junk_f", [P, 2, D])
        load(book, [(rows[:, :, :], A["residual_rows"]), (gain[:, :], A["final_norm"].broadcast_to([P, D]))])
        root_mean_squares(book, rows, [(0, D)], RMS_EPS, stats, junk)
        with Stage(book, "scaled", "stored") as (block, scaled, stored):
            @block.vector
            def _(dve):
                for t in range(T):
                    nc.vector.tensor_tensor(rows[:, t, :], rows[:, t, :], gain[:, :], ALU.mult).then_inc(scaled, 1)

            @block.sync
            def _(sp):
                for t in range(T):
                    sp.wait_ge(scaled, t + 1)
                    sp.dma_start(A["out"][tile(t), :], rows[:, t, :]).then_inc(stored, 16)
                sp.wait_ge(stored, 16 * T)


def program(nc, A, stop=None, only_two=False):
    with ExitStack() as ctx:
        ps = ctx.enter_context(nc.psum_tensor("ps", [P, 8, BANK], F32))
        ident = ctx.enter_context(nc.sbuf_tensor("ident", [P, P], F32))
        ones = ctx.enter_context(nc.sbuf_tensor("ones", [P, P], F32))
        stats = ctx.enter_context(nc.sbuf_tensor("stats", [P, 2, 3 * T], F32))
        book = Book(nc)
        A["residual"] = nc.dram_tensor("residual", (S, D), F32).ap()
        A["normed"] = nc.dram_tensor("normed", (S, D), F32).ap()
        A["expert_out"] = nc.dram_tensor("expert_out", (BLOCKS * P, D), F32).ap()
        A["residual_rows"] = A["residual"].rearrange("(t p) d -> p t d", p=P)
        A["normed_rows"] = A["normed"].rearrange("(t p) d -> p t d", p=P)
        A["x"] = A["x"].rearrange("(t p) d -> p t d", p=P)
        load(book, [(ident[:, :], A["ident"]), (ones[:, :], A["ones"])])
        if only_two:
            with ExitStack() as c2:
                r = c2.enter_context(nc.sbuf_tensor("rr", [P, T, D], F32))
                load(book, [(r[:, :, :], A["x"])])
                load(book, [(A["residual_rows"], r[:, :, :])])
        else:
            block_one(book, ps, A, ident, ones, stats, stop)
        if stop is None or stop.endswith("2") and stop != "ln2" or stop in ("na", "swa", "mla", "choose", "layer"):
            block_two(book, ps, A, ident, stats, stop)




def constants():
    f = np.float32
    out = {"ident": np.eye(P, dtype=f), "ones": np.ones((P, P), f)}
    out["upto"] = np.triu(np.ones((P, P), f))
    hidden = np.where(np.arange(P)[:, None] <= np.arange(P)[None, :], f(0), f(HIDE)).astype(f)
    out["hidden"] = np.ascontiguousarray(np.broadcast_to(hidden[:, None, :], (P, 4, P)))
    out["count"] = np.ascontiguousarray(np.broadcast_to(np.arange(P, dtype=f), (P, P)))
    out["eights"] = np.ascontiguousarray(np.broadcast_to(np.arange(8, dtype=f) * P, (P, 8)))
    out["token"] = np.arange(S, dtype=f).reshape(T, P).T
    out["causal"] = np.ascontiguousarray(hidden.T)

    def rope(dim, before, after):
        inv = (f(10000.0) ** (-np.arange(0, dim, 2, dtype=f) / f(dim))).astype(f)
        ang = np.arange(S, dtype=f)[:, None] * inv[None, :]
        c, s = np.cos(ang).astype(f).T, np.sin(ang).astype(f).T
        cos = np.concatenate([np.ones((before, S), f), c, c, np.ones((after, S), f)])
        sin = np.concatenate([np.zeros((before, S), f), s, s, np.zeros((after, S), f)])
        turner = np.zeros((before + dim + after,) * 2, f)
        for i in range(dim // 2):
            turner[before + dim // 2 + i, before + i] = -1
            turner[before + i, before + dim // 2 + i] = 1
        return cos, sin, turner

    cos, sin, turner = rope(HD, 0, 0)
    out["cos64"], out["sin64"] = np.concatenate([cos, cos]), np.concatenate([sin, sin])
    out["turner64"] = np.kron(np.eye(2, dtype=f), turner)
    out["cos96"], out["sin96"], out["turner96"] = rope(32, HD, 32)
    c = np.arange(GRID_W)
    first = np.clip(c - NA_W // 2, 0, GRID_W - NA_W)
    inside = (c[None, :] >= first[:, None]) & (c[None, :] < first[:, None] + NA_W)
    outside = np.where(inside, f(0), f(HIDE)).astype(f)
    out["na_outside"] = np.tile(outside, (2, 2 * NA_H - 1))
    q, k = np.arange(P)[:, None], np.arange(3 * P)[None, :] - P
    out["swa_band"] = np.where(np.abs(q - k) <= 128, f(0), f(HIDE)).astype(f)
    return {n: np.ascontiguousarray(a) for n, a in out.items()}


def turned_weights(w, columns):
    k = w.shape[0] // P
    out = np.zeros((P, len(columns), k, P), w.dtype)
    for m, cols in enumerate(columns):
        cols = np.asarray(cols)
        there = cols >= 0
        out[:, m][:, :, there] = w[:, cols[there]].reshape(k, P, -1).transpose(1, 0, 2)
    return out


def row_weights(w):
    return np.ascontiguousarray(w.reshape(w.shape[0] // P, P, -1).transpose(1, 0, 2))


def columns_of(a):
    return np.ascontiguousarray(a.reshape(-1, P).T)


def arrays_of(i):
    r = np.arange
    A = constants()
    x = i["x"][0]
    A["x"], A["xt"] = x, np.ascontiguousarray(x.T)
    w = i["w_in"][0]
    k, ik = r(512, 576), r(896, 960)
    cols = [r(128 * m, 128 * m + 128) for m in range(4)] + [r(640, 768), r(768, 896)]
    cols += [np.concatenate([k, k]), np.concatenate([ik, ik])]
    cols += [r(1476 + 128 * m, 1476 + 128 * m + 128) for m in range(6)]
    A["w_turned"] = turned_weights(w, cols)
    A["w_rows"] = row_weights(w[:, np.concatenate([r(964, 1476), r(576, 640), r(960, 964), r(2244, 2252)])])
    A["conv_w"] = np.ascontiguousarray(i["conv_w"][0].T.reshape(6, P, CONV).transpose(1, 0, 2))
    A["conv_b"] = columns_of(i["conv_b"][0])
    for n in ("dt_bias", "a_log", "d_skip", "ssd_norm_w", "ln1_g", "ln1_b", "ln2_g", "ln2_b"):
        A[n] = i[n]
    A["w_out"] = row_weights(i["w_out"][0])
    A["w_route"] = row_weights(np.concatenate([i["w_route_group"][0], i["w_route_expert"][0]], 1))
    A["b_route"] = np.concatenate([i["b_route_group"], i["b_route_expert"]], 1)
    A["w_gate_up"] = np.concatenate([i["w_gate"][0], i["w_up"][0]], -1)
    A["w_down"] = i["w_down"][0]
    for n in ("w_gate", "w_up", "w_down"):
        A[n + "_2"] = i[n + "_2"].reshape(LAYERS * EXPERTS, D, D)
    cols = [r(128 * m, 128 * m + 128) for m in range(4)] + [r(1184 + 128 * m, 1312 + 128 * m) for m in range(3)]
    cols += [np.concatenate([r(1568 + 64 * g, 1632 + 64 * g)] * 2) for g in range(2)]
    cols += [np.concatenate([np.full(64, -1), r(1152, 1184), np.full(32, -1)])]
    rows = np.concatenate([r(512, 768), r(768, 1024), r(1024, 1152), r(1696, 1824)])
    w = i["w_in_2"]
    cat = lambda f: np.concatenate([f(l) for l in range(LAYERS)])
    A["w_turned_2"] = cat(lambda l: turned_weights(w[l], cols))
    A["w_rows_2"] = cat(lambda l: row_weights(w[l][:, rows]))
    A["attn_norm"] = cat(lambda l: columns_of(i["attn_norm_2"][l]))
    A["group_norm"] = cat(lambda l: columns_of(i["group_norm_2"][l]))
    A["ffn_norm"] = cat(lambda l: columns_of(i["ffn_norm_2"][l]))
    A["latent_gain"] = cat(lambda l: columns_of(np.concatenate([i["mla_q_norm_2"][l], i["mla_kv_norm_2"][l]])))
    A["mla_w_uq"] = cat(lambda l: row_weights(i["mla_w_uq_2"][l]))
    kv = np.concatenate([np.concatenate([r(128 * h + s, 128 * h + s + 64) for h in range(MLA_HEADS)]) for s in (0, 64)])
    A["mla_w_ukv"] = cat(lambda l: np.ascontiguousarray(i["mla_w_ukv_2"][l][:, kv]))
    A["swa_sink"] = i["swa_sink_2"]
    A["w_out_2"] = cat(lambda l: row_weights(i["w_out_2"][l]))
    A["w_router"] = cat(lambda l: row_weights(i["w_router_2"][l]))
    A["final_norm"] = i["final_norm_2"].reshape(1, D)
    dc = np.clip(r(GRID_W)[None, :] - r(GRID_W)[:, None] + NA_W - 1, 0, 2 * NA_W - 2)
    A["na_rpb"] = cat(lambda l: i["na_rpb_2"][l][:, :, dc].transpose(2, 0, 1, 3).reshape(GRID_W, NA_HEADS, -1))
    return {n: np.ascontiguousarray(a) for n, a in A.items()}


def kernel(**inputs):
    import concourse.bacc as bacc
    from concourse.bass_utils import run_bass_kernel_spmd as run

    nc = bacc.Bacc("TRN2", target_bir_lowering=False, num_devices=1)
    arrays = arrays_of({n: np.asarray(a) for n, a in inputs.items()})
    A = {n: nc.dram_tensor("in_" + n, a.shape, mybir.dt.from_np(a.dtype), kind="ExternalInput").ap()
         for n, a in arrays.items()}
    A["out"] = nc.dram_tensor("out_0", (S, D), F32, kind="ExternalOutput").ap()
    program(nc, A)
    r = run(nc, [{"in_" + n: a for n, a in arrays.items()}], core_ids=[0])
    return r.results[0]["out_0"].reshape(1, S, D)
```

```python
from contextlib import ExitStack

import numpy as np

import concourse.bass as bass
from concourse import mybir

F32 = mybir.dt.float32
F32R = mybir.dt.float32r
U32 = mybir.dt.uint32
ALU = mybir.AluOpType
ACT = mybir.ActivationFunctionType
AX = mybir.AxisListType

P = 128
S = 1024
D = 1024
T = S // P
KD = D // P
HALF = 512
BANK = 512

HEADS = 8
HD = 64
IDX_HEADS = 4
INDEXER_SCALE = (IDX_HEADS ** -0.5) * (HD ** -0.5)
TOPK = 256
SSD_HEADS = 8
STATE = 64
CONV = 4
EXPERTS = 16
FF = 256
ALPHA = 2.0 ** 0.25
LN_EPS = 1e-5
ROWS_Z = 512
V0, IW0, DT0 = 0, 64, 68
SMALL = 76
ROPE_CHUNKS = 8
XBC_CHUNKS = 6

LAYERS = 2
RMS_EPS = 1e-6
GRID_W = 64
GRID_H = S // GRID_W
NA_HEADS = 4
NA_H = 8
NA_W = 16
MLA_HEADS = 6
INDEX_CHUNKS = (4, 5, 7)
OTHER_CHUNKS = (0, 1, 2, 3, 6)
MLA_D = 96
SWA_HEADS = 6
CAP = 128
HIDE = -1e30
TAKEN = -3e38
BLOCKS = (2 * S - EXPERTS) // P + EXPERTS


class Book:

    def __init__(self, nc):
        self.nc = nc
        self.before = None
        self.count = 0


class Stage:

    def __init__(self, book, *names):
        self.book = book
        self.names = names

    def __enter__(self):
        book = self.book
        nc = book.nc
        book.count += 1
        self.own = ExitStack()
        self.sems = [self.own.enter_context(nc.semaphore(f"{n}_{book.count}")) for n in self.names]
        self.opened = ExitStack()
        block = self.opened.enter_context(nc.Block(no_gpsimd_drain=False))
        old = book.before.sems if book.before else []

        @block.sync
        def _(sp):
            for s in old:
                sp.sem_clear(s)

        return (block, *self.sems)

    def __exit__(self, kind, value, trace):
        if kind is not None:
            return False
        self.opened.close()
        if self.book.before:
            self.book.before.own.close()
        self.book.before = self
        return False


class Chain:

    def __init__(self, eng, sem):
        self.eng, self.sem, self.n = eng, sem, 0

    def step(self, ins):
        ins.then_inc(self.sem, 1)
        self.n += 1
        self.eng.wait_ge(self.sem, self.n)


def tile(t, size=P):
    return slice(t * size, (t + 1) * size)


def spread(ap, shape):
    return ap.unsqueeze(len(shape) - 1).broadcast_to(shape)




def turn(book, ps, ident, rows, turned, width, gain=None):
    nc = book.nc
    chunks = width // P
    groups = [(c, h) for c in range(chunks) for h in range(2)]
    with Stage(book, "turned_full", "read_by_act", "read_by_dve") as (block, full, by_act, by_dve):

        @block.tensor
        def _(pe):
            for g, (c, h) in enumerate(groups):
                if g >= 8:
                    if g % 2:
                        pe.wait_ge(by_dve, g // 2 - 3)
                    else:
                        pe.wait_ge(by_act, g // 2 - 3)
                for j in range(4):
                    t = 4 * h + j
                    last = nc.tensor.transpose(ps[:, g % 8, tile(j)], rows[:, t, tile(c)], ident[:, :])
                last.then_inc(full, 1)

        @block.scalar
        def _(act):
            for g, (c, h) in enumerate(groups):
                if g % 2 == 0:
                    act.wait_ge(full, g + 1)
                    out = turned[:, c, tile(h, HALF)]
                    if gain is None:
                        nc.scalar.activation(out, ps[:, g % 8, :], ACT.Copy).then_inc(by_act, 1)
                    else:
                        nc.scalar.activation(out, ps[:, g % 8, :], ACT.Copy, scale=gain[:, c:c + 1]).then_inc(by_act, 1)

        @block.vector
        def _(dve):
            for g, (c, h) in enumerate(groups):
                if g % 2 == 1:
                    dve.wait_ge(full, g + 1)
                    out = turned[:, c, tile(h, HALF)]
                    if gain is None:
                        nc.vector.tensor_copy(out, ps[:, g % 8, :]).then_inc(by_dve, 1)
                    else:
                        nc.vector.tensor_scalar(out, ps[:, g % 8, :], gain[:, c:c + 1], None, ALU.mult).then_inc(by_dve, 1)


def root_mean_squares(book, rows, segments, eps, stats, junk, out=None):
    nc = book.nc
    n = len(segments)
    if out is None:
        out = rows
    ss = stats[:, 0, 0:T * n].rearrange("p (t n) -> p t n", n=n)
    root = stats[:, 1, 0:T * n].rearrange("p (t n) -> p t n", n=n)
    with Stage(book, "squares", "means", "roots", "dve_steps") as (block, squares, means, roots, steps):

        @block.scalar
        def _(act):
            for t in range(T):
                for j, (a, b) in enumerate(segments):
                    if t * n + j >= 2:
                        act.wait_ge(squares, t * n + j - 1)
                    nc.scalar.activation(junk[:, (t * n + j) % 2, 0:b - a], rows[:, t, a:b], ACT.Square,
                                         accum_out=ss[:, t, j:j + 1]).then_inc(squares, 1)
            act.wait_ge(means, 1)
            act.wait_ge(squares, T * n)
            nc.scalar.activation(root, ss, ACT.Sqrt).then_inc(roots, 1)

        @block.vector
        def _(dve):
            chain = Chain(dve, steps)
            dve.wait_ge(squares, T * n)
            for j, (a, b) in enumerate(segments):
                ins = nc.vector.tensor_scalar(ss[:, :, j], ss[:, :, j], 1.0 / (b - a), eps, ALU.mult, ALU.add)
                if j == n - 1:
                    ins.then_inc(means, 1)
                else:
                    chain.step(ins)
            dve.wait_ge(roots, 1)
            chain.step(nc.vector.reciprocal(root, root))
            for t in range(T):
                for j, (a, b) in enumerate(segments):
                    nc.vector.tensor_scalar(out[:, t, a:b], rows[:, t, a:b], root[:, t, j:j + 1], None, ALU.mult)


def layer_norm(book, rows, gain, shift, stats, after=None):
    nc = book.nc
    with ExitStack() as ctx, Stage(book, "moments", "roots", "dve_steps", "scaled", "stored") as (
            block, moments, roots, steps, scaled, stored):
        bn = ctx.enter_context(nc.sbuf_tensor(f"bn{book.count}", [P, T, 2, 6], F32))
        mv = ctx.enter_context(nc.sbuf_tensor(f"mv{book.count}", [P, T, 2], F32))
        var, root = stats[:, 0, 0:T], stats[:, 1, 0:T]

        @block.vector
        def _(dve):
            chain = Chain(dve, steps)
            for t in range(T):
                for h in range(2):
                    ins = nc.vector.bn_stats(bn[:, t, h, :], rows[:, t, tile(h, HALF)])
            chain.step(ins)
            for t in range(T):
                ins = nc.vector.bn_aggr(mv[:, t, :], bn[:, t, :, :])
            chain.step(ins)
            nc.vector.tensor_scalar(var, mv[:, :, 1], LN_EPS, None, ALU.add).then_inc(moments, 1)
            dve.wait_ge(roots, 1)
            chain.step(nc.vector.reciprocal(root, root))
            for t in range(T):
                chain.step(nc.vector.tensor_scalar(rows[:, t, :], rows[:, t, :], mv[:, t, 0:1], root[:, t:t + 1],
                                                   ALU.subtract, ALU.mult))
                chain.step(nc.vector.tensor_tensor(rows[:, t, :], rows[:, t, :], gain[:, :], ALU.mult))
                nc.vector.tensor_tensor(rows[:, t, :], rows[:, t, :], shift[:, :], ALU.add).then_inc(scaled, 1)

        @block.scalar
        def _(act):
            act.wait_ge(moments, 1)
            nc.scalar.activation(root, var, ACT.Sqrt).then_inc(roots, 1)

        if after is not None:
            @block.sync
            def _(sp):
                sp.wait_ge(scaled, T)
                sp.dma_start(after, rows[:, :, :]).then_inc(stored, 16)
                sp.wait_ge(stored, 16)


def turn_split(book, ps, ident, rows, high, low, width, gain=None):
    nc = book.nc
    groups = [(c, h) for c in range(width // P) for h in range(2)]
    with Stage(book, "turned_full", "high_ready", "low_ready") as (block, full, high_ready, low_ready):

        @block.tensor
        def _(pe):
            for g, (c, h) in enumerate(groups):
                if g >= 8:
                    pe.wait_ge(low_ready, g - 7)
                for j in range(4):
                    last = nc.tensor.transpose(ps[:, g % 8, tile(j)], rows[:, 4 * h + j, tile(c)], ident[:, :])
                last.then_inc(full, 1)

        @block.scalar
        def _(act):
            for g, (c, h) in enumerate(groups):
                act.wait_ge(full, g + 1)
                out = high[:, c, tile(h, HALF)]
                if gain is None:
                    nc.scalar.activation(out, ps[:, g % 8, :], ACT.Copy).then_inc(high_ready, 1)
                else:
                    nc.scalar.activation(out, ps[:, g % 8, :], ACT.Copy, scale=gain[:, c:c + 1]).then_inc(high_ready, 1)

        @block.vector
        def _(dve):
            for g, (c, h) in enumerate(groups):
                dve.wait_ge(high_ready, g + 1)
                out = low[:, c, tile(h, HALF)]
                top = high[:, c, tile(h, HALF)].bitcast(F32)
                if gain is None:
                    nc.vector.tensor_tensor(out, ps[:, g % 8, :], top, ALU.subtract).then_inc(low_ready, 1)
                else:
                    nc.vector.scalar_tensor_tensor(out=out, in0=ps[:, g % 8, :], scalar=gain[:, c:c + 1], in1=top,
                                                   op0=ALU.mult, op1=ALU.subtract).then_inc(low_ready, 1)


def split_products(nc, out, pairs):
    terms = [t for lh, ll, rh, rl in pairs for t in ((lh, rh), (lh, rl), (ll, rh))]
    for n, (left, right) in enumerate(terms):
        last = nc.tensor.matmul(out, left, right, start=(n == 0), stop=(n == len(terms) - 1))
    return last


def rotate(book, ps, turner, cos, sin, raw, chunks, parts=P):
    nc = book.nc
    order, chunks = chunks, len(chunks)
    with ExitStack() as ctx, Stage(book, "turned_full", "cos_done", "sin_done", "rotated") as (
            block, full, cos_done, sin_done, rotated):
        by_cos = ctx.enter_context(nc.sbuf_tensor(f"by_cos{book.count}", [P, 2, S], F32))
        by_sin = ctx.enter_context(nc.sbuf_tensor(f"by_sin{book.count}", [P, 2, S], F32))

        @block.tensor
        def _(pe):
            for n in range(chunks):
                if n >= 4:
                    pe.wait_ge(sin_done, n - 3)
                for h in range(2):
                    last = nc.tensor.matmul(ps[0:parts, 2 * (n % 4) + h, :], turner[0:parts, 0:parts],
                                            raw[0:parts, order[n], tile(h, HALF)], start=True, stop=True)
                last.then_inc(full, 1)

        @block.gpsimd
        def _(pool):
            for n in range(chunks):
                if n >= 2:
                    pool.wait_ge(rotated, n - 1)
                nc.gpsimd.tensor_tensor(by_cos[0:parts, n % 2, :], raw[0:parts, order[n], :], cos[0:parts, :],
                                        ALU.mult).then_inc(cos_done, 1)

        @block.vector
        def _(dve):
            for n in range(chunks):
                dve.wait_ge(full, n + 1)
                if n >= 2:
                    dve.wait_ge(rotated, n - 1)
                nc.vector.tensor_tensor(by_sin[0:parts, n % 2, :],
                                        ps[0:parts, 2 * (n % 4):2 * (n % 4) + 2, :].rearrange("p a b -> p (a b)"),
                                        sin[0:parts, :], ALU.mult).then_inc(sin_done, 1)
                dve.wait_ge(cos_done, n + 1)
                dve.wait_ge(sin_done, n + 1)
                nc.vector.tensor_tensor(raw[0:parts, order[n], :], by_cos[0:parts, n % 2, :], by_sin[0:parts, n % 2, :],
                                        ALU.add).then_inc(rotated, 1)


def attend(book, ps, ident, items, scale, widest):
    nc = book.nc
    N = len(items)
    groups = [(n, j) for n, item in enumerate(items) for j in range((item["keys"] // P + 3) // 4)]
    count = [len([1 for m, _ in groups if m == n]) for n in range(N)]
    first = [sum(count[:n]) for n in range(N)]
    by_act = [items[n]["add"] is not None or g % 2 == 0 for g, (n, _) in enumerate(groups)]

    def copied(eng, act_copied, dve_copied, g):
        if by_act[g]:
            eng.wait_ge(act_copied, sum(by_act[:g + 1]))
        else:
            eng.wait_ge(dve_copied, g + 1 - sum(by_act[:g + 1]))

    with ExitStack() as ctx, Stage(
            book, "scores_full", "logits_ready", "probs_ready", "turned_full", "act_copied", "dve_copied",
            "values_used", "dve_steps", "sink_done", "written") as (
            block, scores_full, logits_ready, probs_ready, turned_full, act_copied, dve_copied,
            values_used, steps, sink_done, written):
        sb = lambda name, shape: ctx.enter_context(nc.sbuf_tensor(f"{name}{book.count}", shape, F32))
        logits = sb("logits", [P, 2, widest])
        probs = sb("probs", [P, 2, widest])
        turned = sb("turned", [P, 4, BANK])
        top = sb("top", [P, 4])
        less = sb("less", [P, 4])
        total = sb("total", [P, 4])
        sunk = sb("sunk", [P, 4])
        over = sb("over", [P, 4])

        def raw(n, a=0, b=P):
            flat = ps[:, 2 * (n % 2):2 * (n % 2) + 2, :].rearrange("p a b -> p (a b)")
            return flat[a:b, 0:items[n]["keys"]]

        @block.tensor
        def _(pe):
            def score(n):
                item = items[n]
                if n >= 2:
                    pe.wait_ge(probs_ready, n - 1)
                for a, b, q, k in item["scores"]:
                    for h in range((item["keys"] + BANK - 1) // BANK):
                        lo, hi = h * BANK, min((h + 1) * BANK, item["keys"])
                        last = nc.tensor.matmul(ps[a:b, 2 * (n % 2) + h, 0:hi - lo], q, k[:, lo:hi],
                                                start=True, stop=True)
                last.then_inc(scores_full, 1)

            score(0)
            score(1)
            for n, item in enumerate(items):
                pe.wait_ge(probs_ready, n + 1)
                chunks = item["keys"] // P
                for j in range(count[n]):
                    g = first[n] + j
                    if g >= 2:
                        copied(pe, act_copied, dve_copied, g - 2)
                    for i in range(min(4, chunks - 4 * j)):
                        last = nc.tensor.transpose(ps[:, 4 + g % 2, tile(i)], probs[:, n % 2, tile(4 * j + i)],
                                                   ident[:, :])
                    last.then_inc(turned_full, 1)
                if n + 2 < N:
                    score(n + 2)
                if n >= 2:
                    pe.wait_ge(written, n - 1)
                for j in range(count[n]):
                    g = first[n] + j
                    copied(pe, act_copied, dve_copied, g)
                    for i in range(min(4, chunks - 4 * j)):
                        c = 4 * j + i
                        for a, b, values in item["values"]:
                            last = nc.tensor.matmul(ps[a:b, 6 + n % 2, 0:HD], turned[:, g % 4, i * P + a:i * P + b],
                                                    values[c], start=(c == 0), stop=(c == chunks - 1))
                    last.then_inc(values_used, 1)

        @block.scalar
        def _(act):
            def exponentials(n):
                item = items[n]
                s4 = slice(n % 4, n % 4 + 1)
                act.wait_ge(logits_ready, n + 1)
                if n >= 2:
                    act.wait_ge(turned_full, first[n - 1])
                if n >= 4:
                    act.wait_ge(written, n - 3)
                source = logits[:, n % 2, 0:item["keys"]] if item["add"] else raw(n)
                nc.scalar.activation(probs[:, n % 2, 0:item["keys"]], source, ACT.Exp, scale=scale,
                                     bias=less[:, s4], accum_out=total[:, s4]).then_inc(probs_ready, 1)
                if item["sink"] is not None:
                    nc.scalar.activation(sunk[:, s4], item["sink"], ACT.Exp, bias=less[:, s4]).then_inc(sink_done, 1)

            exponentials(0)
            exponentials(1)
            for n, item in enumerate(items):
                for j in range(count[n]):
                    g = first[n] + j
                    if by_act[g]:
                        act.wait_ge(turned_full, g + 1)
                        if g >= 4:
                            act.wait_ge(values_used, g - 3)
                        w = min(4, item["keys"] // P - 4 * j) * P
                        nc.scalar.activation(turned[:, g % 4, 0:w], ps[:, 4 + g % 2, 0:w],
                                             ACT.Copy).then_inc(act_copied, 1)
                if n + 2 < N:
                    exponentials(n + 2)

        @block.vector
        def _(dve):
            chain = Chain(dve, steps)

            def maxima(n):
                item = items[n]
                dve.wait_ge(scores_full, n + 1)
                if n >= 2:
                    dve.wait_ge(probs_ready, n - 1)
                if item["sink"] is not None and n >= 4:
                    dve.wait_ge(sink_done, n - 3)
                m = top[:, n % 4:n % 4 + 1]
                if item["add"]:
                    for a, b, add in item["add"]:
                        ins = nc.vector.tensor_tensor_reduce(
                            logits[a:b, n % 2, 0:item["keys"]], raw(n, a, b), add, 1.0, -3e38, ALU.add, ALU.max,
                            m[a:b, :])
                        if b < P:
                            ins.then_inc(steps, 1)
                            chain.n += 1
                    chain.step(ins)
                else:
                    chain.step(nc.vector.tensor_reduce(m, raw(n), AX.X, ALU.max))
                if item["sink"] is not None:
                    chain.step(nc.vector.tensor_scalar(m, m, scale, item["sink"], ALU.mult, ALU.max))
                nc.vector.tensor_scalar(less[:, n % 4:n % 4 + 1], m, -1.0 if item["sink"] is not None else -scale,
                                        None, ALU.mult).then_inc(logits_ready, 1)

            def write(n):
                item = items[n]
                dve.wait_ge(probs_ready, n + 1)
                s4 = slice(n % 4, n % 4 + 1)
                if item["sink"] is not None:
                    dve.wait_ge(sink_done, n + 1)
                    chain.step(nc.vector.tensor_tensor(total[:, s4], total[:, s4], sunk[:, s4], ALU.add))
                chain.step(nc.vector.reciprocal(over[:, s4], total[:, s4]))
                dve.wait_ge(values_used, first[n] + count[n])
                nc.vector.tensor_scalar(item["out"], ps[:, 6 + n % 2, 0:HD], over[:, s4], None,
                                        ALU.mult).then_inc(written, 1)

            maxima(0)
            maxima(1)
            for n, item in enumerate(items):
                for j in range(count[n]):
                    g = first[n] + j
                    if not by_act[g]:
                        dve.wait_ge(turned_full, g + 1)
                        if g >= 4:
                            dve.wait_ge(values_used, g - 3)
                        w = min(4, item["keys"] // P - 4 * j) * P
                        nc.vector.tensor_copy(turned[:, g % 4, 0:w], ps[:, 4 + g % 2, 0:w]).then_inc(dve_copied, 1)
                if n + 2 < N:
                    maxima(n + 2)
                write(n)




def project_index(book, ps, A, xt, raw, small):
    nc = book.nc
    with ExitStack() as ctx, Stage(book, "x_in0", "x_in1", "w_in", "w_rows_in", "full", "read") as (
            block, x_in0, x_in1, w_in, w_rows_in, full, read):
        x_in = [x_in0, x_in1]
        wt = ctx.enter_context(nc.sbuf_tensor("wt_index", [P, len(INDEX_CHUNKS), KD, P], F32))
        wr = ctx.enter_context(nc.sbuf_tensor("wr_small", [P, KD, SMALL], F32))

        @block.sync
        def _(sp):
            sp.dma_start(wt[:, :, :, :], A["w_turned_index"]).then_inc(w_in, 16)
            for h in range(2):
                sp.dma_start(xt[:, :, tile(h, HALF)],
                             A["xt"].rearrange("(k p) s -> p k s", p=P)[:, :, tile(h, HALF)]).then_inc(x_in[h], 16)
            sp.dma_start(wr[:, :, :], A["w_rows_small"]).then_inc(w_rows_in, 16)

        @block.tensor
        def _(pe):
            g = 0
            pe.wait_ge(w_in, 16)
            for h in range(2):
                pe.wait_ge(x_in[h], 16)
                for m in range(len(INDEX_CHUNKS)):
                    for k in range(KD):
                        last = nc.tensor.matmul(ps[:, g, :], wt[:, m, k, :], xt[:, k, tile(h, HALF)],
                                                start=(k == 0), stop=(k == KD - 1))
                    last.then_inc(full, 1)
                    g += 1
            pe.wait_ge(w_rows_in, 16)
            for t in range(T):
                if g >= 8:
                    pe.wait_ge(read, g - 7)
                for k in range(KD):
                    last = nc.tensor.matmul(ps[:, g % 8, 0:SMALL], xt[:, k, tile(t)], wr[:, k, :],
                                            start=(k == 0), stop=(k == KD - 1))
                last.then_inc(full, 1)
                g += 1

        @block.scalar
        def _(act):
            g = 0
            for h in range(2):
                for chunk in INDEX_CHUNKS:
                    act.wait_ge(full, g + 1)
                    nc.scalar.activation(raw[:, chunk, tile(h, HALF)], ps[:, g, :], ACT.Copy).then_inc(read, 1)
                    g += 1
            for t in range(T):
                act.wait_ge(full, g + 1)
                nc.scalar.activation(small[:, t, :], ps[:, g % 8, 0:SMALL], ACT.Copy).then_inc(read, 1)
                g += 1


def choose_keys(book, ps, A, xt, raw, small, xbc, z, masks, moff):
    nc = book.nc
    rounds = TOPK // 8
    chunks = [raw[:, c, :] for c in OTHER_CHUNKS] + [xbc[:, c, CONV - 1:] for c in range(XBC_CHUNKS)]
    M = len(chunks)
    pieces = [(0, 3), (3, 7), (7, M)]
    piece_of = [n for n, (a, b) in enumerate(pieces) for _ in range(a, b)]
    groups = [(m, h) for m in range(M) for h in range(2)] + [(None, t) for t in range(T)]
    before = {2: 0, 3: 0}
    for t in range(4, T):
        before[t] = len(groups) * sum(range(3, t)) // sum(range(3, T + 1))
    order = []
    done = 0
    for t in range(2, T):
        while done < before[t]:
            order.append(("project", done))
            done += 1
        order.append(("scores", t))
    order += [("project", g) for g in range(done, len(groups))]
    with ExitStack() as ctx, Stage(book, "causal_in", "w_in0", "w_in1", "w_in2", "w_z_in", "edge_zero", "projected",
                                   "kept", "full", "positive", "scored", "dve_steps") as (
            block, causal_in, w_in0, w_in1, w_in2, w_z_in, edge_zero, projected, kept, full, positive, scored, steps):
        w_in = [w_in0, w_in1, w_in2]
        sb = lambda name, shape: ctx.enter_context(nc.sbuf_tensor(name, shape, F32))
        wt = sb("wt", [P, M, KD, P])
        wz = wt[:, 0:4, :, :].rearrange("p m k c -> p (m k c)").rearrange("p (k w) -> p k w", w=ROWS_Z)
        causal = sb("causal", [P, P])
        iw = sb("iw", [P, T, IDX_HEADS])
        relu = sb("relu", [P, 4, S])
        score = sb("score", [P, S])
        best = sb("best", [P, 8])

        @block.sync
        def _(sp):
            sp.dma_start(causal[:, :], A["causal"]).then_inc(causal_in, 16)
            for n, (a, b) in enumerate(pieces):
                sp.dma_start(wt[:, a:b], A["w_turned"][:, a:b]).then_inc(w_in[n], 16)
            sp.wait_ge(projected, 8)
            sp.dma_start(wz, A["w_rows_z"]).then_inc(w_z_in, 16)

        @block.gpsimd
        def _(pool):
            nc.gpsimd.memset(xbc[:, :, 0:CONV - 1], 0.0).then_inc(edge_zero, 1)

        @block.tensor
        def _(pe):
            n = 0
            for what, i in order:
                if what == "project":
                    m, part = groups[i]
                    if i >= 4:
                        pe.wait_ge(kept, i - 3)
                    if m is None:
                        pe.wait_ge(w_z_in, 16)
                    else:
                        pe.wait_ge(w_in[piece_of[m]], 16)
                    for k in range(KD):
                        if m is None:
                            lhs, rhs = xt[:, k, tile(part)], wz[:, k, :]
                        else:
                            lhs, rhs = wt[:, m, k, :], xt[:, k, tile(part, HALF)]
                        last = nc.tensor.matmul(ps[:, 4 + i % 4, :], lhs, rhs, start=(k == 0), stop=(k == KD - 1))
                    last.then_inc(projected, 1)
                    continue
                keys = (i + 1) * P
                for h in range(IDX_HEADS):
                    half = slice((h % 2) * HD, (h % 2 + 1) * HD)
                    if n >= 2:
                        pe.wait_ge(positive, n - 1)
                    for b in range((keys + BANK - 1) // BANK):
                        lo, hi = b * BANK, min((b + 1) * BANK, keys)
                        last = nc.tensor.matmul(ps[:, 2 * (n % 2) + b, 0:hi - lo], raw[half, 4 + h // 2, tile(i)],
                                                raw[half, 7, lo:hi], start=True, stop=True)
                    last.then_inc(full, 1)
                    n += 1

        @block.scalar
        def _(act):
            n = 0
            for what, i in order:
                if what == "project":
                    m, part = groups[i]
                    act.wait_ge(projected, i + 1)
                    out = z[:, part, :] if m is None else chunks[m][:, tile(part, HALF)]
                    nc.scalar.activation(out, ps[:, 4 + i % 4, :], ACT.Copy).then_inc(kept, 1)
                    continue
                keys = (i + 1) * P
                for h in range(IDX_HEADS):
                    act.wait_ge(full, n + 1)
                    if n >= 4:
                        act.wait_ge(scored, n - 3)
                    flat = ps[:, 2 * (n % 2):2 * (n % 2) + 2, :].rearrange("p a b -> p (a b)")
                    nc.scalar.activation(relu[:, n % 4, 0:keys], flat[:, 0:keys], ACT.Relu).then_inc(positive, 1)
                    n += 1

        @block.vector
        def _(dve):
            chain = Chain(dve, steps)
            chain.step(nc.vector.tensor_scalar(iw[:, :, :], small[:, :, IW0:IW0 + IDX_HEADS], INDEXER_SCALE, None,
                                               ALU.mult))
            dve.wait_ge(causal_in, 16)
            n = 0
            for t in range(T):
                keys = (t + 1) * P
                mask = masks[:, moff[t]:moff[t] + keys]
                if t < 2:
                    if t:
                        nc.vector.memset(mask[:, 0:t * P], 0.0)
                    nc.vector.tensor_copy(mask[:, t * P:keys], causal[:, :])
                    continue
                sc = score[:, 0:keys]
                for h in range(IDX_HEADS):
                    dve.wait_ge(positive, n + 1)
                    if h == 0:
                        ins = nc.vector.tensor_scalar(sc, relu[:, n % 4, 0:keys], iw[:, t, h:h + 1], None, ALU.mult)
                    else:
                        ins = nc.vector.scalar_tensor_tensor(out=sc, in0=relu[:, n % 4, 0:keys],
                                                             scalar=iw[:, t, h:h + 1], in1=sc, op0=ALU.mult,
                                                             op1=ALU.add)
                    ins.then_inc(scored, 1)
                    n += 1
                    dve.wait_ge(scored, n)
                chain.step(nc.vector.tensor_tensor(sc[:, t * P:keys], sc[:, t * P:keys], causal[:, :], ALU.add))
                for _ in range(rounds):
                    chain.step(nc.vector.max(best[:, :], sc))
                    chain.step(nc.vector.match_replace(sc, best[:, :], sc, TAKEN))
                chain.step(nc.vector.tensor_scalar(mask, sc, TAKEN / 2, HIDE, ALU.is_ge, ALU.mult))


def convolve(book, A, xbc, mixed):
    nc = book.nc
    with ExitStack() as ctx, Stage(book, "taps_in", "dve_steps", "summed", "done") as (
            block, taps_in, steps, summed, done):
        taps = ctx.enter_context(nc.sbuf_tensor("taps", [P, XBC_CHUNKS, CONV], F32))
        bias = ctx.enter_context(nc.sbuf_tensor("conv_bias", [P, XBC_CHUNKS], F32))
        acc = ctx.enter_context(nc.sbuf_tensor("conv_acc", [P, 2, S], F32))

        @block.sync
        def _(sp):
            sp.dma_start(taps[:, :, :], A["conv_w"]).then_inc(taps_in, 16)
            sp.dma_start(bias[:, :], A["conv_b"]).then_inc(taps_in, 16)

        @block.vector
        def _(dve):
            chain = Chain(dve, steps)
            dve.wait_ge(taps_in, 32)
            for m in range(XBC_CHUNKS):
                if m >= 2:
                    dve.wait_ge(done, m - 1)
                a = acc[:, m % 2, :]
                chain.step(nc.vector.tensor_scalar(a, xbc[:, m, 0:S], taps[:, m, 0:1], None, ALU.mult))
                for j in range(1, CONV):
                    ins = nc.vector.scalar_tensor_tensor(out=a, in0=xbc[:, m, j:j + S], scalar=taps[:, m, j:j + 1],
                                                         in1=a, op0=ALU.mult, op1=ALU.add)
                    if j < CONV - 1:
                        chain.step(ins)
                ins.then_inc(summed, 1)

        @block.scalar
        def _(act):
            act.wait_ge(taps_in, 32)
            for m in range(XBC_CHUNKS):
                act.wait_ge(summed, m + 1)
                nc.scalar.activation(mixed[:, m, :], acc[:, m % 2, :], ACT.Silu,
                                     bias=bias[:, m:m + 1]).then_inc(done, 1)


def state_space(book, ps, A, ident, ones, mixed, small, z, ssd):
    nc = book.nc
    H = SSD_HEADS
    G = H // 2
    with ExitStack() as ctx:
        sb = lambda name, shape: ctx.enter_context(nc.sbuf_tensor(name, shape, F32))
        xs = sb("xs", [P, T, 5 * P])
        upto = sb("upto", [P, P])
        hidden = sb("hidden", [P, 4, P])
        bias = sb("dt_bias", [P, H])
        a_log = sb("a_log", [P, H])
        skip = sb("skip", [P, H])
        norm_w = sb("norm_w", [P, BANK])
        dt = sb("dt", [P, T, H])
        u1 = sb("u1", [P, T, H])
        u2 = sb("u2", [P, T, H])
        u3 = sb("u3", [P, T, H])
        adt = sb("adt", [P, T, H])
        cum = sb("cum", [P, T, H])
        less_cum = sb("less_cum", [P, T, H])
        grown = sb("grown", [P, T, H])
        fade = sb("fade", [P, T, H])
        last_fade = sb("last_fade", [P, T, H])
        ss = sb("ss_ssd", [P, T])
        root = sb("root_ssd", [P, T])

        with Stage(book, "consts_in", "full", "read", "exp_a", "exp_x", "one_more", "logged", "dt_ready",
                   "adt_ready", "cum_full", "cum_read", "fades", "dve_steps") as (
                block, consts_in, full, read, exp_a, exp_x, one_more, logged, dt_ready, adt_ready, cum_full,
                cum_read, fades, steps):
            raw_dt = small[:, :, DT0:DT0 + H]

            @block.sync
            def _(sp):
                for to, what in ((upto, A["upto"]), (bias, A["dt_bias"].broadcast_to([P, H])),
                                 (a_log, A["a_log"].broadcast_to([P, H])), (skip, A["d_skip"].broadcast_to([P, H])),
                                 (norm_w, A["ssd_norm_w"].broadcast_to([P, BANK]))):
                    sp.dma_start(to[:, :], what).then_inc(consts_in, 16)
                sp.dma_start(hidden[:, :, :], A["hidden"]).then_inc(consts_in, 16)

            @block.tensor
            def _(pe):
                for g in range(T * 2):
                    t, part = divmod(g, 2)
                    if g >= 8:
                        pe.wait_ge(read, g - 7)
                    for j in range(4 if part == 0 else 1):
                        c = 4 * part + j
                        last = nc.tensor.transpose(ps[:, g % 8, tile(j)], mixed[:, c, tile(t)], ident[:, :])
                    last.then_inc(full, 1)
                pe.wait_ge(read, T * 2)
                pe.wait_ge(adt_ready, 1)
                nc.tensor.matmul(ps[:, 0, 0:T * H], upto[:, :], adt[:, :, :].rearrange("p t h -> p (t h)"),
                                 start=True, stop=True).then_inc(cum_full, 1)
                nc.tensor.matmul(ps[:, 1, 0:T * H], ones[:, :], adt[:, :, :].rearrange("p t h -> p (t h)"),
                                 start=True, stop=True).then_inc(cum_full, 1)

            @block.scalar
            def _(act):
                act.wait_ge(consts_in, 96)
                nc.scalar.activation(a_log[:, :], a_log[:, :], ACT.Exp).then_inc(exp_a, 1)
                act.wait_ge(exp_x, 1)
                nc.scalar.activation(u1[:, :, :], u1[:, :, :], ACT.Exp, scale=-1.0).then_inc(exp_a, 1)
                act.wait_ge(one_more, 1)
                nc.scalar.activation(u3[:, :, :], u2[:, :, :], ACT.Ln).then_inc(logged, 1)
                for g in range(T * 2):
                    t, part = divmod(g, 2)
                    act.wait_ge(full, g + 1)
                    w = HALF if part == 0 else P
                    nc.scalar.activation(xs[:, t, part * HALF:part * HALF + w], ps[:, g % 8, 0:w],
                                         ACT.Copy).then_inc(read, 1)
                act.wait_ge(cum_read, 1)
                nc.scalar.activation(grown[:, :, :], cum[:, :, :], ACT.Exp).then_inc(fades, 1)
                nc.scalar.activation(fade[:, :, :], u1[:, :, :], ACT.Exp).then_inc(fades, 1)
                nc.scalar.activation(last_fade[:, :, :], u2[:, :, :], ACT.Exp).then_inc(fades, 1)

            @block.vector
            def _(dve):
                chain = Chain(dve, steps)
                dve.wait_ge(consts_in, 96)
                over = bias[:, :].unsqueeze(1).broadcast_to([P, T, H])
                chain.step(nc.vector.tensor_tensor(dt[:, :, :], raw_dt, over, ALU.add))
                chain.step(nc.vector.tensor_scalar(u1[:, :, :], dt[:, :, :], -1.0, None, ALU.mult))
                nc.vector.tensor_tensor(u1[:, :, :], u1[:, :, :], dt[:, :, :], ALU.max).then_inc(exp_x, 1)
                dve.wait_ge(exp_a, 2)
                nc.vector.tensor_scalar(u2[:, :, :], u1[:, :, :], 1.0, None, ALU.add).then_inc(one_more, 1)
                dve.wait_ge(one_more, 1)
                dve.wait_ge(logged, 1)
                chain.step(nc.vector.tensor_scalar(u2[:, :, :], u2[:, :, :], -1.0, None, ALU.add))
                chain.step(nc.vector.tensor_scalar(cum[:, :, :], u2[:, :, :], 0.0, None, ALU.is_equal))
                chain.step(nc.vector.tensor_tensor(u2[:, :, :], u2[:, :, :], cum[:, :, :], ALU.add))
                chain.step(nc.vector.tensor_tensor(u3[:, :, :], u3[:, :, :], cum[:, :, :], ALU.add))
                chain.step(nc.vector.reciprocal(u2[:, :, :], u2[:, :, :]))
                chain.step(nc.vector.tensor_tensor(u3[:, :, :], u3[:, :, :], u2[:, :, :], ALU.mult))
                chain.step(nc.vector.tensor_tensor(u3[:, :, :], u3[:, :, :], u1[:, :, :], ALU.mult))
                chain.step(nc.vector.tensor_scalar(dt[:, :, :], dt[:, :, :], 0.0, None, ALU.max))
                chain.step(nc.vector.tensor_tensor(dt[:, :, :], dt[:, :, :], u3[:, :, :], ALU.add))
                rate = a_log[:, :].unsqueeze(1).broadcast_to([P, T, H])
                chain.step(nc.vector.tensor_tensor(adt[:, :, :], dt[:, :, :], rate, ALU.mult))
                nc.vector.tensor_scalar(adt[:, :, :], adt[:, :, :], -1.0, None, ALU.mult).then_inc(adt_ready, 1)
                dve.wait_ge(cum_full, 2)
                cums = ps[:, 0, 0:T * H].rearrange("p (t h) -> p t h", t=T)
                lasts = ps[:, 1, 0:T * H].rearrange("p (t h) -> p t h", t=T)
                chain.step(nc.vector.tensor_copy(cum[:, :, :], cums))
                chain.step(nc.vector.tensor_scalar(less_cum[:, :, :], cum[:, :, :], -1.0, None, ALU.mult))
                chain.step(nc.vector.tensor_copy(u2[:, :, :], lasts))
                nc.vector.tensor_tensor(u1[:, :, :], u2[:, :, :], cum[:, :, :], ALU.subtract).then_inc(cum_read, 1)

        with Stage(book, "a_upto_ready", "spans_full", "spans_ready", "pairs_full", "pairs_ready", "x_ready",
                   "inner_full", "outer_full", "state_full", "state_ready", "decayed", "skip_ready", "y_ready",
                   "pool_steps", "dve_steps") as (
                block, a_upto_ready, spans_full, spans_ready, pairs_full, pairs_ready, x_ready, inner_full,
                outer_full, state_full, state_ready, decayed, skip_ready, y_ready, pool_steps, steps), \
                ExitStack() as inner:
            sb = lambda name, shape: inner.enter_context(nc.sbuf_tensor(name, shape, F32))
            a_upto = sb("a_upto", [P, H, P])
            spans = sb("spans", [P, H, P])
            pairs = sb("pairs", [P, H, P])
            xdt = sb("xdt", [P, 2, H * HD])
            xdec = sb("xdec", [P, 2, H * HD])
            state = sb("state", [P, G * HD])
            state_new = sb("state_new", [P, G * HD])
            fade_pair = sb("fade_pair", [P, T, G])
            skipped = sb("skipped", [P, 2, H * HD])
            yo = sb("yo", [P, H * HD])

            @block.tensor
            def _(pe):
                for c in range(T):
                    pe.wait_ge(a_upto_ready, c + 1)
                    for h in range(2):
                        if c >= 1 and h == 0:
                            pe.wait_ge(spans_ready, c)
                        nc.tensor.matmul(ps[:, h, :], ident[:, :], hidden[:, :, :].rearrange("p a b -> p (a b)"),
                                         start=True, stop=False)
                        last = nc.tensor.matmul(ps[:, h, :], ones[:, :],
                                                a_upto[:, 4 * h:4 * h + 4, :].rearrange("p a b -> p (a b)"),
                                                start=False, stop=True)
                    last.then_inc(spans_full, 1)
                    if c >= 1:
                        pe.wait_ge(pairs_ready, 2 * c)
                    for g in range(2):
                        half = slice(g * STATE, (g + 1) * STATE)
                        last = nc.tensor.matmul(ps[:, 2 + g, 0:P], mixed[half, 4, tile(c)], mixed[half, 5, tile(c)],
                                                start=True, stop=True)
                    last.then_inc(pairs_full, 1)
                    if c >= 1:
                        pe.wait_ge(state_ready, c)
                        pe.wait_ge(y_ready, c)
                        for g in range(2):
                            half = slice(g * STATE, (g + 1) * STATE)
                            last = nc.tensor.matmul(ps[:, 5 + 2 * g, 0:256], mixed[half, 5, tile(c)],
                                                    state[half, :], start=True, stop=True)
                        last.then_inc(outer_full, 1)
                    pe.wait_ge(x_ready, c + 1)
                    if c >= 1:
                        pe.wait_ge(state_ready, c)
                    for g in range(2):
                        last = nc.tensor.matmul(ps[g * STATE:(g + 1) * STATE, 6, 0:256],
                                                xs[:, c, HALF + g * STATE:HALF + (g + 1) * STATE],
                                                xdec[:, c % 2, g * 256:(g + 1) * 256], start=True, stop=True)
                    last.then_inc(state_full, 1)
                    pe.wait_ge(pairs_ready, 2 * c + 2)
                    if c >= 1:
                        pe.wait_ge(y_ready, c)
                    for h in range(H):
                        last = nc.tensor.matmul(ps[:, 4, h * HD:(h + 1) * HD], pairs[:, h, :],
                                                xdt[:, c % 2, h * HD:(h + 1) * HD], start=True, stop=True,
                                                skip_group_check=True)
                    last.then_inc(inner_full, 1)

            @block.scalar
            def _(act):
                for c in range(T):
                    act.wait_ge(spans_full, c + 1)
                    if c >= 1:
                        act.wait_ge(pairs_ready, 2 * c)
                    for h in range(H):
                        ins = nc.scalar.activation(spans[:, h, :], ps[:, h // 4, tile(h % 4)], ACT.Exp,
                                                   bias=less_cum[:, c, h:h + 1])
                    ins.then_inc(spans_ready, 1)

            @block.gpsimd
            def _(pool):
                def heads(ap):
                    return ap.rearrange("p (h d) -> p h d", d=HD)

                for g in range(2):
                    half = slice(g * STATE, (g + 1) * STATE)
                    nc.gpsimd.tensor_copy(fade_pair[half, :, :], last_fade[half, :, g * G:(g + 1) * G])\
                        .then_inc(decayed, 1)
                pool.wait_ge(decayed, 2)
                for c in range(T):
                    if c >= 2:
                        pool.wait_ge(inner_full, c - 1)
                        pool.wait_ge(y_ready, c - 1)
                    nc.gpsimd.tensor_tensor(heads(xdt[:, c % 2, :]), heads(xs[:, c, 0:HALF]),
                                            spread(dt[:, c, :], [P, H, HD]), ALU.mult).then_inc(pool_steps, 1)
                    pool.wait_ge(pool_steps, c + 1)
                    nc.gpsimd.tensor_tensor(heads(xdec[:, c % 2, :]), heads(xdt[:, c % 2, :]),
                                            spread(fade[:, c, :], [P, H, HD]), ALU.mult).then_inc(x_ready, 1)
                    nc.gpsimd.tensor_tensor(heads(skipped[:, c % 2, :]), heads(xs[:, c, 0:HALF]),
                                            spread(skip[:, :], [P, H, HD]), ALU.mult).then_inc(skip_ready, 1)

            @block.vector
            def _(dve):
                def heads(ap):
                    return ap.rearrange("p (h d) -> p h d", d=HD)

                chain = Chain(dve, steps)
                for c in range(T):
                    if c >= 1:
                        dve.wait_ge(spans_full, c)
                    nc.vector.tensor_tensor(a_upto[:, :, :], upto[:, :].unsqueeze(1).broadcast_to([P, H, P]),
                                            spread(adt[:, c, :], [P, H, P]), ALU.mult).then_inc(a_upto_ready, 1)
                    dve.wait_ge(spans_ready, c + 1)
                    dve.wait_ge(pairs_full, c + 1)
                    if c >= 1:
                        dve.wait_ge(inner_full, c)
                    for g in range(2):
                        nc.vector.tensor_tensor(pairs[:, 4 * g:4 * g + 4, :], spans[:, 4 * g:4 * g + 4, :],
                                                ps[:, 2 + g, 0:P].unsqueeze(1).broadcast_to([P, 4, P]),
                                                ALU.mult).then_inc(pairs_ready, 1)
                    dve.wait_ge(state_full, c + 1)
                    if c == 0:
                        dve.wait_ge(decayed, 2)
                        nc.vector.tensor_copy(state[:, :], ps[:, 6, 0:256]).then_inc(state_ready, 1)
                    else:
                        dve.wait_ge(outer_full, c)
                        chain.step(nc.vector.tensor_tensor(heads(state_new[:, :]), heads(state[:, :]),
                                                           spread(fade_pair[:, c, :], [P, G, HD]), ALU.mult))
                        nc.vector.tensor_tensor(state[:, :], state_new[:, :], ps[:, 6, 0:256],
                                                ALU.add).then_inc(state_ready, 1)
                    dve.wait_ge(skip_ready, c + 1)
                    dve.wait_ge(inner_full, c + 1)
                    y = ssd[:, c, :]
                    if c >= 1:
                        for g in range(2):
                            part = slice(g * 256, (g + 1) * 256)
                            ins = nc.vector.tensor_tensor(heads(yo[:, part]), heads(ps[:, 5 + 2 * g, 0:256]),
                                                          spread(grown[:, c, g * G:(g + 1) * G], [P, G, HD]),
                                                          ALU.mult)
                        chain.step(ins)
                        chain.step(nc.vector.tensor_tensor(yo[:, :], yo[:, :], ps[:, 4, :], ALU.add))
                        nc.vector.tensor_tensor(y, yo[:, :], skipped[:, c % 2, :], ALU.add).then_inc(y_ready, 1)
                    else:
                        nc.vector.tensor_tensor(y, ps[:, 4, :], skipped[:, c % 2, :], ALU.add).then_inc(y_ready, 1)
        with Stage(book, "gates", "gated", "squares", "means", "roots", "dve_steps") as (
                block, gates, gated, squares, means, roots, steps), ExitStack() as inner:
            junk = inner.enter_context(nc.sbuf_tensor("junk2_ssd", [P, HALF], F32))

            @block.scalar
            def _(act):
                for c in range(T):
                    nc.scalar.activation(z[:, c, :], z[:, c, :], ACT.Silu).then_inc(gates, 1)
                for c in range(T):
                    act.wait_ge(gated, c + 1)
                    nc.scalar.activation(junk[:, :], ssd[:, c, :], ACT.Square,
                                         accum_out=ss[:, c:c + 1]).then_inc(squares, 1)
                    act.wait_ge(squares, c + 1)
                act.wait_ge(means, 1)
                nc.scalar.activation(root[:, :], ss[:, :], ACT.Sqrt).then_inc(roots, 1)

            @block.vector
            def _(dve):
                chain = Chain(dve, steps)
                for c in range(T):
                    dve.wait_ge(gates, c + 1)
                    nc.vector.tensor_tensor(ssd[:, c, :], ssd[:, c, :], z[:, c, :], ALU.mult).then_inc(gated, 1)
                dve.wait_ge(gated, T)
                dve.wait_ge(squares, T)
                nc.vector.tensor_scalar(ss[:, :], ss[:, :], 1.0 / HALF, LN_EPS, ALU.mult, ALU.add).then_inc(means, 1)
                dve.wait_ge(roots, 1)
                chain.step(nc.vector.reciprocal(root[:, :], root[:, :]))
                for c in range(T):
                    nc.vector.scalar_tensor_tensor(out=ssd[:, c, :], in0=ssd[:, c, :], scalar=root[:, c:c + 1],
                                                   in1=norm_w[:, :], op0=ALU.mult, op1=ALU.mult)


def mix_out(book, ps, weights, high, low, residual_scale, rows, source):
    nc = book.nc
    units = [(h, slice(4 * q, 4 * q + 4)) for h in range(2) for q in range(2)]
    with ExitStack() as ctx, Stage(book, "w_in0", "w_in1", "w_in2", "w_in3", "rows_in", "high_ready", "low_ready",
                                   "full", "read") as (
            block, w_in0, w_in1, w_in2, w_in3, rows_in, high_ready, low_ready, full, read):
        w_in = [w_in0, w_in1, w_in2, w_in3]
        w = ctx.enter_context(nc.sbuf_tensor(f"w_mix{book.count}", [P, 2, 4, HALF], F32))
        w_high = ctx.enter_context(nc.sbuf_tensor(f"w_high{book.count}", [P, KD, D], F32R))
        w_low = ctx.enter_context(nc.sbuf_tensor(f"w_low{book.count}", [P, KD, D], F32R))

        @block.sync
        def _(sp):
            for u, (h, ks) in enumerate(units):
                if u >= 2:
                    sp.wait_ge(low_ready, u - 1)
                sp.dma_start(w[:, u % 2, :, :], weights[:, ks, tile(h, HALF)]).then_inc(w_in[u], 16)
            sp.dma_start(rows[:, :, :], source).then_inc(rows_in, 16)

        @block.scalar
        def _(act):
            for u, (h, ks) in enumerate(units):
                act.wait_ge(w_in[u], 16)
                nc.scalar.activation(w_high[:, ks, tile(h, HALF)], w[:, u % 2, :, :],
                                     ACT.Copy).then_inc(high_ready, 1)

        @block.tensor
        def _(pe):
            for g in range(2 * T):
                h, t = divmod(g, T)
                pe.wait_ge(low_ready, 2 * h + 2)
                if g >= 8:
                    pe.wait_ge(read, g - 7)
                cols = tile(h, HALF)
                split_products(nc, ps[:, g % 8, :],
                               [(high[:, k, tile(t)], low[:, k, tile(t)], w_high[:, k, cols], w_low[:, k, cols])
                                for k in range(KD)]).then_inc(full, 1)

        @block.vector
        def _(dve):
            for u, (h, ks) in enumerate(units):
                dve.wait_ge(high_ready, u + 1)
                nc.vector.tensor_tensor(w_low[:, ks, tile(h, HALF)], w[:, u % 2, :, :],
                                        w_high[:, ks, tile(h, HALF)].bitcast(F32), ALU.subtract).then_inc(low_ready, 1)
            dve.wait_ge(rows_in, 16)
            for g in range(2 * T):
                h, t = divmod(g, T)
                dve.wait_ge(full, g + 1)
                out = rows[:, t, tile(h, HALF)]
                if residual_scale == 1.0:
                    nc.vector.tensor_tensor(out, out, ps[:, g % 8, :], ALU.add).then_inc(read, 1)
                else:
                    nc.vector.scalar_tensor_tensor(out=out, in0=out, scalar=residual_scale, in1=ps[:, g % 8, :],
                                                   op0=ALU.mult, op1=ALU.add).then_inc(read, 1)


def route_one(book, ps, A, turned, picked, weights):
    nc = book.nc
    GR, PER = 4, 4
    W = GR + EXPERTS
    with ExitStack() as ctx, Stage(book, "w_in", "bias_in", "full", "shifted", "exps", "dve_steps") as (
            block, w_in, bias_in, full, shifted, exps, steps):
        sb = lambda name, shape: ctx.enter_context(nc.sbuf_tensor(name, shape, F32))
        w = sb("w_route", [P, KD, W])
        bias = sb("b_route", [P, W])
        logit = sb("logit", [P, T, W])
        a = sb("route_a", [P, T, GR])
        b = sb("route_b", [P, T, GR])
        onehot = sb("onehot", [P, T, GR])
        free = sb("free", [P, T])
        m = sb("route_m", [P, T])
        m2 = sb("route_m2", [P, T])
        prob = sb("route_prob", [P, T])
        pick = sb("pick", [P, T, PER])
        both = sb("both", [P, T, PER])
        inner = sb("inner", [P, T, PER])
        tmp = sb("route_tmp", [P, T, PER])
        first_w, second_w = weights[:, 0, :], weights[:, 1, :]

        @block.sync
        def _(sp):
            sp.dma_start(w[:, :, :], A["w_route"]).then_inc(w_in, 16)
            sp.dma_start(bias[:, :], A["b_route"].broadcast_to([P, W])).then_inc(bias_in, 16)

        @block.tensor
        def _(pe):
            pe.wait_ge(w_in, 16)
            for t in range(T):
                for k in range(KD):
                    last = nc.tensor.matmul(ps[:, t, 0:W], turned[:, k, tile(t)], w[:, k, :], start=(k == 0),
                                            stop=(k == KD - 1))
                last.then_inc(full, 1)

        @block.scalar
        def _(act):
            act.wait_ge(shifted, 1)
            nc.scalar.activation(b[:, :, :], b[:, :, :], ACT.Exp).then_inc(exps, 1)
            act.wait_ge(shifted, 2)
            nc.scalar.activation(second_w, second_w, ACT.Exp).then_inc(exps, 1)

        @block.vector
        def _(dve):
            chain = Chain(dve, steps)

            def first_of(out, values, top):
                chain.step(nc.vector.tensor_tensor(out[:, :, :], values, spread(top, [P, T, 4]), ALU.is_equal))
                chain.step(nc.vector.tensor_scalar(free[:, :], out[:, :, 0], -1.0, 1.0, ALU.mult, ALU.add))
                for j in range(1, 4):
                    chain.step(nc.vector.tensor_tensor(out[:, :, j], out[:, :, j], free[:, :], ALU.mult))
                    if j < 3:
                        chain.step(nc.vector.tensor_tensor(free[:, :], free[:, :], out[:, :, j], ALU.subtract))

            dve.wait_ge(bias_in, 16)
            for t in range(T):
                dve.wait_ge(full, t + 1)
                ins = nc.vector.tensor_tensor(logit[:, t, :], ps[:, t, 0:W], bias[:, :], ALU.add)
            chain.step(ins)
            groups = logit[:, :, 0:GR]
            chain.step(nc.vector.tensor_reduce(m[:, :], groups, AX.X, ALU.max))
            nc.vector.tensor_tensor(b[:, :, :], groups, spread(m[:, :], [P, T, GR]), ALU.subtract).then_inc(shifted, 1)
            first_of(onehot, groups, m[:, :])
            dve.wait_ge(exps, 1)
            chain.step(nc.vector.tensor_reduce(prob[:, :], b[:, :, :], AX.X, ALU.add))
            chain.step(nc.vector.reciprocal(prob[:, :], prob[:, :]))
            for g in range(GR):
                of_group = logit[:, :, GR + g * PER:GR + (g + 1) * PER]
                to = inner if g == 0 else tmp
                chain.step(nc.vector.tensor_tensor(to[:, :, :], of_group, spread(onehot[:, :, g], [P, T, PER]),
                                                   ALU.mult))
                if g:
                    chain.step(nc.vector.tensor_tensor(inner[:, :, :], inner[:, :, :], tmp[:, :, :], ALU.add))
            chain.step(nc.vector.tensor_reduce(m[:, :], inner[:, :, :], AX.X, ALU.max))
            first_of(pick, inner[:, :, :], m[:, :])
            chain.step(nc.vector.scalar_tensor_tensor(out=tmp[:, :, :], in0=pick[:, :, :], scalar=HIDE,
                                                      in1=inner[:, :, :], op0=ALU.mult, op1=ALU.add))
            chain.step(nc.vector.tensor_reduce(m2[:, :], tmp[:, :, :], AX.X, ALU.max))
            nc.vector.tensor_tensor(second_w, m2[:, :], m[:, :], ALU.subtract).then_inc(shifted, 1)
            first_of(both, tmp[:, :, :], m2[:, :])
            dve.wait_ge(exps, 2)
            chain.step(nc.vector.tensor_scalar(first_w, second_w, 1.0, None, ALU.add))
            chain.step(nc.vector.reciprocal(first_w, first_w))
            chain.step(nc.vector.tensor_tensor(first_w, first_w, prob[:, :], ALU.mult))
            chain.step(nc.vector.tensor_tensor(second_w, second_w, first_w, ALU.mult))
            for n, of_four in enumerate((pick, both)):
                for g in range(GR):
                    nc.vector.tensor_tensor(picked[:, n, :, g * PER:(g + 1) * PER], of_four[:, :, :],
                                            spread(onehot[:, :, g], [P, T, PER]), ALU.mult)


def place_tokens(book, ps, A, picked, ones, slots, block_tokens, block_expert):
    nc = book.nc
    E = EXPERTS
    with ExitStack() as ctx, Stage(book, "consts_in", "counted_ready", "sums_full", "onehots_ready", "tokens_full",
                                   "dve_steps") as (block, consts_in, counted_ready, sums_full, onehots_ready,
                                                    tokens_full, steps):
        sb = lambda name, shape: ctx.enter_context(nc.sbuf_tensor(name, shape, F32))
        upto = sb("upto_p", [P, P])
        count = sb("count", [P, P])
        eights = sb("eights", [P, 8])
        token = sb("token", [P, T])
        both = sb("both_picked", [P, T, E])
        before = sb("before", [P, T, E])
        pos = sb("pos", [P, T, E])
        n_e = sb("n_e", [P, E])
        over = sb("over_e", [P, E, 8])
        blocks = sb("blocks_e", [P, E])
        ends = sb("ends_e", [P, E])
        starts = sb("starts_e", [P, E])
        past = sb("past", [P, BLOCKS, E])
        expert = sb("expert_b", [P, BLOCKS])
        prod = sb("prod", [P, 2, T, E])
        at = sb("at", [P, 2 * T])
        start = sb("start_t", [P, 2 * T])
        ge = sb("ge", [P, 2 * T, 7])
        q = sb("q_t", [P, 2 * T])
        within = sb("within", [P, 2 * T])
        blk = sb("blk", [P, 2 * T])
        slot = sb("slot", [P, 2 * T])
        hot_slot = sb("hot_slot", [P, 2 * T, P])
        hot_block = sb("hot_block", [P, 2 * T, BLOCKS])
        flat = lambda ap: ap.rearrange("p a b -> p (a b)")
        flat2 = lambda ap: ap.rearrange("p a b c -> p (a b) c")

        @block.sync
        def _(sp):
            for to, what in ((upto, A["upto"]), (count, A["count"]), (eights, A["eights"]), (token, A["token"])):
                sp.dma_start(to[:, :], what).then_inc(consts_in, 16)

        @block.tensor
        def _(pe):
            pe.wait_ge(consts_in, 64)
            pe.wait_ge(counted_ready, 1)
            nc.tensor.matmul(ps[:, 0, 0:T * E], upto[:, :], flat(both[:, :, :]), start=True, stop=True)\
                .then_inc(sums_full, 1)
            nc.tensor.matmul(ps[:, 1, 0:T * E], ones[:, :], flat(both[:, :, :]), start=True, stop=True)\
                .then_inc(sums_full, 1)
            pe.wait_ge(onehots_ready, 1)
            for n in range(2 * T):
                last = nc.tensor.matmul(ps[:, 2, 0:BLOCKS], hot_slot[:, n, :], hot_block[:, n, :], start=(n == 0),
                                        stop=(n == 2 * T - 1))
            last.then_inc(tokens_full, 1)

        @block.vector
        def _(dve):
            chain = Chain(dve, steps)
            tt, ts = nc.vector.tensor_tensor, nc.vector.tensor_scalar
            tt(both[:, :, :], picked[:, 0, :, :], picked[:, 1, :, :], ALU.add).then_inc(counted_ready, 1)
            dve.wait_ge(counted_ready, 1)
            dve.wait_ge(consts_in, 64)
            dve.wait_ge(sums_full, 2)
            inclusive = ps[:, 0, 0:T * E].rearrange("p (t e) -> p t e", t=T)
            totals = ps[:, 1, 0:T * E].rearrange("p (t e) -> p t e", t=T)
            chain.step(nc.vector.memset(before[:, 0, :], 0.0))
            for t in range(1, T):
                chain.step(tt(before[:, t, :], before[:, t - 1, :], totals[:, t - 1, :], ALU.add))
            chain.step(tt(n_e[:, :], before[:, T - 1, :], totals[:, T - 1, :], ALU.add))
            chain.step(tt(pos[:, :, :], inclusive, both[:, :, :], ALU.subtract))
            chain.step(tt(pos[:, :, :], pos[:, :, :], before[:, :, :], ALU.add))
            chain.step(tt(over[:, :, :], spread(n_e[:, :], [P, E, 8]), eights[:, :].unsqueeze(1).broadcast_to([P, E, 8]),
                          ALU.is_gt))
            chain.step(nc.vector.tensor_reduce(blocks[:, :], over[:, :, :], AX.X, ALU.add))
            chain.step(nc.vector.tensor_copy(ends[:, 0:1], blocks[:, 0:1]))
            for e in range(1, E):
                chain.step(tt(ends[:, e:e + 1], ends[:, e - 1:e], blocks[:, e:e + 1], ALU.add))
            chain.step(tt(starts[:, :], ends[:, :], blocks[:, :], ALU.subtract))
            chain.step(tt(past[:, :, :], spread(count[:, 0:BLOCKS], [P, BLOCKS, E]),
                          ends[:, :].unsqueeze(1).broadcast_to([P, BLOCKS, E]), ALU.is_ge))
            chain.step(nc.vector.tensor_reduce(expert[:, :], past[:, :, :], AX.X, ALU.add))
            chain.step(ts(block_expert[:, :], expert[:, :], float(E - 1), None, ALU.min))
            for n in range(2):
                chain.step(tt(prod[:, n, :, :], picked[:, n, :, :], pos[:, :, :], ALU.mult))
            chain.step(nc.vector.tensor_reduce(at[:, :], flat2(prod[:, :, :, :]), AX.X, ALU.add))
            for n in range(2):
                chain.step(tt(prod[:, n, :, :], picked[:, n, :, :],
                              starts[:, :].unsqueeze(1).broadcast_to([P, T, E]), ALU.mult))
            chain.step(nc.vector.tensor_reduce(start[:, :], flat2(prod[:, :, :, :]), AX.X, ALU.add))
            chain.step(tt(ge[:, :, :], spread(at[:, :], [P, 2 * T, 7]),
                          eights[:, 1:8].unsqueeze(1).broadcast_to([P, 2 * T, 7]), ALU.is_ge))
            chain.step(nc.vector.tensor_reduce(q[:, :], ge[:, :, :], AX.X, ALU.add))
            chain.step(nc.vector.scalar_tensor_tensor(out=within[:, :], in0=q[:, :], scalar=-float(P), in1=at[:, :],
                                                      op0=ALU.mult, op1=ALU.add))
            chain.step(tt(blk[:, :], start[:, :], q[:, :], ALU.add))
            chain.step(nc.vector.scalar_tensor_tensor(out=slot[:, :], in0=blk[:, :], scalar=float(P),
                                                      in1=within[:, :], op0=ALU.mult, op1=ALU.add))
            nc.vector.tensor_copy(slots.rearrange("p a b -> p (a b)"), slot[:, :])
            chain.step(tt(hot_slot[:, :, :], count[:, :].unsqueeze(1).broadcast_to([P, 2 * T, P]),
                          spread(within[:, :], [P, 2 * T, P]), ALU.is_equal))
            chain.step(tt(hot_block[:, :, :], count[:, 0:BLOCKS].unsqueeze(1).broadcast_to([P, 2 * T, BLOCKS]),
                          spread(blk[:, :], [P, 2 * T, BLOCKS]), ALU.is_equal))
            for n in range(2):
                ins = tt(hot_block[:, n * T:(n + 1) * T, :], hot_block[:, n * T:(n + 1) * T, :],
                         spread(token[:, :], [P, T, BLOCKS]), ALU.mult)
                if n == 0:
                    chain.step(ins)
            ins.then_inc(onehots_ready, 1)
            dve.wait_ge(tokens_full, 1)
            nc.vector.tensor_copy(block_tokens[:, :], ps[:, 2, 0:BLOCKS])


def experts_one(book, ps, A, ident, block_tokens, block_expert):
    nc = book.nc
    UP, DOWN = 4, 2
    UNITS = UP + DOWN
    with ExitStack() as ctx:
        sb = lambda name, shape, dt=F32: ctx.enter_context(nc.sbuf_tensor(name, shape, dt))
        w_up = sb("w_up_ring", [P, UP, KD // UP, 2 * FF])
        w_down = sb("w_down_ring", [P, DOWN, D])
        taken = sb("taken_1", [P, D])
        xs = sb("xs_1", [P, KD, P])
        silu = sb("silu_1", [P, FF])
        hid = sb("hid_1", [P, FF])
        hidt = sb("hidt_1", [P, 2, P])
        out = sb("out_1", [P, D])
        take_from = sb("take_from_1", [P, 1], U32)
        unit_sems = [f"unit{n}_in" for n in range(UNITS)]
        with Stage(book, *unit_sems, "x_turned", "x_read", "silu_done", "hid_ready", "hid_turned",
                   "hid_read", "out_ready", "stored", "unit_used", "first_ready", "from_ready") as (block, *sems):
            unit_in = sems[:UNITS]
            (x_turned, x_read, silu_done, hid_ready, hid_turned, hid_read, out_ready, stored, unit_used, first_ready,
             from_ready) = sems[UNITS:]
            taken_in = A["taken_one"]

            @block.sync
            def _(sp):
                def units(b, later):
                    expert = sp.value_load(block_expert[0:1, bass.ds(b, 1)], min_val=0, max_val=EXPERTS - 1)
                    one = bass.ds(expert, 1)
                    up = A["w_gate_up"][one].rearrange("a (k p) f -> p (a k) f", p=P)
                    down = A["w_down"][one].rearrange("a (k p) f -> p (a k) f", p=P)
                    for n in range(UNITS):
                        if later:
                            sp.wait_ge(unit_used, (b - 1) * UNITS + n + 1)
                        if n < UP:
                            sp.dma_start(w_up[:, n, :, :], up[:, 2 * n:2 * n + 2, :]).then_inc(unit_in[n], 16)
                        else:
                            sp.dma_start(w_down[:, n - UP, :], down[:, n - UP, :]).then_inc(unit_in[n], 16)

                def store(b):
                    sp.wait_ge(out_ready, 2 * b + 2)
                    sp.dma_start(A["expert_out"][bass.ds(b * P, P), :], out[:, :]).then_inc(stored, 16)

                units(0, False)
                with sp.Fori(1, BLOCKS) as b:
                    units(b, True)
                    store(b - 1)
                store(BLOCKS - 1)
                sp.wait_ge(stored, 16 * BLOCKS)

            @block.gpsimd
            def _(pool):
                def gather(b, ready):
                    nc.gpsimd.tensor_copy(take_from[:, :], block_tokens[:, bass.ds(b, 1)]).then_inc(ready, 1)
                    pool.wait_ge(ready, 1)
                    pool.wait_ge(ready, 1 if isinstance(b, int) else b)
                    pool.indirect_dma_start(taken[:, :], None, A["normed"],
                                            bass.IndirectOffsetOnAxis(ap=take_from[:, 0:1], axis=0))\
                        .then_inc(taken_in, 16)

                gather(0, first_ready)
                with pool.Fori(0, BLOCKS - 1) as b:
                    pool.wait_ge(x_turned, 2 * b + 2)
                    gather(b + 1, from_ready)

            @block.tensor
            def _(pe):
                def turn_rows(b):
                    pe.wait_ge(taken_in, 16 * b + 16)
                    for h in range(2):
                        for j in range(4):
                            last = nc.tensor.transpose(ps[:, 2 + h, tile(j)], taken[:, tile(4 * h + j)], ident[:, :])
                        last.then_inc(x_turned, 1)

                def up(b, later):
                    pe.wait_ge(x_read, 2 * b + 2)
                    for n in range(UP):
                        pe.wait_ge(unit_in[n], 16 * b + 16)
                        for k in range(2):
                            last = nc.tensor.matmul(ps[:, 0, :], xs[:, 2 * n + k, :], w_up[:, n, k, :],
                                                    start=(n == 0 and k == 0), stop=(n == UP - 1 and k == 1))
                        last.then_inc(unit_used, 1)

                def down(b, later):
                    pe.wait_ge(hid_ready, b + 1)
                    for j in range(2):
                        last = nc.tensor.transpose(ps[:, 1, tile(j)], hid[:, tile(j)], ident[:, :])
                    last.then_inc(hid_turned, 1)
                    if later:
                        pe.wait_ge(out_ready, 2 * b)
                    pe.wait_ge(hid_read, b + 1)
                    for n in range(DOWN):
                        pe.wait_ge(unit_in[UP + n], 16 * b + 16)
                        for h in range(2):
                            last = nc.tensor.matmul(ps[:, 4 + h, :], hidt[:, n, :], w_down[:, n, tile(h, HALF)],
                                                    start=(n == 0), stop=(n == DOWN - 1))
                        last.then_inc(unit_used, 1)

                turn_rows(0)
                up(0, False)
                turn_rows(1)
                down(0, False)
                with pe.Fori(1, BLOCKS - 1) as b:
                    up(b, True)
                    turn_rows(b + 1)
                    down(b, True)
                up(BLOCKS - 1, True)
                down(BLOCKS - 1, True)

            @block.scalar
            def _(act):
                def copy_x(b):
                    for h in range(2):
                        act.wait_ge(x_turned, 2 * b + h + 1)
                        nc.scalar.activation(xs[:, 4 * h:4 * h + 4, :].rearrange("p a b -> p (a b)"), ps[:, 2 + h, :],
                                             ACT.Copy).then_inc(x_read, 1)

                def gate(b):
                    act.wait_ge(unit_used, b * UNITS + UP)
                    nc.scalar.activation(silu[:, :], ps[:, 0, 0:FF], ACT.Silu).then_inc(silu_done, 1)

                copy_x(0)
                with act.Fori(0, BLOCKS - 1) as b:
                    gate(b)
                    copy_x(b + 1)
                gate(BLOCKS - 1)

            @block.vector
            def _(dve):
                def finish(b, later):
                    dve.wait_ge(silu_done, b + 1)
                    nc.vector.tensor_tensor(hid[:, :], silu[:, :], ps[:, 0, FF:2 * FF], ALU.mult).then_inc(hid_ready, 1)
                    dve.wait_ge(hid_turned, b + 1)
                    nc.vector.tensor_copy(hidt[:, :, :].rearrange("p a b -> p (a b)"), ps[:, 1, 0:FF])\
                        .then_inc(hid_read, 1)
                    dve.wait_ge(unit_used, b * UNITS + UNITS)
                    if later:
                        dve.wait_ge(stored, 16 * b)
                    for h in range(2):
                        nc.vector.tensor_copy(out[:, tile(h, HALF)], ps[:, 4 + h, :]).then_inc(out_ready, 1)

                finish(0, False)
                with dve.Fori(1, BLOCKS) as b:
                    finish(b, True)



def combine_one(book, A, slots, weights, rows):
    nc = book.nc
    with ExitStack() as ctx, Stage(book, "scaled", "added", "dve_steps") as (block, scaled, added, steps):
        part = ctx.enter_context(nc.sbuf_tensor("part", [P, 4, D], F32))
        came_in = A["came_in"]

        @block.gpsimd
        def _(pool):
            for n in range(2 * T):
                if n >= 4:
                    pool.wait_ge(added, n - 3)
                pool.indirect_dma_start(part[:, n % 4, :], None, A["expert_out"],
                                        bass.IndirectOffsetOnAxis(ap=slots[:, n % 2, n // 2:n // 2 + 1], axis=0))\
                    .then_inc(came_in[n % 4], 16)

        @block.vector
        def _(dve):
            for t in range(T):
                nc.vector.tensor_scalar(rows[:, t, :], rows[:, t, :], ALPHA, None, ALU.mult).then_inc(scaled, 1)
            dve.wait_ge(scaled, T)
            for n in range(2 * T):
                dve.wait_ge(came_in[n % 4], 16 * (n // 4 + 1))
                if n % 2:
                    dve.wait_ge(added, n)
                out = rows[:, n // 2, :]
                nc.vector.scalar_tensor_tensor(out=out, in0=part[:, n % 4, :], scalar=weights[:, n % 2, n // 2:n // 2 + 1],
                                               in1=out, op0=ALU.mult, op1=ALU.add).then_inc(added, 1)


def project_two(book, ps, A, layer, high, low, qk, rows_out):
    nc = book.nc
    TURNED, UNITS = 5, 8
    W = 2 * P
    with ExitStack() as ctx, Stage(book, "w_in", "high_ready", "low_ready", "full", "read") as (
            block, w_in, high_ready, low_ready, full, read):
        w = ctx.enter_context(nc.sbuf_tensor("w_unit", [P, KD * W], F32))
        w_high = ctx.enter_context(nc.sbuf_tensor("w_unit_high", [P, 2, KD * W], F32R))
        w_low = ctx.enter_context(nc.sbuf_tensor("w_unit_low", [P, 2, KD * W], F32R))
        mine = bass.ds(layer * P, P)
        groups = [(u, m, h) for u in range(TURNED) for m in range(2) for h in range(2)]
        groups += [(u, None, t) for u in range(TURNED, UNITS) for t in range(T)]

        def piece(ap, slot, m, k):
            if m is None:
                return ap[:, slot, k * W:(k + 1) * W]
            return ap[:, slot, (m * KD + k) * P:(m * KD + k + 1) * P]

        @block.sync
        def _(sp):
            for u in range(UNITS):
                if u < TURNED:
                    what = A["w_turned_2"][mine, 2 * u:2 * u + 2].rearrange("p m k c -> p (m k c)")
                    to = w[:, :]
                else:
                    what = A["w_rows_2"][mine][:, :, tile(u - TURNED, W)]
                    to = w[:, :].rearrange("p (k w) -> p k w", w=W)
                if u >= 1:
                    sp.wait_ge(low_ready, u)
                sp.dma_start(to, what).then_inc(w_in, 16)

        @block.tensor
        def _(pe):
            for g, (u, m, part) in enumerate(groups):
                pe.wait_ge(low_ready, u + 1)
                if g >= 8:
                    pe.wait_ge(read, g - 7)
                if m is None:
                    pairs = [(high[:, k, tile(part)], low[:, k, tile(part)],
                              piece(w_high, u % 2, m, k), piece(w_low, u % 2, m, k)) for k in range(KD)]
                    out = ps[:, g % 8, 0:W]
                else:
                    pairs = [(piece(w_high, u % 2, m, k), piece(w_low, u % 2, m, k),
                              high[:, k, tile(part, HALF)], low[:, k, tile(part, HALF)]) for k in range(KD)]
                    out = ps[:, g % 8, :]
                split_products(nc, out, pairs).then_inc(full, 1)

        @block.scalar
        def _(act):
            def split(u):
                act.wait_ge(w_in, 16 * (u + 1))
                nc.scalar.activation(w_high[:, u % 2, :], w[:, :], ACT.Copy).then_inc(high_ready, 1)

            split(0)
            for g, (u, m, part) in enumerate(groups):
                if (g == 0 or groups[g - 1][0] != u) and u + 1 < UNITS:
                    split(u + 1)
                act.wait_ge(full, g + 1)
                if m is None:
                    out, made = rows_out[:, part, tile(u - TURNED, W)], ps[:, g % 8, 0:W]
                else:
                    out, made = qk[:, 2 * u + m, tile(part, HALF)], ps[:, g % 8, :]
                nc.scalar.activation(out, made, ACT.Copy).then_inc(read, 1)

        @block.vector
        def _(dve):
            for u in range(UNITS):
                if u >= 2:
                    dve.wait_ge(full, len([g for g in groups if g[0] <= u - 2]))
                dve.wait_ge(high_ready, u + 1)
                nc.vector.tensor_tensor(w_low[:, u % 2, :], w[:, :],
                                        w_high[:, u % 2, :].bitcast(F32), ALU.subtract).then_inc(low_ready, 1)


def expand_latents(book, ps, A, layer, latents, k_rope, q, k, v):
    nc = book.nc
    H = MLA_HEADS
    with ExitStack() as ctx, Stage(book, "w_in", "full", "read", "shared") as (block, w_in, full, read, shared):
        wq = ctx.enter_context(nc.sbuf_tensor("w_uq", [P, 2, H * MLA_D], F32))
        wkv = ctx.enter_context(nc.sbuf_tensor("w_ukv", [P, 2 * H * HD], F32))
        mine = bass.ds(layer * P, P)

        @block.sync
        def _(sp):
            sp.dma_start(wq[:, :, :], A["mla_w_uq"][mine]).then_inc(w_in, 16)
            sp.dma_start(wkv[:, :], A["mla_w_ukv"][mine]).then_inc(w_in, 16)

        @block.tensor
        def _(pe):
            pe.wait_ge(w_in, 32)
            g = 0
            for h in range(H):
                for s in range(2):
                    if g >= 8:
                        pe.wait_ge(read, g - 7)
                    for c in range(2):
                        last = nc.tensor.matmul(ps[0:MLA_D, g % 8, :], wq[:, c, h * MLA_D:(h + 1) * MLA_D],
                                                latents[:, c, tile(s, HALF)], start=(c == 0), stop=(c == 1))
                    last.then_inc(full, 1)
                    g += 1
            for h in range(H):
                for s in range(2):
                    pe.wait_ge(read, g - 7)
                    nc.tensor.matmul(ps[0:HD, g % 8, :], wkv[:, h * HD:(h + 1) * HD], latents[:, 2, tile(s, HALF)],
                                     start=True, stop=True).then_inc(full, 1)
                    g += 1
            for t in range(T):
                pe.wait_ge(read, g - 7)
                nc.tensor.matmul(ps[:, g % 8, 0:H * HD], latents[:, 2, tile(t)], wkv[:, H * HD:2 * H * HD],
                                 start=True, stop=True).then_inc(full, 1)
                g += 1

        @block.scalar
        def _(act):
            g = 0
            for h in range(H):
                for s in range(2):
                    act.wait_ge(full, g + 1)
                    nc.scalar.activation(q[0:MLA_D, h, tile(s, HALF)], ps[0:MLA_D, g % 8, :], ACT.Copy)\
                        .then_inc(read, 1)
                    g += 1
            for h in range(H):
                for s in range(2):
                    act.wait_ge(full, g + 1)
                    nc.scalar.activation(k[0:HD, h, tile(s, HALF)], ps[0:HD, g % 8, :], ACT.Copy).then_inc(read, 1)
                    g += 1
            for t in range(T):
                act.wait_ge(full, g + 1)
                nc.scalar.activation(v[:, t, :], ps[:, g % 8, 0:H * HD], ACT.Copy).then_inc(read, 1)
                g += 1

        @block.vector
        def _(dve):
            for h in range(H):
                nc.vector.tensor_copy(k[HD:MLA_D, h, :], k_rope[HD:MLA_D, :])


def choose_tokens(book, ps, A, layer, ident, turned, gates, index):
    nc = book.nc
    rounds = CAP // 8
    with ExitStack() as ctx, Stage(book, "w_in", "full", "shifted", "exps", "aff_ready", "aff_turned", "dve_steps",
                                   "chosen", "slots_full") as (
            block, w_in, full, shifted, exps, aff_ready, aff_turned, steps, chosen, slots_full):
        sb = lambda name, shape, dt=F32: ctx.enter_context(nc.sbuf_tensor(name, shape, dt))
        w = sb("w_router", [P, KD, EXPERTS])
        aff = sb("aff", [P, T, EXPERTS])
        m = sb("aff_m", [P, T])
        total = sb("aff_total", [P, T])
        byexp = sb("byexp", [EXPERTS, S])
        best = sb("best_aff", [EXPERTS, CAP])
        where = sb("where", [EXPERTS, CAP], U32)
        wheref = sb("wheref", [EXPERTS, CAP])

        @block.sync
        def _(sp):
            sp.dma_start(w[:, :, :], A["w_router"][bass.ds(layer * P, P)]).then_inc(w_in, 16)

        @block.tensor
        def _(pe):
            pe.wait_ge(w_in, 16)
            for t in range(T):
                for k in range(KD):
                    last = nc.tensor.matmul(ps[:, t, 0:EXPERTS], turned[:, k, tile(t)], w[:, k, :], start=(k == 0),
                                            stop=(k == KD - 1))
                last.then_inc(full, 1)
            pe.wait_ge(aff_ready, 1)
            for t in range(T):
                last = nc.tensor.transpose(ps[0:EXPERTS, t // 4, tile(t % 4)], aff[:, t, :], ident[:, :])
            last.then_inc(aff_turned, 1)
            pe.wait_ge(chosen, 1)
            nc.tensor.transpose(ps[:, 2, 0:EXPERTS], best[:, :], ident[0:EXPERTS, 0:EXPERTS])
            nc.tensor.transpose(ps[:, 3, 0:EXPERTS], wheref[:, :], ident[0:EXPERTS, 0:EXPERTS]).then_inc(slots_full, 1)

        @block.scalar
        def _(act):
            act.wait_ge(shifted, 1)
            nc.scalar.activation(aff[:, :, :], aff[:, :, :], ACT.Exp).then_inc(exps, 1)

        @block.vector
        def _(dve):
            chain = Chain(dve, steps)
            dve.wait_ge(full, T)
            logit = ps[:, 0:T, 0:EXPERTS]
            chain.step(nc.vector.tensor_reduce(m[:, :], logit, AX.X, ALU.max))
            nc.vector.tensor_tensor(aff[:, :, :], logit, spread(m[:, :], [P, T, EXPERTS]), ALU.subtract)\
                .then_inc(shifted, 1)
            dve.wait_ge(exps, 1)
            chain.step(nc.vector.tensor_reduce(total[:, :], aff[:, :, :], AX.X, ALU.add))
            chain.step(nc.vector.reciprocal(total[:, :], total[:, :]))
            nc.vector.tensor_tensor(aff[:, :, :], aff[:, :, :], spread(total[:, :], [P, T, EXPERTS]), ALU.mult)\
                .then_inc(aff_ready, 1)
            dve.wait_ge(aff_turned, 1)
            chain.step(nc.vector.tensor_copy(byexp[:, :].rearrange("p (a b) -> p a b", a=2), ps[0:EXPERTS, 0:2, :]))
            for r in range(rounds):
                top = best[:, 8 * r:8 * r + 8]
                chain.step(nc.vector.max(top, byexp[:, :]))
                nc.vector.max_index(where[:, 8 * r:8 * r + 8], top, byexp[:, :])
                chain.step(nc.vector.match_replace(byexp[:, :], top, byexp[:, :], -1.0))
            nc.vector.tensor_copy(wheref[:, :], where[:, :]).then_inc(chosen, 1)
            dve.wait_ge(slots_full, 1)
            nc.vector.tensor_copy(gates[:, :], ps[:, 2, 0:EXPERTS])
            nc.vector.tensor_copy(index[:, :], ps[:, 3, 0:EXPERTS])


def experts_two(book, ps, A, layer, taken_in, summed, ident, gain, gates, index, rows_dram, sum_dram):
    nc = book.nc
    UNITS, UP, RING, AHEAD = 12, 8, 6, 4
    with ExitStack() as ctx:
        sb = lambda name, shape, dt=F32: ctx.enter_context(nc.sbuf_tensor(name, shape, dt))
        raw = sb("raw_ring", [P, RING, 2048])
        w_high = sb("high_ring", [P, RING, 2048], F32R)
        w_low = sb("low_ring", [P, RING, 2048], F32R)
        taken = sb("taken", [P, D])
        x_high = sb("x_high", [P, KD, P], F32R)
        x_low = sb("x_low", [P, KD, P], F32R)
        silu = sb("silu_e", [P, D])
        hid = sb("hid_e", [P, D])
        h_high = sb("h_high", [P, KD, P], F32R)
        h_low = sb("h_low", [P, KD, P], F32R)
        out = sb("out_e", [P, D])
        take_from = sb("take_from", [P, 1], U32)
        add_to = sb("add_to", [P, 1], U32)
        gcol = sb("gcol", [P, 1])
        base = 16 * EXPERTS * layer
        wg, wu, wd = A["w_gate_2"], A["w_up_2"], A["w_down_2"]

        def unit_source(e, n):
            row = layer * EXPERTS + e
            if n < UP:
                h, kind, q = n // 4, (n // 2) % 2, n % 2
                w = (wg, wu)[kind]
                return w[bass.ds(row, 1)].rearrange("a (k p) f -> p (a k) f", p=P)[:, 4 * q:4 * q + 4, tile(h, HALF)]
            q = n - UP
            return wd[bass.ds(row, 1)].rearrange("a (k p) f -> p (a k) f", p=P)[:, 2 * q:2 * q + 2, :]

        def unit_view(ring, n):
            return ring[:, n % RING, :].rearrange("p (k f) -> p k f", k=4 if n < UP else 2)

        unit_sems = [f"unit{n}_in" for n in range(RING)]
        with Stage(book, *unit_sems, "high_ready", "low_ready", "unit_used", "x_turned", "x_high_ready",
                   "x_low_ready", "silu_done", "hid_ready", "hid_turned", "h_high_ready", "h_low_ready",
                   "out_ready", "first_ready", "from_ready", "to_ready", "gate_ready") as (block, *sems):
            unit_in = sems[:RING]
            (high_ready, low_ready, unit_used, x_turned, x_high_ready, x_low_ready, silu_done, hid_ready, hid_turned,
             h_high_ready, h_low_ready, out_ready, first_ready, from_ready, to_ready, gate_ready) = sems[RING:]

            @block.sync
            def _(sp):
                def load_unit(e, n, later):
                    if later or n >= RING:
                        sp.wait_ge(low_ready, e * UNITS + n - RING + 1)
                    sp.dma_start(unit_view(raw, n), unit_source(e, n)).then_inc(unit_in[n % RING], 16)

                for n in range(UNITS):
                    load_unit(0, n, False)
                with sp.Fori(1, EXPERTS) as e:
                    for n in range(UNITS):
                        load_unit(e, n, True)

            @block.gpsimd
            def _(pool):
                def gather(e, ready):
                    nc.gpsimd.tensor_copy(take_from[:, :], index[:, bass.ds(e, 1)]).then_inc(ready, 1)
                    pool.wait_ge(ready, 1)
                    pool.wait_ge(ready, 1 if isinstance(e, int) else e)
                    pool.indirect_dma_start(taken[:, :], None, rows_dram,
                                            bass.IndirectOffsetOnAxis(ap=take_from[:, 0:1], axis=0))\
                        .then_inc(taken_in, 16)

                def scatter(e):
                    nc.gpsimd.tensor_copy(add_to[:, :], index[:, bass.ds(e, 1)]).then_inc(to_ready, 1)
                    pool.wait_ge(to_ready, 1)
                    pool.wait_ge(to_ready, e + 1)
                    pool.wait_ge(out_ready, 2 * e + 2)
                    pool.indirect_dma_start(sum_dram, bass.IndirectOffsetOnAxis(ap=add_to[:, 0:1], axis=0),
                                            out[:, :], None, compute_op=ALU.add).then_inc(summed, 16)
                    pool.wait_ge(summed, base + 16 * e + 16)

                gather(0, first_ready)
                with pool.Fori(0, EXPERTS - 1) as e:
                    pool.wait_ge(x_turned, 2 * e + 2)
                    gather(e + 1, from_ready)
                    scatter(e)
                scatter(EXPERTS - 1)

            @block.tensor
            def _(pe):
                def turn_x(e):
                    pe.wait_ge(taken_in, base + 16 * e + 16)
                    for h in range(2):
                        for j in range(4):
                            last = nc.tensor.transpose(ps[:, h, tile(j)], taken[:, tile(4 * h + j)], ident[:, :])
                        last.then_inc(x_turned, 1)

                def turn_hid(e, h):
                    pe.wait_ge(hid_ready, 2 * e + h + 1)
                    for j in range(4):
                        last = nc.tensor.transpose(ps[:, 4 + h, tile(j)], hid[:, tile(4 * h + j)], ident[:, :])
                    last.then_inc(hid_turned, 1)

                def product(bank, left_high, left_low, n, k, cols, first, final):
                    high, low = unit_view(w_high, n)[:, k, cols], unit_view(w_low, n)[:, k, cols]
                    nc.tensor.matmul(ps[:, bank, :], left_high, high, start=first, stop=False)
                    nc.tensor.matmul(ps[:, bank, :], left_high, low, start=False, stop=False)
                    return nc.tensor.matmul(ps[:, bank, :], left_low, high, start=False, stop=final)

                def up_unit(e, n):
                    h, kind, q = n // 4, (n // 2) % 2, n % 2
                    pe.wait_ge(low_ready, e * UNITS + n + 1)
                    for k in range(4):
                        c = 4 * q + k
                        last = product(2 * h + kind, x_high[:, c, :], x_low[:, c, :], n, k, slice(0, HALF),
                                       c == 0, c == KD - 1)
                    last.then_inc(unit_used, 1)

                def down_unit(e, n):
                    pe.wait_ge(low_ready, e * UNITS + n + 1)
                    for k in range(2):
                        c = 2 * (n - UP) + k
                        for h in range(2):
                            last = product(6 + h, h_high[:, c, :], h_low[:, c, :], n, k, tile(h, HALF),
                                           c == 0, c == KD - 1)
                    last.then_inc(unit_used, 1)

                def expert(e, later, more):
                    pe.wait_ge(x_low_ready, 2 * e + 2)
                    for n in range(6):
                        up_unit(e, n)
                    turn_hid(e, 0)
                    for n in range(6, UP):
                        up_unit(e, n)
                    if later:
                        pe.wait_ge(out_ready, 2 * e)
                    pe.wait_ge(h_low_ready, 2 * e + 1)
                    down_unit(e, 8)
                    turn_hid(e, 1)
                    down_unit(e, 9)
                    if more:
                        turn_x(e + 1)
                    pe.wait_ge(h_low_ready, 2 * e + 2)
                    down_unit(e, 10)
                    down_unit(e, 11)

                turn_x(0)
                expert(0, False, True)
                with pe.Fori(1, EXPERTS - 1) as e:
                    expert(e, True, True)
                expert(EXPERTS - 1, True, False)

            @block.scalar
            def _(act):
                def split(e, n, later):
                    act.wait_ge(unit_in[n % RING], 32 * e + 16 * (n // RING) + 16)
                    if later or n >= RING:
                        act.wait_ge(unit_used, e * UNITS + n - RING + 1)
                    nc.scalar.activation(w_high[:, n % RING, :], raw[:, n % RING, :], ACT.Copy).then_inc(high_ready, 1)

                def high_x(e):
                    for h in range(2):
                        act.wait_ge(x_turned, 2 * e + h + 1)
                        for j in range(4):
                            c = 4 * h + j
                            ins = nc.scalar.activation(x_high[:, c, :], ps[:, h, tile(j)], ACT.Copy,
                                                       scale=gain[:, c:c + 1])
                        ins.then_inc(x_high_ready, 1)

                def gate(e, h):
                    act.wait_ge(unit_used, e * UNITS + 4 * h + 2)
                    nc.scalar.activation(silu[:, tile(h, HALF)], ps[:, 2 * h, :], ACT.Silu).then_inc(silu_done, 1)

                def high_hid(e, h):
                    act.wait_ge(hid_turned, 2 * e + h + 1)
                    nc.scalar.activation(h_high[:, 4 * h:4 * h + 4, :].rearrange("p a b -> p (a b)"),
                                         ps[:, 4 + h, :], ACT.Copy).then_inc(h_high_ready, 1)

                def expert(e, later, more):
                    units = UNITS + AHEAD if more else UNITS
                    for n in range(AHEAD, units):
                        split(e, n, later)
                        if n == 5:
                            gate(e, 0)
                        if n == 9:
                            gate(e, 1)
                            high_hid(e, 0)
                        if n == 12:
                            high_hid(e, 1)
                        if n == 13:
                            high_x(e + 1)
                    if not more:
                        high_hid(e, 1)

                for n in range(2):
                    split(0, n, False)
                high_x(0)
                for n in range(2, AHEAD):
                    split(0, n, False)
                expert(0, False, True)
                with act.Fori(1, EXPERTS - 1) as e:
                    expert(e, True, True)
                expert(EXPERTS - 1, True, False)

            @block.vector
            def _(dve):
                def split(e, n):
                    dve.wait_ge(high_ready, e * UNITS + n + 1)
                    nc.vector.tensor_tensor(w_low[:, n % RING, :], raw[:, n % RING, :],
                                            w_high[:, n % RING, :].bitcast(F32), ALU.subtract).then_inc(low_ready, 1)

                def low_x(e):
                    for h in range(2):
                        dve.wait_ge(x_high_ready, 2 * e + h + 1)
                        for j in range(4):
                            c = 4 * h + j
                            ins = nc.vector.scalar_tensor_tensor(out=x_low[:, c, :], in0=ps[:, h, tile(j)],
                                                                 scalar=gain[:, c:c + 1],
                                                                 in1=x_high[:, c, :].bitcast(F32), op0=ALU.mult,
                                                                 op1=ALU.subtract)
                        ins.then_inc(x_low_ready, 1)

                def hidden(e, h):
                    dve.wait_ge(silu_done, 2 * e + h + 1)
                    dve.wait_ge(unit_used, e * UNITS + 4 * h + 4)
                    nc.vector.tensor_tensor(hid[:, tile(h, HALF)], silu[:, tile(h, HALF)], ps[:, 2 * h + 1, :],
                                            ALU.mult).then_inc(hid_ready, 1)

                def low_hid(e, h):
                    dve.wait_ge(h_high_ready, 2 * e + h + 1)
                    four = slice(4 * h, 4 * h + 4)
                    nc.vector.tensor_tensor(h_low[:, four, :].rearrange("p a b -> p (a b)"), ps[:, 4 + h, :],
                                            h_high[:, four, :].rearrange("p a b -> p (a b)").bitcast(F32),
                                            ALU.subtract).then_inc(h_low_ready, 1)

                def finish(e, later):
                    if later:
                        dve.wait_ge(out_ready, 2 * e)
                    nc.vector.tensor_copy(gcol[:, :], gates[:, bass.ds(e, 1)]).then_inc(gate_ready, 1)
                    dve.wait_ge(gate_ready, e + 1)
                    dve.wait_ge(unit_used, e * UNITS + UNITS)
                    if later:
                        dve.wait_ge(summed, base + 16 * e)
                    for h in range(2):
                        nc.vector.tensor_scalar(out[:, tile(h, HALF)], ps[:, 6 + h, :], gcol[:, :], None,
                                                ALU.mult).then_inc(out_ready, 1)

                def expert(e, later, more):
                    for n in range(AHEAD, UNITS):
                        split(e, n)
                        if n == 7:
                            hidden(e, 0)
                        if n == 9:
                            low_hid(e, 0)
                        if n == 11:
                            hidden(e, 1)
                    if more:
                        split(e, 12)
                    low_hid(e, 1)
                    if more:
                        split(e, 13)
                        low_x(e + 1)
                        split(e, 14)
                        split(e, 15)
                    finish(e, later)

                split(0, 0)
                split(0, 1)
                low_x(0)
                split(0, 2)
                split(0, 3)
                expert(0, False, True)
                with dve.Fori(1, EXPERTS - 1) as e:
                    expert(e, True, True)
                expert(EXPERTS - 1, True, False)


def neighbourhood_items(qk, v, v_shifted, bias, out):
    items = []
    for t in range(T):
        for h in range(NA_HEADS):
            half = slice((h % 2) * HD, (h % 2 + 1) * HD)
            scores, add, values = [], [], []
            for j in range(2):
                r = 2 * t + j
                start = min(max(r - NA_H // 2, 0), GRID_H - NA_H)
                a, b = j * GRID_W, (j + 1) * GRID_W
                q = qk[half, h // 2, r * GRID_W:(r + 1) * GRID_W]
                k = qk[half, 2 + h // 2, start * GRID_W:(start + NA_H) * GRID_W]
                scores.append((a, b, q, k))
                dr = start - r + NA_H - 1
                add.append((a, b, bias[a:b, h, dr * GRID_W:(dr + NA_H) * GRID_W]))
                rows, first = (v, start // 2) if start % 2 == 0 else (v_shifted, (start - 1) // 2)
                values.append((a, b, [rows[:, first + c, h * HD:(h + 1) * HD] for c in range(4)]))
            items.append(dict(scores=scores, keys=NA_H * GRID_W, add=add, values=values,
                              out=out[:, t, h * HD:(h + 1) * HD], sink=None))
    return items


def sparse_items(raw, small, masks, moff, out):
    items = []
    for t in range(T):
        keys = (t + 1) * P
        for h in range(HEADS):
            half = slice((h % 2) * HD, (h % 2 + 1) * HD)
            items.append(dict(
                scores=[(0, P, raw[half, h // 2, tile(t)], raw[half, 6, 0:keys])], keys=keys,
                add=[(0, P, masks[:, moff[t]:moff[t] + keys])],
                values=[(0, P, [small[:, c, V0:V0 + HD] for c in range(t + 1)])],
                out=out[:, t, h * HD:(h + 1) * HD], sink=None))
    return items


def latent_items(q, k, v, out):
    return [dict(scores=[(0, P, q[0:MLA_D, h, tile(t)], k[0:MLA_D, h, :])], keys=S, add=None,
                 values=[(0, P, [v[:, c, h * HD:(h + 1) * HD] for c in range(T)])],
                 out=out[:, t, 256 + h * HD:256 + (h + 1) * HD], sink=None)
            for t in range(T) for h in range(MLA_HEADS)]


def window_items(qk, v, band, sink, out):
    items = []
    for t in range(T):
        lo, hi = max(t - 1, 0), min(t + 1, T - 1)
        keys = (hi - lo + 1) * P
        at = (lo - t + 1) * P
        for h in range(SWA_HEADS):
            half = slice((h % 2) * HD, (h % 2 + 1) * HD)
            kv = h // (SWA_HEADS // 2)
            items.append(dict(
                scores=[(0, P, qk[half, 4 + h // 2, tile(t)], qk[half, 7 + kv, lo * P:(hi + 1) * P])], keys=keys,
                add=[(0, P, band[:, at:at + keys])],
                values=[(0, P, [v[:, c, kv * HD:(kv + 1) * HD] for c in range(lo, hi + 1)])],
                out=out[:, t, 640 + h * HD:640 + (h + 1) * HD], sink=sink[:, h:h + 1]))
    return items


def block_one(book, ps, A, ident, ones, stats, stop=None):
    nc = book.nc
    moff = [P * t * (t + 1) // 2 for t in range(T)]
    with ExitStack() as outer:
        sb = lambda ctx, name, shape: ctx.enter_context(nc.sbuf_tensor(name, shape, F32))
        rows = None
        with ExitStack() as mid:
            heads_out = sb(mid, "heads_out", [P, T, D])
            ssd = heads_out[:, :, HALF:D]
            with ExitStack() as choice:
                raw = sb(choice, "raw", [P, ROPE_CHUNKS, S])
                small = sb(choice, "small", [P, T, SMALL])
                masks = sb(choice, "masks", [P, moff[T - 1] + S])
                with ExitStack() as early:
                    xbc = sb(early, "xbc", [P, XBC_CHUNKS, S + CONV - 1])
                    z = heads_out[:, :, 0:HALF]

                    def rotate_chunks(chunks):
                        with ExitStack() as part:
                            turner = sb(part, f"turner_{book.count}", [P, P])
                            cos = sb(part, f"cos_{book.count}", [P, S])
                            sin = sb(part, f"sin_{book.count}", [P, S])
                            load(book, [(turner[:, :], A["turner64"]), (cos[:, :], A["cos64"]), (sin[:, :], A["sin64"])])
                            rotate(book, ps, turner, cos, sin, raw, chunks)

                    with ExitStack() as projection:
                        xt = sb(projection, "xt", [P, KD, S])
                        project_index(book, ps, A, xt, raw, small)
                        rotate_chunks(INDEX_CHUNKS)
                        choose_keys(book, ps, A, xt, raw, small, xbc, z, masks, moff)
                    if stop == "proj": return
                    rotate_chunks(OTHER_CHUNKS)
                    mixed = sb(early, "mixed", [P, XBC_CHUNKS, S])
                    convolve(book, A, xbc, mixed)
                    if stop == "conv": return
                    state_space(book, ps, A, ident, ones, mixed, small, z, ssd)
                    if stop == "ssd": return
                attend(book, ps, ident, sparse_items(raw, small, masks, moff, heads_out), HD ** -0.5, S)
                if stop == "dsa": return
            rows = heads_out
            with ExitStack() as part:
                high = part.enter_context(nc.sbuf_tensor("mix_high", [P, KD, S], F32R))
                low = part.enter_context(nc.sbuf_tensor("mix_low", [P, KD, S], F32R))
                turn_split(book, ps, ident, heads_out, high, low, D)
                mix_out(book, ps, A["w_out"], high, low, ALPHA, rows, A["x"])
            turned = sb(mid, "turned_mix", [P, KD, S])
            gain = sb(mid, "ln_gain", [P, D])
            shift = sb(mid, "ln_shift", [P, D])
            load(book, [(gain[:, :], A["ln1_g"].broadcast_to([P, D])), (shift[:, :], A["ln1_b"].broadcast_to([P, D]))])
            layer_norm(book, rows, gain, shift, stats, after=A["normed_rows"])
            turn(book, ps, ident, rows, turned, D)
            if stop == "ln1": return
            picked = sb(mid, "picked", [P, 2, T, EXPERTS])
            weights = sb(mid, "pick_weights", [P, 2, T])
            slots = mid.enter_context(nc.sbuf_tensor("slots", [P, 2, T], U32))
            block_tokens = mid.enter_context(nc.sbuf_tensor("block_tokens", [P, BLOCKS], U32))
            block_expert = mid.enter_context(nc.sbuf_tensor("block_expert", [P, BLOCKS], U32))
            route_one(book, ps, A, turned, picked, weights)
            place_tokens(book, ps, A, picked, ones, slots[:, :, :], block_tokens, block_expert)
            if stop == "route": return
            load(book, [(gain[:, :], A["ln2_g"].broadcast_to([P, D])), (shift[:, :], A["ln2_b"].broadcast_to([P, D]))])
            A["taken_one"] = mid.enter_context(nc.semaphore("taken_one"))
            A["came_in"] = [mid.enter_context(nc.semaphore(f"came_in{n}")) for n in range(4)]
            experts_one(book, ps, A, ident, block_tokens, block_expert)
            combine_one(book, A, slots, weights, rows)
            if stop == "moe": return
            layer_norm(book, rows, gain, shift, stats, after=A["residual_rows"])
            if stop == "ln2": return


def load(book, pairs):
    nc = book.nc
    with Stage(book, "loaded") as (block, loaded):
        @block.sync
        def _(sp):
            for to, what in pairs:
                sp.dma_start(to, what).then_inc(loaded, 16)
            sp.wait_ge(loaded, 16 * len(pairs))


def block_two(book, ps, A, ident, stats, stop=None):
    nc = book.nc
    sb = lambda ctx, name, shape, dt=F32: ctx.enter_context(nc.sbuf_tensor(name, shape, dt))
    with ExitStack() as ctx:
        taken_in = ctx.enter_context(nc.semaphore("taken_in"))
        summed = ctx.enter_context(nc.semaphore("summed"))
        with nc.Fori(0, LAYERS) as layer:
            layer_two(book, ps, A, layer, taken_in, summed, ident, stats, sb, stop)
            with Stage(book) as (block,):
                pass
    if stop: return
    finish_two(book, A, stats, sb)


def layer_two(book, ps, A, layer, taken_in, summed, ident, stats, sb, stop):
    nc = book.nc
    with ExitStack() as whole:
        mine = bass.ds(layer * P, P)
        gain_f = sb(whole, "gain_f", [P, KD])
        gates = sb(whole, "slot_gates", [P, EXPERTS])
        index = sb(whole, "slot_index", [P, EXPERTS], U32)
        with ExitStack() as mixing:
            mix = sb(mixing, "mix", [P, T, D])
            with ExitStack() as attention:
                qk = sb(attention, "qk", [P, 10, S])
                feats = sb(attention, "feats", [P, T, 768])
                with ExitStack() as part:
                    high = sb(part, "xn_high", [P, KD, S], F32R)
                    low = sb(part, "xn_low", [P, KD, S], F32R)
                    gain = sb(part, "gain_a", [P, KD])
                    load(book, [(mix[:, :, :], A["residual_rows"]), (gain[:, :], A["attn_norm"][mine])])
                    with ExitStack() as squares:
                        junk = sb(squares, "junk_a", [P, 2, D])
                        root_mean_squares(book, mix, [(0, D)], RMS_EPS, stats, junk)
                    turn_split(book, ps, ident, mix, high, low, D, gain)
                    project_two(book, ps, A, layer, high, low, qk, feats)
                if stop == "proj2": return
                with ExitStack() as part:
                    turner = sb(part, "turner64", [P, P])
                    cos = sb(part, "cos64", [P, S])
                    sin = sb(part, "sin64", [P, S])
                    turner96 = sb(part, "turner96a", [P, P])
                    cos96 = sb(part, "cos96", [P, S])
                    sin96 = sb(part, "sin96", [P, S])
                    load(book, [(turner[:, :], A["turner64"]), (cos[:, :], A["cos64"]), (sin[:, :], A["sin64"]),
                                (turner96[:, :], A["turner96"]), (cos96[:, :], A["cos96"]), (sin96[:, :], A["sin96"])])
                    rotate(book, ps, turner, cos, sin, qk, range(4, 9))
                    rotate(book, ps, turner96, cos96, sin96, qk, [9], MLA_D)
                if stop == "rope2": return
                with ExitStack() as part:
                    shifted = sb(part, "v_shifted", [P, T - 1, 256])
                    bias = sb(part, "na_bias", [P, NA_HEADS, (2 * NA_H - 1) * GRID_W])
                    outside = sb(part, "outside", [P, (2 * NA_H - 1) * GRID_W])
                    band = sb(part, "band", [P, 3 * P])
                    sink = sb(part, "sink", [P, SWA_HEADS])
                    v = feats[:, :, 0:256]
                    with Stage(book, "loaded", "masked", "scaled") as (block, loaded, masked, scaled):
                        @block.sync
                        def _(sp):
                            sp.dma_start(bias[0:GRID_W, :, :], A["na_rpb"][bass.ds(layer * GRID_W, GRID_W)]).then_inc(loaded, 16)
                            sp.dma_start(bias[GRID_W:P, :, :], A["na_rpb"][bass.ds(layer * GRID_W, GRID_W)]).then_inc(loaded, 16)
                            sp.dma_start(outside[:, :], A["na_outside"]).then_inc(loaded, 16)
                            sp.dma_start(band[:, :], A["swa_band"]).then_inc(loaded, 16)
                            sp.dma_start(sink[:, :], A["swa_sink"][bass.ds(layer, 1)].broadcast_to([P, SWA_HEADS])).then_inc(loaded, 16)
                            sp.dma_start(shifted[0:GRID_W, :, :], v[GRID_W:P, 0:T - 1, :]).then_inc(loaded, 16)
                            sp.dma_start(shifted[GRID_W:P, :, :], v[0:GRID_W, 1:T, :]).then_inc(loaded, 16)
                            sp.wait_ge(loaded, 16 * 7)

                        @block.vector
                        def _(dve):
                            dve.wait_ge(loaded, 16 * 7)
                            for h in range(NA_HEADS):
                                nc.vector.scalar_tensor_tensor(out=bias[:, h, :], in0=bias[:, h, :], scalar=HD ** 0.5,
                                                               in1=outside[:, :], op0=ALU.mult, op1=ALU.add)
                    attend(book, ps, ident, neighbourhood_items(qk, v, shifted, bias, mix), HD ** -0.5, 512)
                    if stop == "na": return
                    attend(book, ps, ident, window_items(qk, feats[:, :, 640:768], band, sink, mix), HD ** -0.5, 3 * P)
                if stop == "swa": return
                with ExitStack() as part:
                    q = sb(part, "q_mla", [P, MLA_HEADS, S])
                    k = qk[:, 0:MLA_HEADS, :]
                    v_mla = sb(part, "v_mla", [P, T, MLA_HEADS * HD])
                    with ExitStack() as inner:
                        latents = sb(inner, "latents", [P, 3, S])
                        gain = sb(inner, "gain_l", [P, 3])
                        junk = sb(inner, "junk_l", [P, 2, 256])
                        load(book, [(gain[:, :], A["latent_gain"][mine])])
                        lat = feats[:, :, 256:640]
                        root_mean_squares(book, lat, [(0, 256), (256, 384)], RMS_EPS, stats, junk)
                        turn(book, ps, ident, lat, latents, 384, gain)
                        expand_latents(book, ps, A, layer, latents, qk[:, 9, :], q, k, v_mla)
                        turner96 = sb(inner, "turner96b", [P, P])
                        cos96 = sb(inner, "cos96b", [P, S])
                        sin96 = sb(inner, "sin96b", [P, S])
                        load(book, [(turner96[:, :], A["turner96"]), (cos96[:, :], A["cos96"]), (sin96[:, :], A["sin96"])])
                        rotate(book, ps, turner96, cos96, sin96, q, range(MLA_HEADS), MLA_D)
                    attend(book, ps, ident, latent_items(q, k, v_mla, mix), MLA_D ** -0.5, S)
                if stop == "mla": return
            with ExitStack() as part:
                gain = sb(part, "gain_g", [P, KD])
                junk = sb(part, "junk_g", [P, 2, D])
                load(book, [(gain[:, :], A["group_norm"][mine]), (gain_f[:, :], A["ffn_norm"][mine])])
                root_mean_squares(book, mix, [(0, 256), (256, 640), (640, 1024)], RMS_EPS, stats, junk)
                with ExitStack() as split:
                    high = sb(split, "mix_high2", [P, KD, S], F32R)
                    low = sb(split, "mix_low2", [P, KD, S], F32R)
                    turn_split(book, ps, ident, mix, high, low, D, gain)
                    mix_out(book, ps, A["w_out_2"][mine], high, low, 1.0, mix, A["residual_rows"])
                turned = sb(part, "mix_turned", [P, KD, S])
                if stop == "mix2": return
                with Stage(book, "stored") as (block, stored):
                    @block.sync
                    def _(sp):
                        sp.dma_start(A["residual_rows"], mix[:, :, :]).then_inc(stored, 16)
                        sp.wait_ge(stored, 16)
                root_mean_squares(book, mix, [(0, D)], RMS_EPS, stats, junk)
                with Stage(book, "stored") as (block, stored):
                    @block.sync
                    def _(sp):
                        sp.dma_start(A["normed_rows"], mix[:, :, :]).then_inc(stored, 16)
                        sp.wait_ge(stored, 16)
                turn(book, ps, ident, mix, turned, D, gain_f)
                choose_tokens(book, ps, A, layer, ident, turned, gates, index)
                if stop == "choose": return
        experts_two(book, ps, A, layer, taken_in, summed, ident, gain_f, gates, index, A["normed"], A["residual"])


def finish_two(book, A, stats, sb):
    nc = book.nc
    with ExitStack() as ctx:
        rows = sb(ctx, "final_rows", [P, T, D])
        gain = sb(ctx, "final_gain", [P, D])
        junk = sb(ctx, "junk_f", [P, 2, D])
        load(book, [(rows[:, :, :], A["residual_rows"]), (gain[:, :], A["final_norm"].broadcast_to([P, D]))])
        root_mean_squares(book, rows, [(0, D)], RMS_EPS, stats, junk)
        with Stage(book, "scaled", "stored") as (block, scaled, stored):
            @block.vector
            def _(dve):
                for t in range(T):
                    nc.vector.tensor_tensor(rows[:, t, :], rows[:, t, :], gain[:, :], ALU.mult).then_inc(scaled, 1)

            @block.sync
            def _(sp):
                for t in range(T):
                    sp.wait_ge(scaled, t + 1)
                    sp.dma_start(A["out"][tile(t), :], rows[:, t, :]).then_inc(stored, 16)
                sp.wait_ge(stored, 16 * T)


def program(nc, A, stop=None, only_two=False):
    with ExitStack() as ctx:
        ps = ctx.enter_context(nc.psum_tensor("ps", [P, 8, BANK], F32))
        ident = ctx.enter_context(nc.sbuf_tensor("ident", [P, P], F32))
        ones = ctx.enter_context(nc.sbuf_tensor("ones", [P, P], F32))
        stats = ctx.enter_context(nc.sbuf_tensor("stats", [P, 2, 3 * T], F32))
        book = Book(nc)
        A["residual"] = nc.dram_tensor("residual", (S, D), F32).ap()
        A["normed"] = nc.dram_tensor("normed", (S, D), F32).ap()
        A["expert_out"] = nc.dram_tensor("expert_out", (BLOCKS * P, D), F32).ap()
        A["residual_rows"] = A["residual"].rearrange("(t p) d -> p t d", p=P)
        A["normed_rows"] = A["normed"].rearrange("(t p) d -> p t d", p=P)
        A["x"] = A["x"].rearrange("(t p) d -> p t d", p=P)
        load(book, [(ident[:, :], A["ident"]), (ones[:, :], A["ones"])])
        if only_two:
            with ExitStack() as c2:
                r = c2.enter_context(nc.sbuf_tensor("rr", [P, T, D], F32))
                load(book, [(r[:, :, :], A["x"])])
                load(book, [(A["residual_rows"], r[:, :, :])])
        else:
            block_one(book, ps, A, ident, ones, stats, stop)
        if stop is None or stop.endswith("2") and stop != "ln2" or stop in ("na", "swa", "mla", "choose", "layer"):
            block_two(book, ps, A, ident, stats, stop)




def constants():
    f = np.float32
    out = {"ident": np.eye(P, dtype=f), "ones": np.ones((P, P), f)}
    out["upto"] = np.triu(np.ones((P, P), f))
    hidden = np.where(np.arange(P)[:, None] <= np.arange(P)[None, :], f(0), f(HIDE)).astype(f)
    out["hidden"] = np.ascontiguousarray(np.broadcast_to(hidden[:, None, :], (P, 4, P)))
    out["count"] = np.ascontiguousarray(np.broadcast_to(np.arange(P, dtype=f), (P, P)))
    out["eights"] = np.ascontiguousarray(np.broadcast_to(np.arange(8, dtype=f) * P, (P, 8)))
    out["token"] = np.arange(S, dtype=f).reshape(T, P).T
    out["causal"] = np.ascontiguousarray(hidden.T)

    def rope(dim, before, after):
        inv = (f(10000.0) ** (-np.arange(0, dim, 2, dtype=f) / f(dim))).astype(f)
        ang = np.arange(S, dtype=f)[:, None] * inv[None, :]
        c, s = np.cos(ang).astype(f).T, np.sin(ang).astype(f).T
        cos = np.concatenate([np.ones((before, S), f), c, c, np.ones((after, S), f)])
        sin = np.concatenate([np.zeros((before, S), f), s, s, np.zeros((after, S), f)])
        turner = np.zeros((before + dim + after,) * 2, f)
        for i in range(dim // 2):
            turner[before + dim // 2 + i, before + i] = -1
            turner[before + i, before + dim // 2 + i] = 1
        return cos, sin, turner

    cos, sin, turner = rope(HD, 0, 0)
    out["cos64"], out["sin64"] = np.concatenate([cos, cos]), np.concatenate([sin, sin])
    out["turner64"] = np.kron(np.eye(2, dtype=f), turner)
    out["cos96"], out["sin96"], out["turner96"] = rope(32, HD, 32)
    c = np.arange(GRID_W)
    first = np.clip(c - NA_W // 2, 0, GRID_W - NA_W)
    inside = (c[None, :] >= first[:, None]) & (c[None, :] < first[:, None] + NA_W)
    outside = np.where(inside, f(0), f(HIDE)).astype(f)
    out["na_outside"] = np.tile(outside, (2, 2 * NA_H - 1))
    q, k = np.arange(P)[:, None], np.arange(3 * P)[None, :] - P
    out["swa_band"] = np.where(np.abs(q - k) <= 128, f(0), f(HIDE)).astype(f)
    return {n: np.ascontiguousarray(a) for n, a in out.items()}


def turned_weights(w, columns):
    k = w.shape[0] // P
    out = np.zeros((P, len(columns), k, P), w.dtype)
    for m, cols in enumerate(columns):
        cols = np.asarray(cols)
        there = cols >= 0
        out[:, m][:, :, there] = w[:, cols[there]].reshape(k, P, -1).transpose(1, 0, 2)
    return out


def row_weights(w):
    return np.ascontiguousarray(w.reshape(w.shape[0] // P, P, -1).transpose(1, 0, 2))


def columns_of(a):
    return np.ascontiguousarray(a.reshape(-1, P).T)


def arrays_of(i):
    r = np.arange
    A = constants()
    x = i["x"][0]
    A["x"], A["xt"] = x, np.ascontiguousarray(x.T)
    w = i["w_in"][0]
    k, ik = r(512, 576), r(896, 960)
    cols = [r(128 * m, 128 * m + 128) for m in range(4)] + [r(640, 768), r(768, 896)]
    cols += [np.concatenate([k, k]), np.concatenate([ik, ik])]
    cols += [r(1476 + 128 * m, 1476 + 128 * m + 128) for m in range(6)]
    A["w_turned"] = turned_weights(w, [cols[c] for c in OTHER_CHUNKS] + cols[ROPE_CHUNKS:])
    A["w_turned_index"] = turned_weights(w, [cols[c] for c in INDEX_CHUNKS])
    A["w_rows_z"] = row_weights(w[:, 964:1476])
    A["w_rows_small"] = row_weights(w[:, np.concatenate([r(576, 640), r(960, 964), r(2244, 2252)])])
    A["conv_w"] = np.ascontiguousarray(i["conv_w"][0].T.reshape(6, P, CONV).transpose(1, 0, 2))
    A["conv_b"] = columns_of(i["conv_b"][0])
    for n in ("dt_bias", "a_log", "d_skip", "ssd_norm_w", "ln1_g", "ln1_b", "ln2_g", "ln2_b"):
        A[n] = i[n]
    A["w_out"] = row_weights(i["w_out"][0])
    A["w_route"] = row_weights(np.concatenate([i["w_route_group"][0], i["w_route_expert"][0]], 1))
    A["b_route"] = np.concatenate([i["b_route_group"], i["b_route_expert"]], 1)
    A["w_gate_up"] = np.concatenate([i["w_gate"][0], i["w_up"][0]], -1)
    A["w_down"] = i["w_down"][0]
    for n in ("w_gate", "w_up", "w_down"):
        A[n + "_2"] = i[n + "_2"].reshape(LAYERS * EXPERTS, D, D)
    cols = [r(128 * m, 128 * m + 128) for m in range(4)] + [r(1184 + 128 * m, 1312 + 128 * m) for m in range(3)]
    cols += [np.concatenate([r(1568 + 64 * g, 1632 + 64 * g)] * 2) for g in range(2)]
    cols += [np.concatenate([np.full(64, -1), r(1152, 1184), np.full(32, -1)])]
    rows = np.concatenate([r(512, 768), r(768, 1024), r(1024, 1152), r(1696, 1824)])
    w = i["w_in_2"]
    cat = lambda f: np.concatenate([f(l) for l in range(LAYERS)])
    A["w_turned_2"] = cat(lambda l: turned_weights(w[l], cols))
    A["w_rows_2"] = cat(lambda l: row_weights(w[l][:, rows]))
    A["attn_norm"] = cat(lambda l: columns_of(i["attn_norm_2"][l]))
    A["group_norm"] = cat(lambda l: columns_of(i["group_norm_2"][l]))
    A["ffn_norm"] = cat(lambda l: columns_of(i["ffn_norm_2"][l]))
    A["latent_gain"] = cat(lambda l: columns_of(np.concatenate([i["mla_q_norm_2"][l], i["mla_kv_norm_2"][l]])))
    A["mla_w_uq"] = cat(lambda l: row_weights(i["mla_w_uq_2"][l]))
    kv = np.concatenate([np.concatenate([r(128 * h + s, 128 * h + s + 64) for h in range(MLA_HEADS)]) for s in (0, 64)])
    A["mla_w_ukv"] = cat(lambda l: np.ascontiguousarray(i["mla_w_ukv_2"][l][:, kv]))
    A["swa_sink"] = i["swa_sink_2"]
    A["w_out_2"] = cat(lambda l: row_weights(i["w_out_2"][l]))
    A["w_router"] = cat(lambda l: row_weights(i["w_router_2"][l]))
    A["final_norm"] = i["final_norm_2"].reshape(1, D)
    dc = np.clip(r(GRID_W)[None, :] - r(GRID_W)[:, None] + NA_W - 1, 0, 2 * NA_W - 2)
    A["na_rpb"] = cat(lambda l: i["na_rpb_2"][l][:, :, dc].transpose(2, 0, 1, 3).reshape(GRID_W, NA_HEADS, -1))
    return {n: np.ascontiguousarray(a) for n, a in A.items()}


def kernel(**inputs):
    import concourse.bacc as bacc
    from concourse.bass_utils import run_bass_kernel_spmd as run

    nc = bacc.Bacc("TRN2", target_bir_lowering=False, num_devices=1)
    arrays = arrays_of({n: np.asarray(a) for n, a in inputs.items()})
    A = {n: nc.dram_tensor("in_" + n, a.shape, mybir.dt.from_np(a.dtype), kind="ExternalInput").ap()
         for n, a in arrays.items()}
    A["out"] = nc.dram_tensor("out_0", (S, D), F32, kind="ExternalOutput").ap()
    program(nc, A)
    r = run(nc, [{"in_" + n: a for n, a in arrays.items()}], core_ids=[0])
    return r.results[0]["out_0"].reshape(1, S, D)
```
